# Optimizing a Trainium2 kernel written in Bass

```python
import math
import jax, jax.numpy as jnp
from jax import lax
import numpy as np

D_MODEL = 1024
BATCH = 1
SEQ = 256
DEPTH = 2

CHUNK = 64
HEAD_DIM = 64
SSM_WIDTH = D_MODEL // 4
ATT_WIDTH = (D_MODEL - SSM_WIDTH) // 2
RET_WIDTH = D_MODEL - SSM_WIDTH - ATT_WIDTH
ATT_HEADS = ATT_WIDTH // HEAD_DIM
RET_HEADS = RET_WIDTH // HEAD_DIM
IN_COLS = 3 * ATT_WIDTH + 4 * RET_WIDTH + SSM_WIDTH
ATT_LEFT_CHUNKS = 8
ATT_BAND = (ATT_LEFT_CHUNKS + 1) * CHUNK
REL_CLIP = 256
ROPE_BASE = 10000.0
SSM_GROUP = 16
SSM_GROUPS = SSM_WIDTH // SSM_GROUP
SSM_STATE = 64
PEER_HEADS = 8
PEER_TOPK = 16
PEER_NKEYS = 128
PEER_QDIM = 256
PEER_N = PEER_NKEYS * PEER_NKEYS
PEER_BLOCK = 128
EPS = 1e-6

kernel_name = 'hybrid_streaming_encoder_block'

def _rms(x):
    xf = x.astype(jnp.float32)
    return xf * lax.rsqrt(jnp.mean(xf * xf, axis=-1, keepdims=True) + EPS)

def rms_norm(x, gain):
    return (_rms(x) * gain.astype(jnp.float32)).astype(x.dtype)

def chunk_attention(q, k, v, rel_bias):
    b, l, h, dh = q.shape
    nc = l // CHUNK
    qc = q.reshape(b, nc, CHUNK, h, dh)
    kc = k.reshape(b, nc, CHUNK, h, dh)
    vc = v.reshape(b, nc, CHUNK, h, dh)
    pad = ((0, 0), (ATT_LEFT_CHUNKS, 0), (0, 0), (0, 0), (0, 0))
    kp = jnp.pad(kc, pad)
    vp = jnp.pad(vc, pad)
    kb = jnp.concatenate([kp[:, j:j + nc] for j in range(ATT_LEFT_CHUNKS + 1)], axis=2)
    vb = jnp.concatenate([vp[:, j:j + nc] for j in range(ATT_LEFT_CHUNKS + 1)], axis=2)
    scores = jnp.einsum('bnqhd,bnkhd->bnhqk', qc, kb).astype(jnp.float32) * (dh ** -0.5)
    qpos = jnp.arange(CHUNK) + ATT_LEFT_CHUNKS * CHUNK
    kpos = jnp.arange(ATT_BAND)
    rel = jnp.clip(qpos[:, None] - kpos[None, :], -REL_CLIP, REL_CLIP) + REL_CLIP
    bias = rel_bias.astype(jnp.float32)[:, rel]
    key_chunk = jnp.arange(nc)[:, None] + (kpos // CHUNK)[None, :] - ATT_LEFT_CHUNKS
    valid = (key_chunk >= 0)[None, :, None, None, :]
    scores = jnp.where(valid, scores + bias[None, None], -1e30)
    p = jax.nn.softmax(scores, axis=-1).astype(v.dtype)
    out = jnp.einsum('bnhqk,bnkhd->bnqhd', p, vb)
    return out.reshape(b, l, h * dh)

def rotary(x, pos):
    d = x.shape[-1]
    half = d // 2
    inv = ROPE_BASE ** (-jnp.arange(half, dtype=jnp.float32) / half)
    ang = pos.astype(jnp.float32)[:, None] * inv[None, :]
    cos = jnp.cos(ang)[None, :, None, :]
    sin = jnp.sin(ang)[None, :, None, :]
    xf = x.astype(jnp.float32)
    x1, x2 = xf[..., :half], xf[..., half:]
    return jnp.concatenate([x1 * cos - x2 * sin, x1 * sin + x2 * cos], axis=-1)

def retention(q, k, v, g):
    b, l, h, d = q.shape
    nc = l // CHUNK
    pos = jnp.arange(l)
    qf = rotary(q, pos)
    kf = rotary(k, pos) * (d ** -0.5)
    vf = v.astype(jnp.float32)
    log_g = jnp.log1p(-jnp.power(2.0, -5.0 - jnp.arange(h, dtype=jnp.float32)))
    idx = jnp.arange(CHUNK, dtype=jnp.float32)
    intra_decay = jnp.exp(log_g[:, None, None] * jnp.abs(idx[:, None] - idx[None, :]))
    k_decay = jnp.exp(log_g[:, None] * (CHUNK - 1 - idx)[None, :])
    q_decay = jnp.exp(log_g[:, None] * (idx + 1.0)[None, :])
    chunk_decay = jnp.exp(log_g * CHUNK)[None, :, None, None]
    qc = qf.reshape(b, nc, CHUNK, h, d)
    kc = kf.reshape(b, nc, CHUNK, h, d)
    vc = vf.reshape(b, nc, CHUNK, h, d)
    s = jnp.einsum('bnqhd,bnkhd->bnhqk', qc, kc) * intra_decay
    y_intra = jnp.einsum('bnhqk,bnkhe->bnqhe', s, vc)
    upd = jnp.einsum('bnkhd,bnkhe,hk->nbhde', kc, vc, k_decay)

    def step(state, u):
        return chunk_decay * state + u, state

    _, s_prev = lax.scan(step, jnp.zeros((b, h, d, d), jnp.float32), upd)
    y_cross = jnp.einsum('bnqhd,nbhde,hq->bnqhe', qc, s_prev, q_decay)
    y = y_intra + y_cross
    mu = jnp.mean(y, axis=-1, keepdims=True)
    var = jnp.mean(jnp.square(y - mu), axis=-1, keepdims=True)
    y = (y - mu) * lax.rsqrt(var + EPS)
    y = y.reshape(b, l, h * d) * jax.nn.silu(g.astype(jnp.float32))
    return y.astype(v.dtype)

def s5_ssm(u, lam_re, lam_im, log_dt, b_re, b_im, c_re, c_im, d_skip, w_glu):
    bsz, l, w = u.shape
    uf = u.astype(jnp.float32).reshape(bsz, l, SSM_GROUPS, SSM_GROUP)
    dt = jnp.exp(log_dt.astype(jnp.float32))[:, None]
    lr = lam_re.astype(jnp.float32)
    li = lam_im.astype(jnp.float32)
    mag = jnp.exp(lr * dt)
    ab_re = mag * jnp.cos(li * dt)
    ab_im = mag * jnp.sin(li * dt)
    den = lr * lr + li * li
    nr, ni = ab_re - 1.0, ab_im
    f_re = (nr * lr + ni * li) / den
    f_im = (ni * lr - nr * li) / den
    br, bi = b_re.astype(jnp.float32), b_im.astype(jnp.float32)
    bb_re = f_re[..., None] * br - f_im[..., None] * bi
    bb_im = f_re[..., None] * bi + f_im[..., None] * br
    bu_re = jnp.einsum('gpc,blgc->blgp', bb_re, uf)
    bu_im = jnp.einsum('gpc,blgc->blgp', bb_im, uf)
    a_re = jnp.broadcast_to(ab_re, bu_re.shape)
    a_im = jnp.broadcast_to(ab_im, bu_im.shape)

    def combine(e1, e2):
        ar1, ai1, br1, bi1 = e1
        ar2, ai2, br2, bi2 = e2
        return (ar2 * ar1 - ai2 * ai1,
                ar2 * ai1 + ai2 * ar1,
                ar2 * br1 - ai2 * bi1 + br2,
                ar2 * bi1 + ai2 * br1 + bi2)

    _, _, x_re, x_im = lax.associative_scan(combine, (a_re, a_im, bu_re, bu_im), axis=1)
    y = (jnp.einsum('gcp,blgp->blgc', c_re.astype(jnp.float32), x_re)
         - jnp.einsum('gcp,blgp->blgc', c_im.astype(jnp.float32), x_im)
         + d_skip.astype(jnp.float32).reshape(SSM_GROUPS, SSM_GROUP) * uf)
    y = jax.nn.gelu(y.reshape(bsz, l, w))
    z = y @ w_glu.astype(jnp.float32)
    out = z[..., :w] * jax.nn.sigmoid(z[..., w:])
    return out.astype(u.dtype)

def peer(h, w_q, subkeys, u_tab, v_tab):
    b, l, dm = h.shape
    t = b * l
    hf = h.reshape(t, dm)
    q = (hf @ w_q).astype(jnp.float32).reshape(t, PEER_HEADS, 2, PEER_QDIM // 2)
    s = jnp.einsum('thsd,hskd->thsk', q, subkeys.astype(jnp.float32))
    top_s, top_i = lax.top_k(s, PEER_TOPK)
    cand_s = top_s[:, :, 0, :, None] + top_s[:, :, 1, None, :]
    cand_i = top_i[:, :, 0, :, None] * PEER_NKEYS + top_i[:, :, 1, None, :]
    best_s, best_pos = lax.top_k(cand_s.reshape(t, PEER_HEADS, PEER_TOPK * PEER_TOPK), PEER_TOPK)
    expert = jnp.take_along_axis(cand_i.reshape(t, PEER_HEADS, PEER_TOPK * PEER_TOPK), best_pos, axis=-1)
    gate = jax.nn.softmax(best_s, axis=-1)
    nblk = t // PEER_BLOCK

    def block(args):
        hb, eb, gb = args
        ub = jnp.take(u_tab, eb, axis=0)
        vb = jnp.take(v_tab, eb, axis=0)
        act = jax.nn.gelu(jnp.einsum('thkd,td->thk', ub, hb).astype(jnp.float32))
        return jnp.einsum('thk,thkd->td', (gb * act).astype(vb.dtype), vb)

    out = lax.map(block, (hf.reshape(nblk, PEER_BLOCK, dm),
                          expert.reshape(nblk, PEER_BLOCK, PEER_HEADS, PEER_TOPK),
                          gate.reshape(nblk, PEER_BLOCK, PEER_HEADS, PEER_TOPK)))
    return out.reshape(b, l, dm).astype(h.dtype)

def setup_inputs(seed: int = 0) -> dict:
    key = jax.random.key(seed)
    ks = jax.random.split(key, 26)
    f32 = jnp.float32
    nrm = lambda k, shape, scale: jax.random.normal(k, shape, f32) * scale
    lam_re = -0.5 + nrm(ks[7], (DEPTH, SSM_GROUPS, SSM_STATE), 0.01)
    lam_im = (jnp.pi * jnp.arange(SSM_STATE, dtype=f32))[None, None, :] + nrm(ks[8], (DEPTH, SSM_GROUPS, SSM_STATE), 0.01)
    log_dt = jax.random.uniform(ks[9], (DEPTH, SSM_GROUPS), f32, math.log(1e-3), math.log(1e-1))
    return {
        'x': nrm(ks[0], (BATCH, SEQ, D_MODEL), 1.0),
        'c': nrm(ks[1], (BATCH, D_MODEL), 1.0),
        'w_ada': nrm(ks[2], (DEPTH, D_MODEL, 6 * D_MODEL), 0.5 * D_MODEL ** -0.5),
        'b_ada': nrm(ks[3], (DEPTH, 6 * D_MODEL), 0.02),
        'norm_mix': 1.0 + nrm(ks[4], (DEPTH, D_MODEL), 0.05),
        'norm_ffn': 1.0 + nrm(ks[5], (DEPTH, D_MODEL), 0.05),
        'w_in': nrm(ks[6], (DEPTH, D_MODEL, IN_COLS), D_MODEL ** -0.5),
        'rel_bias': nrm(ks[10], (DEPTH, ATT_HEADS, 2 * REL_CLIP + 1), 0.2),
        'ssm_lambda_re': lam_re,
        'ssm_lambda_im': lam_im,
        'ssm_log_dt': log_dt,
        'ssm_b_re': nrm(ks[11], (DEPTH, SSM_GROUPS, SSM_STATE, SSM_GROUP), (2 * SSM_GROUP) ** -0.5),
        'ssm_b_im': nrm(ks[12], (DEPTH, SSM_GROUPS, SSM_STATE, SSM_GROUP), (2 * SSM_GROUP) ** -0.5),
        'ssm_c_re': nrm(ks[13], (DEPTH, SSM_GROUPS, SSM_GROUP, SSM_STATE), (2 * SSM_STATE) ** -0.5),
        'ssm_c_im': nrm(ks[14], (DEPTH, SSM_GROUPS, SSM_GROUP, SSM_STATE), (2 * SSM_STATE) ** -0.5),
        'ssm_d': nrm(ks[15], (DEPTH, SSM_WIDTH), 1.0),
        'w_glu': nrm(ks[16], (DEPTH, SSM_WIDTH, 2 * SSM_WIDTH), SSM_WIDTH ** -0.5),
        'merge_gain': 1.0 + nrm(ks[17], (DEPTH, D_MODEL), 0.05),
        'w_out': nrm(ks[18], (DEPTH, D_MODEL, D_MODEL), D_MODEL ** -0.5),
        'peer_w_q': nrm(ks[19], (DEPTH, D_MODEL, PEER_HEADS * PEER_QDIM), D_MODEL ** -0.5),
        'peer_subkeys': nrm(ks[20], (DEPTH, PEER_HEADS, 2, PEER_NKEYS, PEER_QDIM // 2), (PEER_QDIM // 2) ** -0.5),
        'peer_u': nrm(ks[21], (DEPTH, PEER_N, D_MODEL), D_MODEL ** -0.5),
        'peer_v': nrm(ks[22], (DEPTH, PEER_N, D_MODEL), 0.5),
        'final_norm': 1.0 + nrm(ks[23], (D_MODEL,), 0.05),
    }

def reference(x, c, w_ada, b_ada, norm_mix, norm_ffn, w_in, rel_bias, ssm_lambda_re, ssm_lambda_im,
              ssm_log_dt, ssm_b_re, ssm_b_im, ssm_c_re, ssm_c_im, ssm_d, w_glu, merge_gain, w_out,
              peer_w_q, peer_subkeys, peer_u, peer_v, final_norm):
    b, l, dm = x.shape
    sizes = [ATT_WIDTH] * 3 + [RET_WIDTH] * 4 + [SSM_WIDTH]
    splits = [int(v) for v in np.cumsum(sizes)[:-1]]
    cond = jax.nn.silu(c)
    for layer in range(DEPTH):
        mod = (cond @ w_ada[layer] + b_ada[layer])[:, None, :]
        sh1, sc1, g1, sh2, sc2, g2 = jnp.split(mod, 6, axis=-1)
        hmix = rms_norm(x, norm_mix[layer]) * (1.0 + sc1) + sh1
        proj = hmix @ w_in[layer]
        qa, ka, va, qr, kr, vr, gr, us = jnp.split(proj, splits, axis=-1)
        hs = lambda t: t.reshape(b, l, -1, HEAD_DIM)
        att = chunk_attention(hs(qa), hs(ka), hs(va), rel_bias[layer])
        ret = retention(hs(qr), hs(kr), hs(vr), gr)
        ssm = s5_ssm(us, ssm_lambda_re[layer], ssm_lambda_im[layer], ssm_log_dt[layer],
                     ssm_b_re[layer], ssm_b_im[layer], ssm_c_re[layer], ssm_c_im[layer],
                     ssm_d[layer], w_glu[layer])
        merged = jnp.concatenate([_rms(att), ret.astype(jnp.float32), _rms(ssm)], axis=-1)
        merged = (merged * merge_gain[layer].astype(jnp.float32)).astype(x.dtype)
        x = x + g1 * (merged @ w_out[layer])
        hffn = rms_norm(x, norm_ffn[layer]) * (1.0 + sc2) + sh2
        x = x + g2 * peer(hffn, peer_w_q[layer], peer_subkeys[layer], peer_u[layer], peer_v[layer])
    return rms_norm(x, final_norm)


_drawn_inputs = setup_inputs


def setup_inputs(seed=0):
    import zlib

    import numpy as np

    out = dict(_drawn_inputs(seed))
    spreads = {}
    factors = {'ssm_lambda_re': 64.0,
     'ssm_lambda_im': 23.27,
     'ssm_log_dt': 24.531,
     'ssm_b_re': 30.712,
     'ssm_b_im': 32.528,
     'ssm_c_re': 30.944,
     'ssm_c_im': 33.032}
    for name, (base, spread) in spreads.items():
        noise = np.random.default_rng([zlib.crc32(name.encode()), seed]).standard_normal(out[name].shape)
        drawn = base * np.exp(spread * noise) if base else spread * noise
        out[name] = __import__('jax').numpy.asarray(drawn.astype(out[name].dtype))
    for name, factor in factors.items():
        out[name] = (out[name] * factor).astype(out[name].dtype)
    return out
```

```python
import math
from contextlib import ExitStack

import numpy as np

import concourse.bass as bass
from concourse import mybir

F32 = mybir.dt.float32
F32R = mybir.dt.float32r
U32 = mybir.dt.uint32
ALU = mybir.AluOpType
ACT = mybir.ActivationFunctionType
AX = mybir.AxisListType

P = 128
L = 2
D = 1024
T = 256
KT = D // P
TT = T // P
CHUNK = 64
HD = 64
NH = 6
AW = NH * HD
SW = 256
STATES = 64
GCH = 16
ST = 16 * STATES // P
IN_COLS = 3 * AW + 4 * AW + SW
IN_TILES = IN_COLS // P
PH = 8
NK = 128
TOPK = 16
NE = NK
NB = 2 * AW // P
EPS = 1e-6
NEG = -1e30
TWO_PI_HI = 6.28125
TWO_PI_LO = 2.0 * math.pi - 6.28125
ROUND = 1.5 * 2.0 ** 23
PI = 3.1415925

C_BADA, C_NMIX, C_NFFN, C_GAIN, C_D, C_LRE, C_LIM, C_LDT = 0, 48, 56, 64, 72, 74, 82, 90
C_ALL = 98
SH1, SC1, G1, SH2, SC2, G2 = range(6)


def trunk(nc, xT, c, cols, fcol, w_ada, w_in, w_out, w_q, w_glu, rel_bias, b_re, b_im, c_re, c_im,
          subkeys, u_tab, v_tab, ident_c, iota_c, decay_c, rope_c, perm_c, mask_c, outT):
    ctx = ExitStack()
    with ctx:
        base = 16512

        def at(name, floats, shape, dt=F32):
            return nc.alloc_sbuf_tensor_at(name, shape, dt, offset=base + 4 * floats)

        def sem(name):
            return ctx.enter_context(nc.semaphore(name))

        WT = at("gates_T", 0, [P, NE, T])
        HT = at("h_T", 0, [P, KT, T])
        MERGED = at("merged", 0, [P, TT, D])
        QA = at("q_att_T", 10240, [P, 2, 3, T])
        KA = at("k_att_T", 2816, [P, 3, T])
        VA = at("v_att", 3584, [P, TT, AW])
        QK = at("qk_ret_T", 4352, [P, 6, T])
        VR = at("v_ret", 5888, [P, TT, AW])
        GR = at("g_ret", 6656, [P, TT, AW])
        UT = at("u_ssm_T", 7424, [P, 2, T])
        SQ = at("squares", 7936, [P, KT, T])
        SAB = at("scores_ab", 7936, [P, NH * (P + T)])
        SA = SAB[:, 0:NH * P].rearrange("p (h t) -> p h t", h=NH)
        SB = SAB[:, NH * P:].rearrange("p (h t) -> p h t", h=NH)
        PT = at("probs_T", 10240, [P, 18, P])
        SR0 = at("ret_scores_0", 12544, [P, NH, T])
        SR1 = at("ret_scores_1", 14080, [P, NH, P])
        UM = at("u_masked", 12544, [P, 2, 4, T])
        DEC0 = at("decay_0", 14848, [P, NH, T])
        DEC1 = at("decay_1", 16384, [P, NH, P])
        BIAS = at("rel_bias_rows", 17152, [P, NH, T])
        ROPE = at("rope", 18688, [P, 2, T])
        GEXP = at("gate_exp_ret", 20736, [P, TT, AW])[:, :, :]
        YSQ = at("y_squares", 19968, [P, 2 * NH, HD])[:, :, :]
        YR = at("y_ret", 19200, [P, TT, AW])
        ROT = at("rotated", 19968, [P, 6, T])
        QM = at("q_ret_masked", 21760, [P, 2, 3, T])
        MT = at("merged_T", 21504, [P, KT, T])
        RSTD = at("rstd", 23552, [P, T])
        ADA = at("w_ada_ring", 24576, [P, 8, D])
        QT = at("query_T", 2048, [P, 2, T])
        SUBT = at("subkeys_T", 4096, [P, 16, NK])
        KS = at("key_scores", 6144, [P, TT, 16, NK])
        CAND = at("candidates", 10240, [P, PH, TOPK, TOPK])
        EQ = at("equal", 12288, [P, PH, TOPK, TOPK])
        V16 = at("top_scores", 14336, [P, TT, 16, TOPK])
        I16 = at("top_keys", 14848, [P, TT, 16, TOPK], U32)
        I16F = at("top_keys_f", 15360, [P, TT, 16, TOPK])
        BEST = at("best", 15872, [P, TT, PH, TOPK])
        POS = at("best_pos", 16128, [P, TT, PH, TOPK], U32)
        POSA = at("pos_a", 16384, [P, TT, PH, TOPK], U32)
        POSB = at("pos_b", 16640, [P, TT, PH, TOPK], U32)
        AF = at("pos_a_f", 16896, [P, TT, PH, TOPK])
        BF = at("pos_b_f", 17152, [P, TT, PH, TOPK])
        SEL = at("picks", 17408, [P, 3, TT, P])
        GSUM = at("gate_sum", 18176, [P, TT, PH])
        ACC = at("mixed", 2048, [P, TT, D])
        X = at("x_T", 32768, [P, KT, T])
        RING = at("weight_ring", 34816, [P, 4, D])
        UH = at("u_hi", 38912, [P, 2, KT, P], F32R)
        UL = at("u_lo", 40960, [P, 2, KT, P], F32R)
        VH = at("v_hi", 43008, [P, 2, D], F32R)
        VL = at("v_lo", 45056, [P, 2, D], F32R)
        HH = at("h_hi", 47104, [P, KT, T], F32R)
        HL = at("h_lo", 49152, [P, KT, T], F32R)
        COS = at("cos_t", 38912, [P, 4, T])
        SIN = at("sin_t", 39936, [P, 4, T])
        ZRE = at("z_re", 40960, [P, 4, T])
        ZIM = at("z_im", 41984, [P, 4, T])
        TA = at("tmp_a", 43008, [P, 4, T])
        TB = at("tmp_b", 44032, [P, 4, T])
        CFRE = at("cf_re", 45056, [P, ST, P])
        CFIM = at("cf_im", 46080, [P, ST, P])
        BTRE = at("b_re_T", 47104, [P, 2, P])
        BTIM = at("b_im_T", 47360, [P, 2, P])
        WGLU = at("w_glu_sb", 47616, [P, 2, 2 * SW])
        YG = at("y_gelu_T", 48640, [P, 2, T])
        BRAW = at("b_raw", 49152, [P, 2, 2, STATES])
        CRAW = at("c_raw", 49408, [P, 2, ST, GCH])
        CTMP = at("c_tmp", 49664, [P, 4, ST, GCH])
        ZG = at("z_gate", 50176, [P, TT, SW])
        CB = at("cond", 40960, [P, D])
        CE = at("cond_exp", 41984, [P, D])
        SCR = at("scratch_row", 43008, [P, D])
        TURNS = at("turns", 14848, [P, 4, T])
        OHA = at("onehot_gate", 38912, [P, 4, 4, P])
        OHB = at("onehot_key", 40960, [P, 4, 4, P])
        GE = at("gelu", 51200, [P, 2, T])
        G32 = at("gated", 51712, [P, T])
        GH = at("gated_hi", 51968, [P, T], F32R)
        GL = at("gated_lo", 52224, [P, T], F32R)
        ONES = at("ones", 51200, [P, P])
        IOTA = at("iota", 51328, [P, T])
        IDENT = at("ident", 51584, [P, P])
        SELT = at("picks_T", 51712, [P, 3, T])
        COLS = at("cols", 52480, [P, L, C_ALL])
        FCOL = at("final_gain", 52680, [P, KT])
        MOD = at("mod", 52688, [P, 6, KT])
        AMP = at("amp", 52736, [P, KT])
        MASK = at("masks", 52944, [P, 10])
        SM = at("softmax_stat", 52752, [P, 4, 12])
        SV = at("ssm_vec", 52800, [P, 15, ST])
        ADA8 = at("ada_dots", 52928, [P, KT])
        RMS = at("rms_stat", 52936, [P, 4])

        PS = ctx.enter_context(nc.psum_tensor("ps", [P, 8, 512], F32))
        ps = PS[:, :, :].rearrange("p b n -> p (b n)")

        in_x = sem("x_loaded")
        in_cols = sem("cols_loaded")
        in_c = sem("c_loaded")
        in_const = sem("const_loaded")
        in_mix = sem("mix_tables_loaded")
        in_sub = sem("subkeys_loaded")
        in_perm = sem("perm_loaded")
        in_ada = [sem(f"ada_loaded_{i}") for i in range(8)]
        in_ring = [sem(f"ring_loaded_{i}") for i in range(4)]
        out_done = sem("out_done")
        dve_step = sem("dve_step")
        act_step = sem("act_step")
        ada_used = sem("ada_used")
        cond_exp = sem("cond_exp_done")
        mod_done = sem("mod_done")
        x_ready = sem("x_ready")
        squared = sem("squared")
        ones_ready = sem("ones_ready")
        sumsq = sem("sumsq_done")
        var_done = sem("var_done")
        std_done = sem("std_done")
        normed = sem("normed")
        h_done = sem("h_done")
        h_hi = sem("h_hi_done")
        rvar = sem("ret_var_done")
        rstd_done = sem("ret_std_done")
        mvar = sem("merge_var_done")
        mstd = sem("merge_std_done")
        h_split = sem("h_split_done")
        proj_mm = sem("proj_product")
        proj_ev = sem("proj_evacuated")
        rot_mm = sem("rot_product")
        rot_done = sem("rotated_done")
        att_mm = sem("att_scores")
        att_in = sem("att_scores_taken")
        att_sub = sem("att_shifted")
        att_exp = sem("att_exp_done")
        ret_mm = sem("ret_scores")
        ret_in = sem("ret_scores_decayed")
        pt_mm = sem("probs_transposed")
        pt_ev = sem("probs_T_taken")
        ry_mm = sem("ret_product")
        ry_ev = sem("ret_product_taken")
        ao_mm = sem("att_product")
        ao_ev = sem("att_product_taken")
        gexp = sem("gate_exp_done")
        ssm_e = sem("ssm_exp_in")
        ssm_x = sem("ssm_exp_out")
        ssm_a = sem("ssm_angle_in")
        ssm_s = sem("ssm_sine_out")
        bt_done = sem("b_masked")
        bu_mm = sem("bu_product")
        bu_ev = sem("bu_taken")
        xs_done = sem("states_done")
        cf_done = sem("cf_done")
        sy_mm = sem("ssm_y_product")
        sy_in = sem("ssm_y_sum")
        sy_gelu = sem("ssm_gelu_done")
        glu_mm = sem("glu_product")
        glu_exp = sem("glu_exp_done")
        merged = sem("merged_done")
        mt_mm = sem("merged_transposed")
        mt_ev = sem("merged_T_taken")
        wo_mm = sem("w_out_product")
        q_mm = sem("query_product")
        q_ev = sem("query_taken")
        ks_mm = sem("key_scores_product")
        ks_ev = sem("key_scores_taken")
        gate_in = sem("gate_shifted")
        gate_exp = sem("gate_exp")
        picks = sem("picks_done")
        pickt_mm = sem("picks_transposed")
        pickt = sem("picks_T_taken")
        onehot = sem("onehots_done")
        w_mm = sem("gates_product")
        w_ev = sem("gates_taken")
        u_hi = sem("u_hi_done")
        u_split = sem("u_split_done")
        v_hi = sem("v_hi_done")
        v_split = sem("v_split_done")
        s_mm = sem("expert_scores")
        gelu_done = sem("expert_gelu")
        g_prod = sem("gated_product")
        g_hi = sem("gated_hi_done")
        g_ready = sem("gated_split")
        v_used = sem("experts_summed")
        acc_ev = sem("mixed_taken")
        acc_mm = sem("mixed_transposed")
        fin = sem("final_done")

        NSTREAM = IN_TILES + KT + 16
        assert NSTREAM % 4 == 3

        def ring_pos(l, n):
            full, slot = (NSTREAM + 1) // 4 + NE // 2, n % 4
            return slot, 16 * (l * full - (l if slot == 3 else 0) + n // 4 + 1)

        def expert_pos(l, v, b):
            full, slot = (NSTREAM + 1) // 4 + NE // 2, 2 * v + b
            n = (NSTREAM + 1) // 4 - (1 if slot == 3 else 0)
            return slot, l * full - (l if slot == 3 else 0) + n + 1

        TILE_IN, TILE_OUT, TILE_Q = 0, IN_TILES, IN_TILES + KT
        IN_ORDER = [21, 22, 9, 10, 11, 12, 13, 14, 0, 1, 2, 3, 4, 5, 6, 7, 8, 15, 16, 17, 18, 19, 20]

        N_PROJ = 20
        PROJ_OF = list(range(14)) + [15] * 3 + [17] * 3 + [19] * 3

        block = ctx.enter_context(nc.Block())

        @block.sync
        def _(sp):
            sp.dma_start(COLS[:, :, :], cols).then_inc(in_cols, 16)
            sp.dma_start(FCOL[:, :], fcol).then_inc(in_cols, 16)
            sp.dma_start(MASK[:, :], mask_c).then_inc(in_cols, 16)
            sp.dma_start(X[:, :, :], xT.rearrange("(k p) t -> p k t", p=P)).then_inc(in_x, 16)
            for l in range(L):
                if l == 0:
                    sp.dma_start(IDENT[:, :], ident_c).then_inc(in_const, 16)
                    sp.dma_start(IOTA[:, :], iota_c).then_inc(in_const, 16)
                sp.dma_start(CB[:, :], bass.AP(c.tensor, 0, [[0, P], [1, D]])).then_inc(in_c, 16)

                def ada(m):
                    n = l * 48 + m
                    if m >= 8:
                        sp.wait_ge(ada_used, n - 7)
                    sp.dma_start(ADA[:, m % 8, :], w_ada[l, m * P:(m + 1) * P, :]).then_inc(in_ada[m % 8], 16)

                def stream(n):
                    slot, value = ring_pos(l, n)
                    if n >= 4:
                        m = n - 4
                        if m < TILE_OUT:
                            sp.wait_ge(proj_mm, l * N_PROJ + PROJ_OF[m] + 1)
                        elif m < TILE_Q:
                            sp.wait_ge(wo_mm, l * KT + m - TILE_OUT + 1)
                        else:
                            sp.wait_ge(q_mm, l * 16 + m - TILE_Q + 1)
                    if n < TILE_OUT:
                        src = w_in[l, IN_ORDER[n]]
                    elif n < TILE_Q:
                        src = w_out[l, n - TILE_OUT]
                    else:
                        src = w_q[l, n - TILE_Q]
                    sp.dma_start(RING[:, slot, :], src).then_inc(in_ring[slot], 16)

                for m in range(16):
                    ada(m)
                for n in range(4):
                    stream(n)
                sp.dma_start(ROPE[:, :, :], rope_c).then_inc(in_mix, 16)
                sp.dma_start(DEC0[:, :, :], decay_c[:, 0:NH * T].rearrange("p (h t) -> p h t", h=NH)).then_inc(in_mix, 16)
                sp.dma_start(DEC1[:, :, :], decay_c[:, NH * T:].rearrange("p (h t) -> p h t", h=NH)).then_inc(in_mix, 16)
                sp.dma_start(BIAS[:, :, :], bass.AP(rel_bias.tensor, l * NH * 513 + 129,
                                                    [[1, P], [513, NH], [1, T]])).then_inc(in_mix, 16)
                sp.dma_start(BRAW[:, 0, :, :], b_re[l]).then_inc(in_mix, 16)
                sp.dma_start(BRAW[:, 1, :, :], b_im[l]).then_inc(in_mix, 16)
                sp.dma_start(CRAW[:, 0, :, :], c_re[l]).then_inc(in_mix, 16)
                sp.dma_start(CRAW[:, 1, :, :], c_im[l]).then_inc(in_mix, 16)
                sp.dma_start(WGLU[:, :, :], w_glu[l].rearrange("(k p) n -> p k n", p=P)).then_inc(in_mix, 16)
                sp.dma_start(MT[:, 0, 0:P], perm_c).then_inc(in_perm, 16)
                m = 16
                for n in range(4, IN_TILES):
                    stream(n)
                    for _ in range(2):
                        if m < 48:
                            ada(m)
                            m += 1
                for n in range(IN_TILES, NSTREAM):
                    if n == TILE_Q:
                        sp.wait_ge(merged, l + 1)
                        sp.dma_start(SUBT[:, :, :], subkeys[l].rearrange("p (n k) -> p n k", k=NK)).then_inc(in_sub, 16)
                    stream(n)
                for v in (0, 1):
                    for e in (0, 1):
                        slot, _ = expert_pos(l, v, e)
                        last = NSTREAM - 1 - (NSTREAM - 1 - slot) % 4
                        sp.wait_ge(q_mm, l * 16 + last - TILE_Q + 1)
                        sp.dma_start(RING[:, slot, :], (v_tab if v else u_tab)[l, e]).then_inc(in_ring[slot], 16)
                with sp.Fori(0, NE // 2 - 1) as i:
                    for b in (0, 1):
                        sp.wait_ge(u_split, i * 2 + (l * NE + b + 1))
                        sp.dma_start(RING[:, b, :], u_tab[l, i * 2 + (b + 2)]).then_inc(in_ring[b], 16)
                        sp.wait_ge(v_split, i * 2 + (l * NE + b + 1))
                        sp.dma_start(RING[:, 2 + b, :], v_tab[l, i * 2 + (b + 2)]).then_inc(in_ring[2 + b], 16)
                sp.wait_ge(v_used, (l + 1) * NE)
                sp.dma_start(IDENT[:, :], ident_c).then_inc(in_const, 16)
                sp.dma_start(IOTA[:, :], iota_c).then_inc(in_const, 16)
            sp.wait_ge(fin, 1)
            sp.dma_start(outT.rearrange("(k p) t -> p k t", p=P), HT[:, :, :]).then_inc(out_done, 16)
            sp.wait_ge(out_done, 16)

        @block.tensor
        def _(pe):
            mm = nc.tensor.matmul

            def sum_squares(n):
                pe.wait_ge(ones_ready, n // 2 + 1)
                pe.wait_ge(squared, n + 1)
                for k in range(KT):
                    last = mm(ps[:, 0:T], ONES[:, :], SQ[:, k, :], start=(k == 0), stop=(k == KT - 1))
                last.then_inc(sumsq, 1)

            for l in range(L):
                pe.wait_ge(in_const, 32 * (l + 1))
                sum_squares(2 * l)

                pe.wait_ge(h_done, 2 * l + 1)
                loaded = set()

                def tile(n):
                    slot, value = ring_pos(l, n)
                    if n not in loaded:
                        pe.wait_ge(in_ring[slot], value)
                        loaded.add(n)
                    return RING[:, slot, :].rearrange("p (k n) -> p k n", n=P)

                for j in range(N_PROJ):
                    if j >= 8:
                        pe.wait_ge(proj_ev, l * N_PROJ + j - 7)
                    if j < 14:
                        w = tile(j)
                        for k in range(KT):
                            last = mm(PS[:, j % 8, 0:T], w[:, k, :], HT[:, k, :], start=(k == 0), stop=(k == KT - 1))
                    else:
                        t = j % 2
                        for a in range(3):
                            w = tile(14 + 3 * ((j - 14) // 2) + a)
                            for k in range(KT):
                                last = mm(PS[:, j % 8, a * P:(a + 1) * P], HT[:, k, t * P:(t + 1) * P], w[:, k, :],
                                          start=(k == 0), stop=(k == KT - 1))
                    last.then_inc(proj_mm, 1)

                pe.wait_ge(in_perm, 16 * (l + 1))
                pe.wait_ge(proj_ev, (l + 1) * N_PROJ)
                for a in range(6):
                    last = mm(ps[:, a * T:(a + 1) * T], MT[:, 0, 0:P], QK[:, a, :], start=True, stop=True)
                last.then_inc(rot_mm, 1)
                for h in range(NH):
                    mm(ps[:, 1536 + h * P:1536 + (h + 1) * P], QA[:, h % 2, h // 2, 0:P], KA[:, h // 2, 0:P],
                       start=True, stop=True)
                for h in range(NH):
                    last = mm(ps[:, 2560 + h * T:2560 + (h + 1) * T], QA[:, h % 2, h // 2, P:T], KA[:, h // 2, :],
                              start=True, stop=True)
                last.then_inc(att_mm, 1)
                pe.wait_ge(rot_done, l + 1)
                pe.wait_ge(att_in, l + 1)
                for h in range(NH):
                    mm(ps[:, h * T:(h + 1) * T], QK[:, 3 + h // 2, 0:P], QM[:, h % 2, h // 2, :], start=True, stop=True)
                for h in range(NH):
                    o = 1536 + h * P
                    last = mm(ps[:, o:o + P], QK[:, 3 + h // 2, P:T], QM[:, h % 2, h // 2, P:T], start=True, stop=True)
                last.then_inc(ret_mm, 1)

                pe.wait_ge(ret_in, l + 1)
                for h in range(NH):
                    mm(PS[:, 6, h * HD:(h + 1) * HD], SR0[:, h, 0:P], VR[:, 0, h * HD:(h + 1) * HD], start=True, stop=True)
                for h in range(NH):
                    o = PS[:, 7, h * HD:(h + 1) * HD]
                    mm(o, SR0[:, h, P:T], VR[:, 0, h * HD:(h + 1) * HD], start=True, stop=False)
                    last = mm(o, SR1[:, h, :], VR[:, 1, h * HD:(h + 1) * HD], start=False, stop=True)
                last.then_inc(ry_mm, 1)

                pe.wait_ge(att_exp, l + 1)
                for h in range(NH):
                    nc.tensor.transpose(ps[:, h * P:(h + 1) * P], SA[:, h, :], IDENT[:, :])
                for h in range(NH):
                    for b in range(2):
                        o = (6 + 2 * h + b) * P
                        last = nc.tensor.transpose(ps[:, o:o + P], SB[:, h, b * P:(b + 1) * P], IDENT[:, :])
                last.then_inc(pt_mm, 1)
                pe.wait_ge(pt_ev, l + 1)
                for h in range(NH):
                    mm(PS[:, 5, h * HD:(h + 1) * HD], PT[:, h, :], VA[:, 0, h * HD:(h + 1) * HD], start=True, stop=True)
                pe.wait_ge(ry_ev, l + 1)
                for h in range(NH):
                    o = PS[:, 6, h * HD:(h + 1) * HD]
                    mm(o, PT[:, 6 + 2 * h, :], VA[:, 0, h * HD:(h + 1) * HD], start=True, stop=False)
                    last = mm(o, PT[:, 7 + 2 * h, :], VA[:, 1, h * HD:(h + 1) * HD], start=False, stop=True)
                last.then_inc(ao_mm, 1)

                pe.wait_ge(bt_done, l + 1)
                for u in range(2):
                    if u:
                        pe.wait_ge(bu_ev, 2 * l + 1)
                    for im, bt in enumerate((BTRE, BTIM)):
                        for r in range(4):
                            o = im * 1024 + r * T
                            last = mm(ps[:, o:o + T], bt[:, u, :], UM[:, u, r, :], start=True, stop=True)
                    last.then_inc(bu_mm, 1)
                    if u == 0:
                        pe.wait_ge(cf_done, l + 1)
                    pe.wait_ge(xs_done, 2 * l + u + 1)
                    for r in range(4):
                        mm(PS[:, 4, u * T:(u + 1) * T], CFRE[:, 4 * u + r, :], ZRE[:, r, :], start=(r == 0), stop=False)
                        last = mm(PS[:, 4, u * T:(u + 1) * T], CFIM[:, 4 * u + r, :], ZIM[:, r, :],
                                  start=False, stop=(r == 3))
                    last.then_inc(sy_mm, 1)
                pe.wait_ge(sy_gelu, l + 1)
                for t in range(TT):
                    for k in range(2):
                        last = mm(PS[:, t, :], YG[:, k, t * P:(t + 1) * P], WGLU[:, k, :], start=(k == 0), stop=(k == 1))
                last.then_inc(glu_mm, 1)

                pe.wait_ge(merged, l + 1)
                for k in range(KT):
                    for t in range(TT):
                        o = 2048 + k * T + t * P
                        last = nc.tensor.transpose(ps[:, o:o + P], MERGED[:, t, k * P:(k + 1) * P], IDENT[:, :])
                last.then_inc(mt_mm, 1)
                pe.wait_ge(mt_ev, l + 1)
                for d in range(KT):
                    w = tile(TILE_OUT + d)
                    for k in range(KT):
                        last = mm(ps[:, d * T:(d + 1) * T], w[:, k, :], MT[:, k, :], start=(k == 0), stop=(k == KT - 1))
                    last.then_inc(wo_mm, 1)

                sum_squares(2 * l + 1)
                pe.wait_ge(h_done, 2 * l + 2)
                pe.wait_ge(in_sub, 16 * (l + 1))
                def key_scores(n):
                    g = l * 16 + n
                    pe.wait_ge(q_ev, g + 1)
                    if n >= 2:
                        pe.wait_ge(ks_ev, g - 1)
                    for t in range(TT):
                        last = mm(PS[:, 6 + n % 2, t * P:(t + 1) * P], QT[:, n % 2, t * P:(t + 1) * P],
                                  SUBT[:, n, :], start=True, stop=True)
                    last.then_inc(ks_mm, 1)
                for n in range(16):
                    w = tile(TILE_Q + n)
                    if n >= 2:
                        pe.wait_ge(q_ev, l * 16 + n - 1)
                    for k in range(KT):
                        last = mm(PS[:, 4 + n % 2, 0:T], w[:, k, :], HT[:, k, :], start=(k == 0), stop=(k == KT - 1))
                    last.then_inc(q_mm, 1)
                    if n:
                        key_scores(n - 1)
                key_scores(15)

                pe.wait_ge(picks, l + 1)
                for a in range(3):
                    for t in range(TT):
                        o = a * T + t * P
                        last = nc.tensor.transpose(ps[:, o:o + P], SEL[:, a, t, :], IDENT[:, :])
                last.then_inc(pickt_mm, 1)
                def gates(g, b):
                    pe.wait_ge(onehot, g + 1)
                    for q in range(4):
                        last = mm(PS[:, 4 + b, q * P:(q + 1) * P], OHB[:, b, q, :], OHA[:, b, q, :], start=True, stop=True)
                    last.then_inc(w_mm, 1)
                for b in range(4):
                    gates(l * 64 + b, b)
                with pe.Fori(1, 16) as i:
                    for b in range(4):
                        pe.wait_ge(w_ev, i * 4 + (l * 64 + b - 3))
                        gates(i * 4 + (l * 64 + b), b)

                def scores(e, b, first):
                    pe.wait_ge(u_split, e + 1)
                    if not first:
                        pe.wait_ge(gelu_done, e - 1)
                    for k in range(KT):
                        mm(PS[:, 4 + b, 0:T], UH[:, b, k, :], HH[:, k, :], start=(k == 0), stop=False)
                        mm(PS[:, 4 + b, 0:T], UH[:, b, k, :], HL[:, k, :], start=False, stop=False)
                        last = mm(PS[:, 4 + b, 0:T], UL[:, b, k, :], HH[:, k, :], start=False, stop=(k == KT - 1))
                    last.then_inc(s_mm, 1)

                def add_experts(e, b, start=False, stop=False):
                    pe.wait_ge(v_split, e + 1)
                    pe.wait_ge(g_ready, e + 1)
                    for t in range(TT):
                        for n, (g, v) in enumerate(((GH, VH), (GH, VL), (GL, VH))):
                            for d in range(2):
                                last = mm(PS[:, 2 * t + d, :], g[:, t * P:(t + 1) * P], v[:, b, d * 512:(d + 1) * 512],
                                          start=start and n == 0, stop=stop and n == 2)
                    last.then_inc(v_used, 1)

                E0 = l * NE
                pe.wait_ge(w_ev, (l + 1) * 64)
                scores(E0, 0, True)
                scores(E0 + 1, 1, l == 0)
                add_experts(E0, 0, start=True)
                scores(E0 + 2, 0, False)
                add_experts(E0 + 1, 1)
                with pe.Fori(1, NE // 2 - 1) as i:
                    for b in (0, 1):
                        scores(i * 2 + (E0 + b + 1), 1 - b, False)
                        add_experts(i * 2 + (E0 + b), b)
                scores(E0 + NE - 1, 1, False)
                add_experts(E0 + NE - 2, 0)
                add_experts(E0 + NE - 1, 1, stop=True)
                pe.wait_ge(acc_ev, l + 1)
                pe.wait_ge(in_const, 32 * (l + 2))
                for k in range(KT):
                    for t in range(TT):
                        o = 2048 + k * T + t * P
                        last = nc.tensor.transpose(ps[:, o:o + P], ACC[:, t, k * P:(k + 1) * P], IDENT[:, :])
                last.then_inc(acc_mm, 1)
            sum_squares(2 * L)

        @block.scalar
        def _(act):
            fn = nc.scalar.activation

            def square(n):
                act.wait_ge(in_x, 16) if n == 0 else act.wait_ge(x_ready, n)
                fn(SQ[:, :, :], X[:, :, :], ACT.Square).then_inc(squared, 1)
                act.wait_ge(var_done, n + 1)
                fn(RSTD[:, :], RSTD[:, :], ACT.Sqrt).then_inc(std_done, 1)

            act.wait_ge(in_cols, 48)
            for l in range(L):
                act.wait_ge(in_c, 16 * (l + 1))
                fn(CE[:, :], CB[:, :], ACT.Exp, scale=-1.0).then_inc(cond_exp, 1)
                square(2 * l)
                act.wait_ge(normed, 2 * l + 1)
                for k in range(KT):
                    last = fn(HT[:, k, :], HT[:, k, :], ACT.Identity, scale=AMP[:, k:k + 1], bias=MOD[:, SH1, k:k + 1])
                last.then_inc(h_done, 1)

                place = ([(UT[:, a, :], 1.0) for a in range(2)] + [(QK[:, a, :], 1.0) for a in range(6)]
                         + [(QA[:, :, a, :], None) for a in range(3)] + [(KA[:, a, :], 1.0) for a in range(3)]
                         + [(o[:, t, :], 1.0) for o in (VA, VR, GR) for t in range(TT)])
                for j, (o, scale) in enumerate(place):
                    act.wait_ge(proj_mm, l * N_PROJ + j + 1)
                    if scale is None:
                        for parity in range(2):
                            last = fn(o[:, parity, :], PS[:, j % 8, 0:T], ACT.Copy, scale=MASK[:, 6 + parity:7 + parity])
                        last.then_inc(proj_ev, 1)
                    else:
                        fn(o, PS[:, j % 8, 0:o.shape[-1]], ACT.Copy).then_inc(proj_ev, 1)

                fn(SV[:, 0, :], COLS[:, l, C_LDT:C_LDT + ST], ACT.Exp).then_inc(ssm_x, 1)
                act.wait_ge(ssm_e, l + 1)
                fn(SV[:, 2, :], SV[:, 1, :], ACT.Exp).then_inc(ssm_x, 1)
                act.wait_ge(att_sub, l + 1)
                fn(SAB[:, :], SAB[:, :], ACT.Exp).then_inc(att_exp, 1)
                act.wait_ge(rot_done, l + 1)
                fn(GEXP, GR[:, :, :], ACT.Exp, scale=-1.0).then_inc(gexp, 1)
                act.wait_ge(pt_mm, l + 1)
                fn(PT[:, :, :], ps[:, 0:18 * P].rearrange("p (n k) -> p n k", k=P), ACT.Copy).then_inc(pt_ev, 1)
                act.wait_ge(rvar, l + 1)
                fn(SM[:, 3, :], SM[:, 3, :], ACT.Sqrt).then_inc(rstd_done, 1)
                act.wait_ge(ssm_a, 3 * l + 1)
                fn(SV[:, 6, :], SV[:, 5, :], ACT.Sin)
                fn(SV[:, 7, :], SV[:, 5, :], ACT.Sin, scale=0.5).then_inc(ssm_s, 1)
                for u in range(2):
                    act.wait_ge(ssm_a, 3 * l + 2 + u)
                    fn(SIN[:, :, :], TA[:, :, :], ACT.Sin)
                    fn(COS[:, :, :], TA[:, :, :], ACT.Sin, scale=0.5).then_inc(ssm_s, 1)
                act.wait_ge(sy_in, l + 1)
                fn(YG[:, :, :], YG[:, :, :], ACT.Gelu_apprx_tanh).then_inc(sy_gelu, 1)
                act.wait_ge(glu_mm, l + 1)
                fn(ZG[:, :, :], PS[:, 0:2, SW:2 * SW], ACT.Exp, scale=-1.0).then_inc(glu_exp, 1)
                act.wait_ge(mvar, l + 1)
                fn(RMS[:, :], RMS[:, :], ACT.Sqrt).then_inc(mstd, 1)
                act.wait_ge(mt_mm, l + 1)
                for k in range(KT):
                    last = fn(MT[:, k, :], ps[:, 2048 + k * T:2048 + (k + 1) * T], ACT.Copy,
                              scale=COLS[:, l, C_GAIN + k:C_GAIN + k + 1])
                last.then_inc(mt_ev, 1)

                square(2 * l + 1)
                act.wait_ge(normed, 2 * l + 2)
                for k in range(KT):
                    last = fn(HT[:, k, :], HT[:, k, :], ACT.Identity, scale=AMP[:, k:k + 1], bias=MOD[:, SH2, k:k + 1])
                last.then_inc(h_done, 1)
                act.wait_ge(h_done, 2 * l + 2)
                fn(HH[:, :, :], HT[:, :, :], ACT.Copy).then_inc(h_hi, 1)
                for n in range(16):
                    act.wait_ge(q_mm, l * 16 + n + 1)
                    if n >= 2:
                        act.wait_ge(ks_mm, l * 16 + n - 1)
                    fn(QT[:, n % 2, :], PS[:, 4 + n % 2, 0:T], ACT.Copy).then_inc(q_ev, 1)
                act.wait_ge(gate_in, l + 1)
                fn(SEL[:, 2, :, :], SEL[:, 2, :, :], ACT.Exp).then_inc(gate_exp, 1)
                act.wait_ge(pickt_mm, l + 1)
                fn(SELT[:, :, :], ps[:, 0:3 * T].rearrange("p (a t) -> p a t", a=3), ACT.Copy).then_inc(pickt, 1)

                def gates(g, b, tok):
                    act.wait_ge(w_mm, g + 1)
                    fn(WT[:, :, bass.ds(tok, 4)], PS[:, 4 + b, :].rearrange("p (t i) -> p i t", t=4),
                       ACT.Copy).then_inc(w_ev, 1)
                for b in range(4):
                    gates(l * 64 + b, b, b * 4)
                with act.Fori(1, 16) as i:
                    for b in range(4):
                        gates(i * 4 + (l * 64 + b), b, i * 16 + b * 4)

                E0 = l * NE

                def u_high(e, b, i):
                    slot, n = expert_pos(l, 0, b)
                    act.wait_ge(in_ring[slot], i * 16 + n * 16)
                    return fn(UH[:, b, :, :], RING[:, slot, :].rearrange("p (k n) -> p k n", n=P), ACT.Copy).then_inc(u_hi, 1)

                def v_high(e, b, i):
                    slot, n = expert_pos(l, 1, b)
                    act.wait_ge(in_ring[slot], i * 16 + n * 16)
                    return fn(VH[:, b, :], RING[:, slot, :], ACT.Copy).then_inc(v_hi, 1)

                def gelu(e, b):
                    act.wait_ge(s_mm, e + 1)
                    return fn(GE[:, b, :], PS[:, 4 + b, 0:T], ACT.Gelu_apprx_tanh).then_inc(gelu_done, 1)

                u_high(E0, 0, 0)
                for e in (0, 1):
                    if e == 1:
                        act.wait_ge(s_mm, E0 + 1)
                    u_high(E0 + e + 1, (e + 1) % 2, (e + 1) // 2)
                    v_high(E0 + e, e, 0)
                    gelu(E0 + e, e)
                with act.Fori(1, NE // 2 - 1) as i:
                    for b in (0, 1):
                        act.wait_ge(s_mm, i * 2 + (E0 + b))
                        u_high(i * 2 + (E0 + b + 1), 1 - b, i + b)
                        act.wait_ge(v_used, i * 2 + (E0 + b - 1))
                        v_high(i * 2 + (E0 + b), b, i)
                        act.wait_ge(g_ready, i * 2 + (E0 + b - 1))
                        gelu(i * 2 + (E0 + b), b)
                for e in (NE - 2, NE - 1):
                    if e < NE - 1:
                        act.wait_ge(s_mm, E0 + e)
                        u_high(E0 + e + 1, 1, NE // 2 - 1)
                    act.wait_ge(v_used, E0 + e - 1)
                    v_high(E0 + e, e % 2, NE // 2 - 1)
                    act.wait_ge(g_ready, E0 + e - 1)
                    gelu(E0 + e, e % 2)
                act.wait_ge(v_used, E0 + NE)
                fn(ACC[:, :, :], PS[:, 0:4, :], ACT.Copy).then_inc(acc_ev, 1)
            square(2 * L)
            act.wait_ge(normed, 2 * L + 1)
            for k in range(KT):
                last = fn(HT[:, k, :], HT[:, k, :], ACT.Copy, scale=FCOL[:, k:k + 1])
            last.then_inc(fin, 1)

        @block.vector
        def _(dve):
            v = nc.vector
            steps = [0]

            def link(ins):
                steps[0] += 1
                ins.then_inc(dve_step, 1)
                dve.wait_ge(dve_step, steps[0])

            def norm(n):
                dve.wait_ge(sumsq, n + 1)
                v.tensor_scalar(RSTD[:, :], ps[:, 0:T], 1.0 / D, EPS, ALU.mult, ALU.add).then_inc(var_done, 1)
                dve.wait_ge(std_done, n + 1)
                link(v.reciprocal(RSTD[:, :], RSTD[:, :]))
                v.tensor_tensor(HT[:, :, :], X[:, :, :], RSTD[:, :].unsqueeze(1).to_broadcast([P, KT, T]),
                                ALU.mult).then_inc(normed, 1)

            def modulate(which, gain):
                v.scalar_tensor_tensor(AMP[:, :], MOD[:, which, :], 1.0, COLS[:, l, gain:gain + KT], ALU.add, ALU.mult)

            def wrap(out, x, k):
                link(v.tensor_scalar(k, x, 1.0 / (2 * math.pi), ROUND, ALU.mult, ALU.add))
                link(v.tensor_scalar(k, k, ROUND, None, ALU.subtract))
                link(v.scalar_tensor_tensor(out, k, -TWO_PI_HI, x, ALU.mult, ALU.add))
                link(v.scalar_tensor_tensor(out, k, -TWO_PI_LO, out, ALU.mult, ALU.add))
                return v.tensor_scalar(out, out, PI, -PI, ALU.min, ALU.max)

            def top16(rows, vals, idx):
                for half in range(2):
                    o = slice(8 * half, 8 * half + 8)
                    for r, a in zip(rows, vals):
                        last = v.max(a[:, o], r)
                    link(last)
                    for r, a, n in zip(rows, vals, idx):
                        last = v.max_index(n[:, o], a[:, o], r)
                    if half == 0:
                        link(last)
                        for r, a in zip(rows, vals):
                            last = v.match_replace(r, a[:, o], r, -3.0e38)
                    link(last)

            dve.wait_ge(in_cols, 48)
            for l in range(L):
                v.memset(ONES[:, :], 1.0).then_inc(ones_ready, 1)
                dve.wait_ge(cond_exp, l + 1)
                link(v.tensor_scalar(CE[:, :], CE[:, :], 1.0, None, ALU.add))
                link(v.reciprocal(CE[:, :], CE[:, :]))
                link(v.tensor_tensor(CB[:, :], CB[:, :], CE[:, :], ALU.mult))

                def ada(i):
                    for j in range(8):
                        dve.wait_ge(in_ada[j], i * 16 + (l * 6 + 1) * 16)
                        v.tensor_tensor_reduce(out=ADA[:, j, :], in0=ADA[:, j, :], in1=CB[:, :], scale=1.0, scalar=0.0,
                                               op0=ALU.mult, op1=ALU.add, accum_out=ADA8[:, j:j + 1]).then_inc(ada_used, 1)
                    dve.wait_ge(ada_used, i * 8 + (l * 48 + 8))
                    v.tensor_tensor(MOD[:, i, :], ADA8[:, :], COLS[:, l, bass.ds(i * 8, 8)], ALU.add).then_inc(mod_done, 1)
                    dve.wait_ge(mod_done, i + (l * 6 + 1))
                with dve.Fori(0, 2) as i:
                    ada(i)
                link(v.scalar_tensor_tensor(AMP[:, :], MOD[:, SC1, :], 1.0, COLS[:, l, C_NMIX:C_NMIX + KT],
                                            ALU.add, ALU.mult))
                norm(2 * l)
                with dve.Fori(2, 6) as i:
                    ada(i)

                lre, lim = (COLS[:, l, o:o + ST] for o in (C_LRE, C_LIM))
                sv = lambda n: SV[:, n, :]
                dve.wait_ge(ssm_x, 2 * l + 1)
                v.tensor_tensor(sv(1), lre, sv(0), ALU.mult).then_inc(ssm_e, 1)
                link(v.tensor_tensor(sv(3), lim, sv(0), ALU.mult))
                wrap(sv(5), sv(3), sv(4)).then_inc(ssm_a, 1)

                dve.wait_ge(in_mix, 144 * (l + 1))
                dve.wait_ge(rot_mm, l + 1)
                v.tensor_tensor(ROT[:, :, :], ps[:, 0:1536].rearrange("p (a t) -> p a t", t=T),
                                ROPE[:, 1, :].unsqueeze(1).to_broadcast([P, 6, T]), ALU.mult)
                link(v.tensor_tensor(QK[:, :, :], QK[:, :, :], ROPE[:, 0, :].unsqueeze(1).to_broadcast([P, 6, T]), ALU.mult))
                link(v.tensor_tensor(QK[:, :, :], QK[:, :, :], ROT[:, :, :], ALU.add))
                for parity in range(2):
                    last = v.tensor_scalar(QM[:, parity, :, :], QK[:, 0:3, :], MASK[:, 8 + parity:9 + parity], None, ALU.mult)
                last.then_inc(rot_done, 1)

                dve.wait_ge(att_mm, l + 1)
                v.tensor_tensor(SA[:, :, :], ps[:, 1536:2304].rearrange("p (h t) -> p h t", h=NH),
                                bass.AP(BIAS, P - 1, [[NH * T, P], [T, NH], [-1, P]]), ALU.add)
                link(v.tensor_tensor(SB[:, :, :], ps[:, 2560:4096].rearrange("p (h t) -> p h t", h=NH),
                                     bass.AP(BIAS, T - 1, [[NH * T, P], [T, NH], [-1, T]]), ALU.add))
                v.memset(SA[0:CHUNK, :, CHUNK:P], NEG)
                link(v.memset(SB[0:CHUNK, :, T - CHUNK:T], NEG))
                v.reduce_max(SM[:, 0, 0:NH], SA[:, :, :], AX.X).then_inc(att_in, 1)
                link(v.reduce_max(SM[:, 0, NH:12], SB[:, :, :], AX.X))
                v.tensor_tensor(SA[:, :, :], SA[:, :, :], SM[:, 0, 0:NH].unsqueeze(2).to_broadcast([P, NH, P]), ALU.subtract)
                v.tensor_tensor(SB[:, :, :], SB[:, :, :], SM[:, 0, NH:12].unsqueeze(2).to_broadcast([P, NH, T]),
                                ALU.subtract).then_inc(att_sub, 1)

                dve.wait_ge(ret_mm, l + 1)
                v.tensor_tensor(SR0[:, :, :], ps[:, 0:1536].rearrange("p (h t) -> p h t", h=NH), DEC0[:, :, :], ALU.mult)
                v.tensor_tensor(SR1[:, :, :], ps[:, 1536:2304].rearrange("p (h t) -> p h t", h=NH), DEC1[:, :, :],
                                ALU.mult).then_inc(ret_in, 1)
                dve.wait_ge(att_exp, l + 1)
                v.reduce_sum(SM[:, 1, 0:NH], SA[:, :, :], AX.X)
                link(v.reduce_sum(SM[:, 1, NH:12], SB[:, :, :], AX.X))
                link(v.reciprocal(SM[:, 1, :], SM[:, 1, :]))

                yr = YR[:, :, :].rearrange("p t (h e) -> p (t h) e", e=HD)
                dve.wait_ge(ry_mm, l + 1)
                v.tensor_copy(YR[:, :, :], PS[:, 6:8, 0:AW]).then_inc(ry_ev, 1)
                dve.wait_ge(ry_ev, l + 1)
                link(v.reduce_sum(SM[:, 2, :], yr, AX.X))
                link(v.tensor_scalar(SM[:, 2, :], SM[:, 2, :], -1.0 / HD, None, ALU.mult))
                link(v.tensor_tensor(yr, yr, SM[:, 2, :].unsqueeze(2).to_broadcast([P, 12, HD]), ALU.add))
                link(v.tensor_tensor(YSQ, yr, yr, ALU.mult))
                link(v.reduce_sum(SM[:, 3, :], YSQ, AX.X))
                v.tensor_scalar(SM[:, 3, :], SM[:, 3, :], 1.0 / HD, EPS, ALU.mult, ALU.add).then_inc(rvar, 1)
                dve.wait_ge(gexp, l + 1)
                link(v.tensor_scalar(GEXP, GEXP, 1.0, None, ALU.add))
                link(v.reciprocal(GEXP, GEXP))
                link(v.tensor_tensor(GEXP, GEXP, GR[:, :, :], ALU.mult))
                dve.wait_ge(rstd_done, l + 1)
                link(v.reciprocal(SM[:, 3, :], SM[:, 3, :]))
                link(v.tensor_tensor(yr, yr, SM[:, 3, :].unsqueeze(2).to_broadcast([P, 12, HD]), ALU.mult))
                link(v.tensor_tensor(MERGED[:, :, AW:2 * AW], YR[:, :, :], GEXP, ALU.mult))

                dve.wait_ge(ao_mm, l + 1)
                for t in range(TT):
                    link(v.tensor_tensor(MERGED[:, t, 0:AW].rearrange("p (h e) -> p h e", e=HD),
                                         PS[:, 5 + t, 0:AW].rearrange("p (h e) -> p h e", e=HD),
                                         SM[:, 1, t * NH:(t + 1) * NH].unsqueeze(2).to_broadcast([P, NH, HD]), ALU.mult))
                for t in range(TT):
                    link(v.tensor_tensor_reduce(out=SCR[:, 0:AW], in0=MERGED[:, t, 0:AW], in1=MERGED[:, t, 0:AW],
                                                scale=1.0, scalar=0.0, op0=ALU.mult, op1=ALU.add,
                                                accum_out=RMS[:, t:t + 1]))

                for u in range(2):
                    v.tensor_tensor(UM[:, u, :, :], UT[:, u, :].unsqueeze(1).to_broadcast([P, 4, T]),
                                    MASK[:, 2:6].unsqueeze(2).to_broadcast([P, 4, T]), ALU.mult)
                for n, bt in enumerate((BTRE, BTIM)):
                    for half in range(2):
                        last = v.tensor_scalar(bt[:, :, half * STATES:(half + 1) * STATES], BRAW[:, n, :, :],
                                               MASK[:, half:half + 1], None, ALU.mult)
                last.then_inc(bt_done, 1)
                dve.wait_ge(ssm_x, 2 * l + 2)
                dve.wait_ge(ssm_s, 3 * l + 1)
                link(v.tensor_tensor(sv(8), sv(7), sv(7), ALU.mult))
                link(v.tensor_scalar(sv(8), sv(8), -2.0, 1.0, ALU.mult, ALU.add))
                link(v.tensor_tensor(sv(8), sv(8), sv(2), ALU.mult))
                link(v.tensor_scalar(sv(8), sv(8), 1.0, None, ALU.subtract))
                link(v.tensor_tensor(sv(9), sv(6), sv(2), ALU.mult))
                link(v.tensor_tensor(sv(10), lre, lre, ALU.mult))
                link(v.tensor_tensor(sv(11), lim, lim, ALU.mult))
                link(v.tensor_tensor(sv(10), sv(10), sv(11), ALU.add))
                link(v.reciprocal(sv(10), sv(10)))
                link(v.tensor_tensor(sv(11), sv(8), lre, ALU.mult))
                link(v.tensor_tensor(sv(12), sv(9), lim, ALU.mult))
                link(v.tensor_tensor(sv(11), sv(11), sv(12), ALU.add))
                link(v.tensor_tensor(sv(13), sv(11), sv(10), ALU.mult))
                link(v.tensor_tensor(sv(11), sv(9), lre, ALU.mult))
                link(v.tensor_tensor(sv(12), sv(8), lim, ALU.mult))
                link(v.tensor_tensor(sv(11), sv(11), sv(12), ALU.subtract))
                link(v.tensor_tensor(sv(14), sv(11), sv(10), ALU.mult))
                bc = lambda n: SV[:, n, :].unsqueeze(2).to_broadcast([P, ST, GCH])
                v.memset(CFRE[:, :, :], 0.0)
                v.memset(CFIM[:, :, :], 0.0)
                v.tensor_tensor(CTMP[:, 0, :, :], CRAW[:, 0, :, :], bc(13), ALU.mult)
                v.tensor_tensor(CTMP[:, 1, :, :], CRAW[:, 1, :, :], bc(14), ALU.mult)
                v.tensor_tensor(CTMP[:, 2, :, :], CRAW[:, 0, :, :], bc(14), ALU.mult)
                link(v.tensor_tensor(CTMP[:, 3, :, :], CRAW[:, 1, :, :], bc(13), ALU.mult))
                v.tensor_tensor(CTMP[:, 0, :, :], CTMP[:, 0, :, :], CTMP[:, 1, :, :], ALU.subtract)
                link(v.tensor_tensor(CTMP[:, 2, :, :], CTMP[:, 2, :, :], CTMP[:, 3, :, :], ALU.add))
                for n, (cf, sign) in enumerate(((CFRE, 1.0), (CFIM, -1.0))):
                    for g in range(2):
                        rows = slice(g * STATES, (g + 1) * STATES)
                        out = bass.AP(cf, g * STATES * ST * P + GCH * g, [[ST * P, STATES], [4 * P, 2], [P + 32, 4], [1, GCH]])
                        last = v.tensor_scalar(out, CTMP[rows, 2 * n, :, :].rearrange("p (u r) c -> p u r c", r=4),
                                               sign, None, ALU.mult)
                last.then_inc(cf_done, 1)

                for u in range(2):
                    link(v.tensor_tensor(TB[:, :, :], IOTA[:, :].unsqueeze(1).to_broadcast([P, 4, T]),
                                         SV[:, 5, 4 * u:4 * u + 4].unsqueeze(2).to_broadcast([P, 4, T]), ALU.mult))
                    wrap(TA[:, :, :], TB[:, :, :], TURNS[:, :, :]).then_inc(ssm_a, 1)
                    dve.wait_ge(ssm_s, 3 * l + 2 + u)
                    link(v.tensor_tensor(COS[:, :, :], COS[:, :, :], COS[:, :, :], ALU.mult))
                    link(v.tensor_scalar(COS[:, :, :], COS[:, :, :], -2.0, 1.0, ALU.mult, ALU.add))
                    dve.wait_ge(bu_mm, 2 * l + u + 1)
                    bre = ps[:, 0:1024].rearrange("p (r t) -> p r t", t=T)
                    bim = ps[:, 1024:2048].rearrange("p (r t) -> p r t", t=T)
                    if u:
                        dve.wait_ge(sy_mm, 2 * l + 1)
                    v.tensor_tensor(TA[:, :, :], COS[:, :, :], bre, ALU.mult)
                    link(v.tensor_tensor(TB[:, :, :], SIN[:, :, :], bim, ALU.mult))
                    link(v.tensor_tensor(ZRE[:, :, :], TA[:, :, :], TB[:, :, :], ALU.add))
                    v.tensor_tensor(TA[:, :, :], COS[:, :, :], bim, ALU.mult)
                    link(v.tensor_tensor(TB[:, :, :], SIN[:, :, :], bre, ALU.mult))
                    v.tensor_tensor(ZIM[:, :, :], TA[:, :, :], TB[:, :, :], ALU.subtract).then_inc(bu_ev, 1)
                    dve.wait_ge(bu_ev, 2 * l + u + 1)
                    for r in range(4):
                        mag = SV[:, 2, 4 * u + r:4 * u + r + 1].to_broadcast([P, T])
                        v.tensor_tensor_scan(ZRE[:, r, :], mag, ZRE[:, r, :], 0.0, ALU.mult, ALU.add)
                        last = v.tensor_tensor_scan(ZIM[:, r, :], mag, ZIM[:, r, :], 0.0, ALU.mult, ALU.add)
                    link(last)
                    v.tensor_tensor(TA[:, :, :], COS[:, :, :], ZRE[:, :, :], ALU.mult)
                    v.tensor_tensor(TB[:, :, :], SIN[:, :, :], ZIM[:, :, :], ALU.mult)
                    v.tensor_tensor(COS[:, :, :], COS[:, :, :], ZIM[:, :, :], ALU.mult)
                    link(v.tensor_tensor(SIN[:, :, :], SIN[:, :, :], ZRE[:, :, :], ALU.mult))
                    v.tensor_tensor(ZRE[:, :, :], TA[:, :, :], TB[:, :, :], ALU.subtract)
                    v.tensor_tensor(ZIM[:, :, :], COS[:, :, :], SIN[:, :, :], ALU.add).then_inc(xs_done, 1)
                    dve.wait_ge(xs_done, 2 * l + u + 1)
                dve.wait_ge(sy_mm, 2 * l + 2)
                for u in range(2):
                    last = v.scalar_tensor_tensor(YG[:, u, :], UT[:, u, :], COLS[:, l, C_D + u:C_D + u + 1],
                                                  PS[:, 4, u * T:(u + 1) * T], ALU.mult, ALU.add)
                last.then_inc(sy_in, 1)
                dve.wait_ge(glu_exp, l + 1)
                link(v.tensor_scalar(ZG[:, :, :], ZG[:, :, :], 1.0, None, ALU.add))
                link(v.reciprocal(ZG[:, :, :], ZG[:, :, :]))
                link(v.tensor_tensor(MERGED[:, :, 2 * AW:D], PS[:, 0:2, 0:SW], ZG[:, :, :], ALU.mult))
                for t in range(TT):
                    last = v.tensor_tensor_reduce(out=SCR[:, 0:SW], in0=MERGED[:, t, 2 * AW:D], in1=MERGED[:, t, 2 * AW:D],
                                                  scale=1.0, scalar=0.0, op0=ALU.mult, op1=ALU.add,
                                                  accum_out=RMS[:, 2 + t:3 + t])
                    link(last)
                v.tensor_scalar(RMS[:, 0:2], RMS[:, 0:2], 1.0 / AW, EPS, ALU.mult, ALU.add)
                v.tensor_scalar(RMS[:, 2:4], RMS[:, 2:4], 1.0 / SW, EPS, ALU.mult, ALU.add).then_inc(mvar, 1)
                dve.wait_ge(mstd, l + 1)
                link(v.reciprocal(RMS[:, :], RMS[:, :]))
                for t in range(TT):
                    v.tensor_scalar(MERGED[:, t, 0:AW], MERGED[:, t, 0:AW], RMS[:, t:t + 1], None, ALU.mult)
                    last = v.tensor_scalar(MERGED[:, t, 2 * AW:D], MERGED[:, t, 2 * AW:D], RMS[:, 2 + t:3 + t], None, ALU.mult)
                last.then_inc(merged, 1)

                for d in range(KT):
                    dve.wait_ge(wo_mm, l * KT + d // 2 * 2 + 2)
                    last = v.scalar_tensor_tensor(X[:, d, :], ps[:, d * T:(d + 1) * T], MOD[:, G1, d:d + 1], X[:, d, :],
                                                  ALU.mult, ALU.add)
                last.then_inc(x_ready, 1)
                dve.wait_ge(x_ready, 2 * l + 1)
                link(v.scalar_tensor_tensor(AMP[:, :], MOD[:, SC2, :], 1.0, COLS[:, l, C_NFFN:C_NFFN + KT],
                                            ALU.add, ALU.mult))
                norm(2 * l + 1)
                dve.wait_ge(h_hi, l + 1)
                v.tensor_tensor(HL[:, :, :], HT[:, :, :], HH[:, :, :].bitcast(F32), ALU.subtract).then_inc(h_split, 1)

                for n in range(16):
                    dve.wait_ge(ks_mm, l * 16 + n + 1)
                    v.tensor_copy(KS[:, :, n, :], PS[:, 6 + n % 2, 0:T].rearrange("p (t k) -> p t k", t=TT)).then_inc(ks_ev, 1)
                    dve.wait_ge(ks_ev, l * 16 + n + 1)
                    top16([KS[:, t, n, :] for t in range(TT)], [V16[:, t, n, :] for t in range(TT)],
                          [I16[:, t, n, :] for t in range(TT)])
                link(v.tensor_copy(I16F[:, :, :, :], I16[:, :, :, :]))
                for t in range(TT):
                    side = V16[:, t, :, :].rearrange("p (h s) a -> p h s a", s=2)
                    link(v.tensor_tensor(CAND[:, :, :, :], side[:, :, 0, :].unsqueeze(3).to_broadcast([P, PH, TOPK, TOPK]),
                                         side[:, :, 1, :].unsqueeze(2).to_broadcast([P, PH, TOPK, TOPK]), ALU.add))
                    for h in range(0, PH, 4):
                        top16([CAND[:, g, :, :].rearrange("p a b -> p (a b)") for g in range(h, h + 4)],
                              [BEST[:, t, g, :] for g in range(h, h + 4)], [POS[:, t, g, :] for g in range(h, h + 4)])
                gate = SEL[:, 2, :, :].rearrange("p t (h k) -> p t h k", h=PH)
                for t in range(TT):
                    last = v.tensor_tensor(gate[:, t], BEST[:, t, :, :], BEST[:, t, :, 0:1].to_broadcast([P, PH, TOPK]), ALU.subtract)
                last.then_inc(gate_in, 1)
                v.tensor_scalar(POSA[:, :, :, :], POS[:, :, :, :], 4, None, ALU.logical_shift_right)
                link(v.tensor_scalar(POSB[:, :, :, :], POS[:, :, :, :], 15, None, ALU.bitwise_and))
                v.tensor_copy(AF[:, :, :, :], POSA[:, :, :, :])
                link(v.tensor_copy(BF[:, :, :, :], POSB[:, :, :, :]))
                for s, pos in enumerate((AF, BF)):
                    for t in range(TT):
                        keys = I16F[:, t, :, :].rearrange("p (h s) a -> p h s a", s=2)[:, :, s, :]
                        link(v.tensor_tensor(EQ[:, :, :, :], pos[:, t, :, :].unsqueeze(3).to_broadcast([P, PH, TOPK, TOPK]),
                                             IOTA[:, 0:TOPK].unsqueeze(1).unsqueeze(1).to_broadcast([P, PH, TOPK, TOPK]),
                                             ALU.is_equal))
                        link(v.tensor_tensor(EQ[:, :, :, :], EQ[:, :, :, :],
                                             keys.unsqueeze(2).to_broadcast([P, PH, TOPK, TOPK]), ALU.mult))
                        link(v.reduce_sum(SEL[:, s, t, :].rearrange("p (h k) -> p h k", h=PH), EQ[:, :, :, :], AX.X))
                dve.wait_ge(gate_exp, l + 1)
                link(v.reduce_sum(GSUM[:, :, :], gate, AX.X))
                link(v.reciprocal(GSUM[:, :, :], GSUM[:, :, :]))
                for t in range(TT):
                    last = v.tensor_tensor(gate[:, t], gate[:, t], GSUM[:, t, :].unsqueeze(2).to_broadcast([P, PH, TOPK]), ALU.mult)
                last.then_inc(picks, 1)

                dve.wait_ge(pickt, l + 1)

                def onehots(b, tok):
                    for q in range(4):
                        one = lambda a: SELT[:, a, bass.ds(tok + q, 1)]
                        v.tensor_scalar(OHB[:, b, q, :], IOTA[:, 0:P], one(1), None, ALU.is_equal)
                        last = v.tensor_scalar(OHA[:, b, q, :], IOTA[:, 0:P], one(0), one(2), ALU.is_equal, ALU.mult)
                    last.then_inc(onehot, 1)
                for b in range(4):
                    onehots(b, 4 * b)
                with dve.Fori(1, 16) as i:
                    for b in range(4):
                        dve.wait_ge(w_mm, i * 4 + (l * 64 + b - 3))
                        onehots(b, i * 16 + 4 * b)

                E0 = l * NE

                def u_low(e, b):
                    dve.wait_ge(u_hi, e + 1)
                    v.tensor_tensor(UL[:, b, :, :], RING[:, b, :].rearrange("p (k n) -> p k n", n=P),
                                    UH[:, b, :, :].bitcast(F32), ALU.subtract).then_inc(u_split, 1)

                def v_low(e, b):
                    dve.wait_ge(v_hi, e + 1)
                    v.tensor_tensor(VL[:, b, :], RING[:, 2 + b, :], VH[:, b, :].bitcast(F32), ALU.subtract).then_inc(v_split, 1)

                def gated(e, b, i, first=False):
                    dve.wait_ge(gelu_done, e + 1)
                    if not first:
                        dve.wait_ge(g_ready, e)
                    v.tensor_tensor(G32[:, :], GE[:, b, :], WT[:, i, :], ALU.mult).then_inc(g_prod, 1)
                    dve.wait_ge(g_prod, e + 1)
                    if not first:
                        dve.wait_ge(v_used, e)
                    v.tensor_copy(GH[:, :], G32[:, :]).then_inc(g_hi, 1)
                    dve.wait_ge(g_hi, e + 1)
                    v.tensor_tensor(GL[:, :], G32[:, :], GH[:, :].bitcast(F32), ALU.subtract).then_inc(g_ready, 1)

                dve.wait_ge(w_ev, (l + 1) * 64)
                u_low(E0, 0)
                for e in (0, 1):
                    u_low(E0 + e + 1, (e + 1) % 2)
                    v_low(E0 + e, e)
                    gated(E0 + e, e, e, first=(e == 0))
                with dve.Fori(1, NE // 2 - 1) as i:
                    for b in (0, 1):
                        u_low(i * 2 + (E0 + b + 1), 1 - b)
                        v_low(i * 2 + (E0 + b), b)
                        gated(i * 2 + (E0 + b), b, i * 2 + b)
                u_low(E0 + NE - 1, 1)
                for e in (NE - 2, NE - 1):
                    v_low(E0 + e, e % 2)
                    gated(E0 + e, e % 2, e)
                dve.wait_ge(acc_mm, l + 1)
                for k in range(KT):
                    last = v.scalar_tensor_tensor(X[:, k, :], ps[:, 2048 + k * T:2048 + (k + 1) * T], MOD[:, G2, k:k + 1],
                                                  X[:, k, :], ALU.mult, ALU.add)
                last.then_inc(x_ready, 1)
                dve.wait_ge(x_ready, 2 * l + 2)
            v.memset(ONES[:, :], 1.0).then_inc(ones_ready, 1)
            norm(2 * L)


def _tables():
    inv = np.float32(10000.0) ** (-np.arange(32, dtype=np.float32) / np.float32(32))
    ang = inv[:, None] * np.arange(T, dtype=np.float32)[None, :]
    cos, sin = np.cos(ang), np.sin(ang)
    rope = np.stack([np.concatenate([cos] * 4), np.concatenate([-sin, sin] * 2)], axis=1)
    perm = np.zeros((P, P), np.float32)
    for p in range(P):
        perm[p ^ 32, p] = 1.0
    log_g = np.log1p(-np.power(2.0, -5.0 - np.arange(NH)))
    tk, tq = np.arange(T)[:, None], np.arange(T)[None, :]
    dec = np.exp(log_g[:, None, None] * np.abs(tq - tk)) * (tk // CHUNK <= tq // CHUNK) * HD ** -0.5
    dec0 = dec[:, :P, :].transpose(1, 0, 2).reshape(P, -1)
    dec1 = dec[:, P:, P:].transpose(1, 0, 2).reshape(P, -1)
    p = np.arange(P)[:, None]
    mask = np.concatenate([p // GCH % 2 == np.arange(2), p // 32 == np.arange(4), (p // HD == np.arange(2)) * HD ** -0.5,
                           p // HD == np.arange(2)], axis=1)
    f = lambda a: np.ascontiguousarray(a, dtype=np.float32)
    return dict(ident_c=np.eye(P, dtype=np.float32), iota_c=f(np.broadcast_to(np.arange(T), (P, T))),
                decay_c=f(np.concatenate([dec0, dec1], axis=1)), rope_c=f(rope), perm_c=perm, mask_c=f(mask))


def _layout(i):
    col = lambda a: a.reshape(L, -1, P).transpose(0, 2, 1)
    wtile = lambda w: w.reshape(L, KT, P, -1, P).transpose(0, 3, 2, 1, 4).reshape(L, -1, P, D)
    ldt = np.repeat(i["ssm_log_dt"], STATES, axis=1)
    cols = np.concatenate([col(i[n]) for n in ("b_ada", "norm_mix", "norm_ffn", "merge_gain", "ssm_d",
                                               "ssm_lambda_re", "ssm_lambda_im")] + [col(ldt)], axis=2)
    bt = lambda b: b.transpose(0, 1, 3, 2).reshape(L, 2, P, STATES).transpose(0, 2, 1, 3)
    ct = lambda c: c.reshape(L, ST, 2, GCH, STATES).transpose(0, 2, 4, 1, 3).reshape(L, P, ST, GCH)
    return dict(
        xT=i["x"][0].T, c=i["c"][0], cols=cols.transpose(1, 0, 2), fcol=i["final_norm"].reshape(KT, P).T,
        w_ada=i["w_ada"].transpose(0, 2, 1), w_in=wtile(i["w_in"]), w_out=wtile(i["w_out"]), w_q=wtile(i["peer_w_q"]),
        w_glu=i["w_glu"], rel_bias=i["rel_bias"], b_re=bt(i["ssm_b_re"]), b_im=bt(i["ssm_b_im"]),
        c_re=ct(i["ssm_c_re"]), c_im=ct(i["ssm_c_im"]),
        subkeys=i["peer_subkeys"].reshape(L, 16 * NK, P).transpose(0, 2, 1),
        u_tab=i["peer_u"].reshape(L, NE, P, KT, P).transpose(0, 1, 4, 3, 2).reshape(L, NE, P, D),
        v_tab=i["peer_v"].reshape(L, NE, P, D))


_ORDER = ["xT", "c", "cols", "fcol", "w_ada", "w_in", "w_out", "w_q", "w_glu", "rel_bias", "b_re", "b_im", "c_re",
          "c_im", "subkeys", "u_tab", "v_tab", "ident_c", "iota_c", "decay_c", "rope_c", "perm_c", "mask_c"]


def kernel(**inputs):
    import concourse.bacc as _bacc
    from concourse.bass_utils import run_bass_kernel_spmd as _run

    data = _layout({k: np.asarray(a) for k, a in inputs.items()})
    data.update(_tables())
    nc = _bacc.Bacc("TRN2", target_bir_lowering=False, num_devices=1)
    arrays, args = {}, []
    for name in _ORDER:
        a = np.ascontiguousarray(data[name])
        arrays[f"in_{name}_dram"] = a
        args.append(nc.dram_tensor(f"in_{name}_dram", a.shape, mybir.dt.from_np(a.dtype), kind="ExternalInput").ap())
    out = nc.dram_tensor("out_T_dram", (D, T), F32, kind="ExternalOutput")
    trunk(nc, *args, out.ap())
    r = _run(nc, [arrays], core_ids=[0])
    return np.ascontiguousarray(r.results[0]["out_T_dram"].T)[None]
```

```python
import math
from contextlib import ExitStack

import numpy as np

import concourse.bass as bass
from concourse import mybir

F32 = mybir.dt.float32
F32R = mybir.dt.float32r
U32 = mybir.dt.uint32
ALU = mybir.AluOpType
ACT = mybir.ActivationFunctionType
AX = mybir.AxisListType

P = 128
L = 2
D = 1024
T = 256
KT = D // P
TT = T // P
CHUNK = 64
HD = 64
NH = 6
AW = NH * HD
SW = 256
STATES = 64
GCH = 16
ST = 16 * STATES // P
IN_COLS = 3 * AW + 4 * AW + SW
IN_TILES = IN_COLS // P
PH = 8
NK = 128
TOPK = 16
NE = NK
NB = 2 * AW // P
EPS = 1e-6
NEG = -1e30
TWO_PI_HI = 6.28125
TWO_PI_LO = 2.0 * math.pi - 6.28125
ROUND = 1.5 * 2.0 ** 23
PI = 3.1415925

C_BADA, C_NMIX, C_NFFN, C_GAIN, C_D, C_LRE, C_LIM, C_LDT = 0, 48, 56, 64, 72, 74, 82, 90
C_ALL = 98
SH1, SC1, G1, SH2, SC2, G2 = range(6)


def trunk(nc, xT, c, cols, fcol, w_ada, w_in, w_out, w_q, w_glu, rel_bias, b_re, b_im, c_re, c_im,
          subkeys, u_tab, v_tab, ident_c, iota_c, decay_c, rope_c, perm_c, mask_c, outT):
    ctx = ExitStack()
    with ctx:
        base = 16512

        def at(name, floats, shape, dt=F32):
            return nc.alloc_sbuf_tensor_at(name, shape, dt, offset=base + 4 * floats)

        def sem(name):
            return ctx.enter_context(nc.semaphore(name))

        WT = at("gates_T", 0, [P, NE, T])
        HT = at("h_T", 0, [P, KT, T])
        MERGED = at("merged", 0, [P, TT, D])
        QA = at("q_att_T", 10240, [P, 2, 3, T])
        KA = at("k_att_T", 2816, [P, 3, T])
        VA = at("v_att", 3584, [P, TT, AW])
        QK = at("qk_ret_T", 4352, [P, 6, T])
        VR = at("v_ret", 5888, [P, TT, AW])
        GR = at("g_ret", 6656, [P, TT, AW])
        UT = at("u_ssm_T", 7424, [P, 2, T])
        SQ = at("squares", 7936, [P, KT, T])
        SAB = at("scores_ab", 7936, [P, NH * (P + T)])
        SA = SAB[:, 0:NH * P].rearrange("p (h t) -> p h t", h=NH)
        SB = SAB[:, NH * P:].rearrange("p (h t) -> p h t", h=NH)
        PT = at("probs_T", 10240, [P, 18, P])
        SR0 = at("ret_scores_0", 12544, [P, NH, T])
        SR1 = at("ret_scores_1", 14080, [P, NH, P])
        UM = at("u_masked", 12544, [P, 2, 4, T])
        DEC0 = at("decay_0", 14848, [P, NH, T])
        DEC1 = at("decay_1", 16384, [P, NH, P])
        BIAS = at("rel_bias_rows", 17152, [P, NH, T])
        ROPE = at("rope", 18688, [P, 2, T])
        YSQ = at("y_squares", 19968, [P, 2 * NH, HD])[:, :, :]
        YR = at("y_ret", 19200, [P, TT, AW])
        ROT = at("rotated", 19968, [P, 6, T])
        QM = at("q_ret_masked", 21760, [P, 2, 3, T])
        MT = at("merged_T", 21504, [P, KT, T])
        RSTD = at("rstd", 50688, [P, T])
        ADA = at("w_ada_ring", 24576, [P, 8, D])
        QT = at("query_T", 2048, [P, 2, T])
        SUBT = at("subkeys_T", 4096, [P, 16, NK])
        KS = at("key_scores", 6144, [P, TT, 16, NK])
        CAND = at("candidates", 10240, [P, PH, TOPK, TOPK])
        EQ = at("equal", 12288, [P, PH, TOPK, TOPK])
        V16 = at("top_scores", 14336, [P, TT, 16, TOPK])
        I16 = at("top_keys", 14848, [P, TT, 16, TOPK], U32)
        I16F = at("top_keys_f", 15360, [P, TT, 16, TOPK])
        BEST = at("best", 15872, [P, TT, PH, TOPK])
        POS = at("best_pos", 16128, [P, TT, PH, TOPK], U32)
        POSA = at("pos_a", 16384, [P, TT, PH, TOPK], U32)
        POSB = at("pos_b", 16640, [P, TT, PH, TOPK], U32)
        AF = at("pos_a_f", 16896, [P, TT, PH, TOPK])
        BF = at("pos_b_f", 17152, [P, TT, PH, TOPK])
        SEL = at("picks", 17408, [P, 3, TT, P])
        GSUM = at("gate_sum", 18176, [P, TT, PH])
        ACC = at("mixed", 2048, [P, TT, D])
        X = at("x_T", 32768, [P, KT, T])
        RING = at("weight_ring", 34816, [P, 4, D])
        UH = at("u_hi", 38912, [P, 2, KT, P], F32R)
        UL = at("u_lo", 40960, [P, 2, KT, P], F32R)
        VH = at("v_hi", 43008, [P, 2, D], F32R)
        VL = at("v_lo", 45056, [P, 2, D], F32R)
        HH = at("h_hi", 47104, [P, KT, T], F32R)
        HL = at("h_lo", 49152, [P, KT, T], F32R)
        TRIG = [(at("cos_0", 38912, [P, 4, T]), at("sin_0", 39936, [P, 4, T])),
                (at("cos_1", 19200, [P, 4, T]), at("sin_1", 20224, [P, 4, T]))]
        ZRE = at("z_re", 40960, [P, 4, T])
        ZIM = at("z_im", 41984, [P, 4, T])
        TA = at("tmp_a", 43008, [P, 4, T])
        TB = at("tmp_b", 44032, [P, 4, T])
        CFRE = at("cf_re", 45056, [P, ST, P])
        CFIM = at("cf_im", 46080, [P, ST, P])
        BTRE = at("b_re_T", 47104, [P, 2, P])
        BTIM = at("b_im_T", 47360, [P, 2, P])
        WGLU = at("w_glu_sb", 47616, [P, 2, 2 * SW])
        YG = at("y_gelu_T", 48640, [P, 2, T])
        BRAW = at("b_raw", 49152, [P, 2, 2, STATES])
        CRAW = at("c_raw", 49408, [P, 2, ST, GCH])
        CTMP = at("c_tmp", 49664, [P, 4, ST, GCH])
        ZG = at("z_gate", 50176, [P, TT, SW])
        CB = at("cond", 23552, [P, D])
        SCR = at("scratch_row", 43008, [P, D])
        TURNS = at("turns", 7936, [P, 4, T])
        OHA = at("onehot_gate", 38912, [P, 4, 4, P])
        OHB = at("onehot_key", 40960, [P, 4, 4, P])
        GE = at("gelu", 51200, [P, 2, T])
        G32 = at("gated", 51712, [P, T])
        GH = at("gated_hi", 51968, [P, T], F32R)
        GL = at("gated_lo", 52224, [P, T], F32R)
        ONES = at("ones", 51200, [P, P])
        IOTA = at("iota", 51328, [P, T])
        IDENT = at("ident", 51584, [P, P])
        SELT = at("picks_T", 51712, [P, 3, T])
        COLS = at("cols", 52480, [P, L, C_ALL])
        FCOL = at("final_gain", 52680, [P, KT])
        MOD = at("mod", 52688, [P, 6, KT])
        AMP = at("amp", 52736, [P, KT])
        MASK = at("masks", 52944, [P, 10])
        SM = at("softmax_stat", 52752, [P, 4, 12])
        SV = at("ssm_vec", 52800, [P, 15, ST])
        ADA8 = at("ada_dots", 52928, [P, KT])
        KEY4 = at("key_columns", 52960, [P, 4, 8])
        ZERO4 = at("zeros", 52992, [P, 4])
        KB = 2
        RMS = at("rms_stat", 52936, [P, 4])

        PS = ctx.enter_context(nc.psum_tensor("ps", [P, 8, 512], F32))
        ps = PS[:, :, :].rearrange("p b n -> p (b n)")

        in_x = sem("x_loaded")
        in_cols = sem("cols_loaded")
        in_c = sem("c_loaded")
        in_const = sem("const_loaded")
        in_mix = sem("mix_tables_loaded")
        in_sub = sem("subkeys_loaded")
        in_perm = sem("perm_loaded")
        in_ada = [sem(f"ada_loaded_{i}") for i in range(8)]
        in_ring = [sem(f"ring_loaded_{i}") for i in range(4)]
        out_done = sem("out_done")
        dve_step = sem("dve_step")
        act_step = sem("act_step")
        ada_used = sem("ada_used")
        cond_done = sem("cond_done")
        mod_done = sem("mod_done")
        x_ready = sem("x_ready")
        squared = sem("squared")
        ones_ready = sem("ones_ready")
        sumsq = sem("sumsq_done")
        var_done = sem("var_done")
        std_done = sem("std_done")
        normed = sem("normed")
        h_done = sem("h_done")
        h_hi = sem("h_hi_done")
        rvar = sem("ret_var_done")
        rstd_done = sem("ret_std_done")
        mvar = sem("merge_var_done")
        mstd = sem("merge_std_done")
        h_split = sem("h_split_done")
        proj_mm = sem("proj_product")
        proj_ev = sem("proj_evacuated")
        rot_mm = sem("rot_product")
        rot_done = sem("rotated_done")
        att_mm = sem("att_scores")
        att_in = sem("att_scores_taken")
        att_sub = sem("att_shifted")
        att_exp = sem("att_exp_done")
        ret_mm = sem("ret_scores")
        ret_in = sem("ret_scores_decayed")
        pt_mm = sem("probs_transposed")
        pt_ev = sem("probs_T_taken")
        ry_mm = sem("ret_product")
        ry_ev = sem("ret_product_taken")
        ao_mm = sem("att_product")
        ao_ev = sem("att_product_taken")
        gate_silu = sem("gate_silu_done")
        ssm_e = sem("ssm_exp_in")
        ssm_x = sem("ssm_exp_out")
        ssm_a = sem("ssm_angle_in")
        ssm_s = sem("ssm_sine_out")
        bt_done = sem("b_masked")
        bu_mm = sem("bu_product")
        bu_ev = sem("bu_taken")
        xs_done = sem("states_done")
        cf_done = sem("cf_done")
        sy_mm = sem("ssm_y_product")
        sy_in = sem("ssm_y_sum")
        sy_gelu = sem("ssm_gelu_done")
        glu_mm = sem("glu_product")
        glu_gate = sem("glu_gate_done")
        merged = sem("merged_done")
        mt_mm = sem("merged_transposed")
        mt_ev = sem("merged_T_taken")
        wo_mm = sem("w_out_product")
        q_mm = sem("query_product")
        q_ev = sem("query_taken")
        ks_mm = sem("key_scores_product")
        ks_ev = sem("key_scores_taken")
        gate_in = sem("gate_shifted")
        gate_exp = sem("gate_exp")
        picks = sem("picks_done")
        pickt_mm = sem("picks_transposed")
        pickt = sem("picks_T_taken")
        onehot = sem("gate_onehots_done")
        in_ssm = sem("in_ssm_tables")
        um_done = sem("u_masked")
        f_done = sem("ssm_factors_done")
        act_step = sem("scalar_step")
        pool_step = sem("gpsimd_step")
        glu_read = sem("glu_taken")
        rot_read = sem("rotation_product_taken")
        key_copied = sem("key_columns_copied")
        zeros_ready = sem("zeros_ready")
        key_onehot = sem("key_onehots_done")
        w_mm = sem("gates_product")
        w_ev = sem("gates_taken")
        u_hi = sem("u_hi_done")
        u_split = sem("u_split_done")
        v_hi = sem("v_hi_done")
        v_split = sem("v_split_done")
        s_mm = sem("expert_scores")
        gelu_done = sem("expert_gelu")
        g_prod = sem("gated_product")
        g_hi = sem("gated_hi_done")
        g_ready = sem("gated_split")
        v_used = sem("experts_summed")
        acc_ev = sem("mixed_taken")
        acc_mm = sem("mixed_transposed")
        fin = sem("final_done")

        NSTREAM = IN_TILES + KT + 16
        assert NSTREAM % 4 == 3

        def ring_pos(l, n):
            full, slot = (NSTREAM + 1) // 4 + NE // 2, n % 4
            return slot, 16 * (l * full - (l if slot == 3 else 0) + n // 4 + 1)

        def expert_pos(l, v, b):
            full, slot = (NSTREAM + 1) // 4 + NE // 2, 2 * v + b
            n = (NSTREAM + 1) // 4 - (1 if slot == 3 else 0)
            return slot, l * full - (l if slot == 3 else 0) + n + 1

        TILE_IN, TILE_OUT, TILE_Q = 0, IN_TILES, IN_TILES + KT
        IN_ORDER = [21, 22, 9, 10, 11, 12, 13, 14, 0, 1, 2, 3, 4, 5, 6, 7, 8, 15, 16, 17, 18, 19, 20]

        N_PROJ = 20
        PROJ_OF = list(range(14)) + [15] * 3 + [17] * 3 + [19] * 3

        block = ctx.enter_context(nc.Block())

        @block.sync
        def _(sp):
            sp.dma_start(COLS[:, :, :], cols).then_inc(in_cols, 16)
            sp.dma_start(FCOL[:, :], fcol).then_inc(in_cols, 16)
            sp.dma_start(MASK[:, :], mask_c).then_inc(in_cols, 16)
            sp.dma_start(X[:, :, :], xT.rearrange("(k p) t -> p k t", p=P)).then_inc(in_x, 16)
            for l in range(L):
                if l == 0:
                    sp.dma_start(IDENT[:, :], ident_c).then_inc(in_const, 16)
                    sp.dma_start(IOTA[:, :], iota_c).then_inc(in_const, 16)
                sp.dma_start(CB[:, :], bass.AP(c.tensor, 0, [[0, P], [1, D]])).then_inc(in_c, 16)

                def ada(m):
                    n = l * 48 + m
                    if m >= 8:
                        sp.wait_ge(ada_used, n - 7)
                    sp.dma_start(ADA[:, m % 8, :], w_ada[l, m * P:(m + 1) * P, :]).then_inc(in_ada[m % 8], 16)

                def stream(n):
                    slot, value = ring_pos(l, n)
                    if n >= 4:
                        m = n - 4
                        if m < TILE_OUT:
                            sp.wait_ge(proj_mm, l * N_PROJ + PROJ_OF[m] + 1)
                        elif m < TILE_Q:
                            sp.wait_ge(wo_mm, l * KT + m - TILE_OUT + 1)
                        else:
                            sp.wait_ge(q_mm, l * 16 + m - TILE_Q + 1)
                    if n < TILE_OUT:
                        src = w_in[l, IN_ORDER[n]]
                    elif n < TILE_Q:
                        src = w_out[l, n - TILE_OUT]
                    else:
                        src = w_q[l, n - TILE_Q]
                    sp.dma_start(RING[:, slot, :], src).then_inc(in_ring[slot], 16)

                for m in range(16):
                    ada(m)
                for n in range(4):
                    stream(n)
                sp.dma_start(BRAW[:, 0, :, :], b_re[l]).then_inc(in_ssm, 16)
                sp.dma_start(BRAW[:, 1, :, :], b_im[l]).then_inc(in_ssm, 16)
                sp.dma_start(CRAW[:, 0, :, :], c_re[l]).then_inc(in_ssm, 16)
                sp.dma_start(CRAW[:, 1, :, :], c_im[l]).then_inc(in_ssm, 16)
                sp.dma_start(WGLU[:, :, :], w_glu[l].rearrange("(k p) n -> p k n", p=P)).then_inc(in_ssm, 16)
                sp.dma_start(ROPE[:, :, :], rope_c).then_inc(in_mix, 16)
                sp.dma_start(DEC0[:, :, :], decay_c[:, 0:NH * T].rearrange("p (h t) -> p h t", h=NH)).then_inc(in_mix, 16)
                sp.dma_start(DEC1[:, :, :], decay_c[:, NH * T:].rearrange("p (h t) -> p h t", h=NH)).then_inc(in_mix, 16)
                sp.dma_start(BIAS[:, :, :], bass.AP(rel_bias.tensor, l * NH * 513 + 129,
                                                    [[1, P], [513, NH], [1, T]])).then_inc(in_mix, 16)
                sp.dma_start(MT[:, 0, 0:P], perm_c).then_inc(in_perm, 16)
                m = 16
                for n in range(4, NSTREAM):
                    if n == TILE_Q:
                        sp.wait_ge(merged, l + 1)
                        sp.dma_start(SUBT[:, :, :], subkeys[l].rearrange("p (n k) -> p n k", k=NK)).then_inc(in_sub, 16)
                    stream(n)
                    while m < min(24, 16 + 2 * (n - 3)) or (n >= 15 and m < min(32, 24 + 2 * (n - 14))) \
                            or (n >= TILE_OUT + 3 and m < min(48, 40 + 2 * (n - TILE_OUT - 3))):
                        ada(m)
                        m += 1
                for v in (0, 1):
                    for e in (0, 1):
                        slot, _ = expert_pos(l, v, e)
                        last = NSTREAM - 1 - (NSTREAM - 1 - slot) % 4
                        sp.wait_ge(q_mm, l * 16 + last - TILE_Q + 1)
                        sp.dma_start(RING[:, slot, :], (v_tab if v else u_tab)[l, e]).then_inc(in_ring[slot], 16)
                with sp.Fori(0, NE // 2 - 1) as i:
                    for b in (0, 1):
                        sp.wait_ge(u_split, i * 2 + (l * NE + b + 1))
                        sp.dma_start(RING[:, b, :], u_tab[l, i * 2 + (b + 2)]).then_inc(in_ring[b], 16)
                        sp.wait_ge(v_split, i * 2 + (l * NE + b + 1))
                        sp.dma_start(RING[:, 2 + b, :], v_tab[l, i * 2 + (b + 2)]).then_inc(in_ring[2 + b], 16)
                sp.wait_ge(v_used, (l + 1) * NE)
                sp.dma_start(IDENT[:, :], ident_c).then_inc(in_const, 16)
                sp.dma_start(IOTA[:, :], iota_c).then_inc(in_const, 16)
            sp.wait_ge(fin, 1)
            sp.dma_start(outT.rearrange("(k p) t -> p k t", p=P), HT[:, :, :]).then_inc(out_done, 16)
            sp.wait_ge(out_done, 16)

        @block.tensor
        def _(pe):
            mm = nc.tensor.matmul

            def sum_squares(n):
                pe.wait_ge(ones_ready, n // 2 + 1)
                pe.wait_ge(squared, n + 1)
                for k in range(KT):
                    last = mm(ps[:, 0:T], ONES[:, :], SQ[:, k, :], start=(k == 0), stop=(k == KT - 1))
                last.then_inc(sumsq, 1)

            for l in range(L):
                pe.wait_ge(in_const, 32 * (l + 1))
                sum_squares(2 * l)

                pe.wait_ge(h_done, 2 * l + 1)
                loaded = set()

                def tile(n):
                    slot, value = ring_pos(l, n)
                    if n not in loaded:
                        pe.wait_ge(in_ring[slot], value)
                        loaded.add(n)
                    return RING[:, slot, :].rearrange("p (k n) -> p k n", n=P)

                def project(j):
                    bank = 5 + j % 3
                    if j >= 3:
                        pe.wait_ge(proj_ev, l * N_PROJ + j - 2)
                    if j < 14:
                        w = tile(j)
                        for k in range(KT):
                            last = mm(PS[:, bank, 0:T], w[:, k, :], HT[:, k, :], start=(k == 0), stop=(k == KT - 1))
                    else:
                        t = j % 2
                        for a in range(3):
                            w = tile(14 + 3 * ((j - 14) // 2) + a)
                            for k in range(KT):
                                last = mm(PS[:, bank, a * P:(a + 1) * P], HT[:, k, t * P:(t + 1) * P], w[:, k, :],
                                          start=(k == 0), stop=(k == KT - 1))
                    last.then_inc(proj_mm, 1)

                def ssm_input(u):
                    if u:
                        pe.wait_ge(bu_ev, 2 * l + 1)
                    else:
                        pe.wait_ge(bt_done, l + 1)
                        pe.wait_ge(um_done, l + 1)
                    for im, bt in enumerate((BTRE, BTIM)):
                        for r in range(4):
                            o = im * 1024 + r * T
                            last = mm(ps[:, o:o + T], bt[:, u, :], UM[:, u, r, :], start=True, stop=True)
                    last.then_inc(bu_mm, 1)

                def ssm_output(u):
                    if u == 0:
                        pe.wait_ge(cf_done, l + 1)
                    pe.wait_ge(xs_done, 2 * l + u + 1)
                    for r in range(4):
                        mm(PS[:, 4, u * T:(u + 1) * T], CFRE[:, 4 * u + r, :], ZRE[:, r, :], start=(r == 0), stop=False)
                        last = mm(PS[:, 4, u * T:(u + 1) * T], CFIM[:, 4 * u + r, :], ZIM[:, r, :],
                                  start=False, stop=(r == 3))
                    last.then_inc(sy_mm, 1)

                for j in range(0, 3):
                    project(j)
                ssm_input(0)
                for j in range(3, 5):
                    project(j)
                ssm_input(1)
                for j in range(5, 7):
                    project(j)
                ssm_output(0)
                for j in range(7, 11):
                    project(j)
                ssm_output(1)
                project(11)
                pe.wait_ge(sy_gelu, l + 1)
                for t in range(TT):
                    for k in range(2):
                        last = mm(PS[:, t, :], YG[:, k, t * P:(t + 1) * P], WGLU[:, k, :], start=(k == 0), stop=(k == 1))
                last.then_inc(glu_mm, 1)
                for j in range(12, 14):
                    project(j)
                pe.wait_ge(in_perm, 16 * (l + 1))
                pe.wait_ge(proj_ev, l * N_PROJ + 8)
                pe.wait_ge(glu_read, l + 1)
                for a in range(6):
                    last = mm(ps[:, a * T:(a + 1) * T], MT[:, 0, 0:P], QK[:, a, :], start=True, stop=True)
                last.then_inc(rot_mm, 1)
                project(14)
                pe.wait_ge(proj_ev, l * N_PROJ + 14)
                pe.wait_ge(rot_read, l + 1)
                for h in range(NH):
                    mm(ps[:, h * P:(h + 1) * P], QA[:, h % 2, h // 2, 0:P], KA[:, h // 2, 0:P], start=True, stop=True)
                for h in range(NH):
                    last = mm(ps[:, 768 + h * T:768 + (h + 1) * T], QA[:, h % 2, h // 2, P:T], KA[:, h // 2, :],
                              start=True, stop=True)
                last.then_inc(att_mm, 1)
                for j in range(15, N_PROJ):
                    project(j)
                pe.wait_ge(rot_done, l + 1)
                pe.wait_ge(att_in, l + 1)
                for h in range(NH):
                    mm(ps[:, h * T:(h + 1) * T], QK[:, 3 + h // 2, 0:P], QM[:, h % 2, h // 2, :], start=True, stop=True)
                for h in range(NH):
                    o = 1536 + h * P
                    last = mm(ps[:, o:o + P], QK[:, 3 + h // 2, P:T], QM[:, h % 2, h // 2, P:T], start=True, stop=True)
                last.then_inc(ret_mm, 1)

                pe.wait_ge(ret_in, l + 1)
                pe.wait_ge(proj_ev, (l + 1) * N_PROJ)
                for h in range(NH):
                    mm(PS[:, 6, h * HD:(h + 1) * HD], SR0[:, h, 0:P], VR[:, 0, h * HD:(h + 1) * HD], start=True, stop=True)
                for h in range(NH):
                    o = PS[:, 7, h * HD:(h + 1) * HD]
                    mm(o, SR0[:, h, P:T], VR[:, 0, h * HD:(h + 1) * HD], start=True, stop=False)
                    last = mm(o, SR1[:, h, :], VR[:, 1, h * HD:(h + 1) * HD], start=False, stop=True)
                last.then_inc(ry_mm, 1)

                pe.wait_ge(att_exp, l + 1)
                for h in range(NH):
                    nc.tensor.transpose(ps[:, h * P:(h + 1) * P], SA[:, h, :], IDENT[:, :])
                for h in range(NH):
                    for b in range(2):
                        o = (6 + 2 * h + b) * P
                        last = nc.tensor.transpose(ps[:, o:o + P], SB[:, h, b * P:(b + 1) * P], IDENT[:, :])
                last.then_inc(pt_mm, 1)
                pe.wait_ge(pt_ev, l + 1)
                for h in range(NH):
                    mm(PS[:, 5, h * HD:(h + 1) * HD], PT[:, h, :], VA[:, 0, h * HD:(h + 1) * HD], start=True, stop=True)
                pe.wait_ge(ry_ev, l + 1)
                for h in range(NH):
                    o = PS[:, 6, h * HD:(h + 1) * HD]
                    mm(o, PT[:, 6 + 2 * h, :], VA[:, 0, h * HD:(h + 1) * HD], start=True, stop=False)
                    last = mm(o, PT[:, 7 + 2 * h, :], VA[:, 1, h * HD:(h + 1) * HD], start=False, stop=True)
                last.then_inc(ao_mm, 1)

                pe.wait_ge(merged, l + 1)
                for k in range(KT):
                    for t in range(TT):
                        o = 2048 + k * T + t * P
                        last = nc.tensor.transpose(ps[:, o:o + P], MERGED[:, t, k * P:(k + 1) * P], IDENT[:, :])
                last.then_inc(mt_mm, 1)
                pe.wait_ge(mt_ev, l + 1)
                for d in range(KT):
                    w = tile(TILE_OUT + d)
                    for k in range(KT):
                        last = mm(ps[:, d * T:(d + 1) * T], w[:, k, :], MT[:, k, :], start=(k == 0), stop=(k == KT - 1))
                    last.then_inc(wo_mm, 1)

                sum_squares(2 * l + 1)
                pe.wait_ge(h_done, 2 * l + 2)
                pe.wait_ge(in_sub, 16 * (l + 1))
                def key_scores(n):
                    g = l * 16 + n
                    pe.wait_ge(q_ev, g + 1)
                    if n >= 2:
                        pe.wait_ge(ks_ev, g - 1)
                    for t in range(TT):
                        last = mm(PS[:, 6 + n % 2, t * P:(t + 1) * P], QT[:, n % 2, t * P:(t + 1) * P],
                                  SUBT[:, n, :], start=True, stop=True)
                    last.then_inc(ks_mm, 1)
                for n in range(16):
                    w = tile(TILE_Q + n)
                    if n >= 2:
                        pe.wait_ge(q_ev, l * 16 + n - 1)
                    for k in range(KT):
                        last = mm(PS[:, 4 + n % 2, 0:T], w[:, k, :], HT[:, k, :], start=(k == 0), stop=(k == KT - 1))
                    last.then_inc(q_mm, 1)
                    if n:
                        key_scores(n - 1)
                key_scores(15)

                pe.wait_ge(picks, l + 1)
                for a in range(3):
                    for t in range(TT):
                        o = a * T + t * P
                        last = nc.tensor.transpose(ps[:, o:o + P], SEL[:, a, t, :], IDENT[:, :])
                last.then_inc(pickt_mm, 1)
                def gates(g, b, i):
                    pe.wait_ge(onehot, g + 1)
                    if b < KB:
                        pe.wait_ge(key_onehot, i * KB + (l * 16 * KB + b + 1))
                    for q in range(4):
                        last = mm(PS[:, 4 + b, q * P:(q + 1) * P], OHB[:, b, q, :], OHA[:, b, q, :], start=True, stop=True)
                    last.then_inc(w_mm, 1)
                for b in range(4):
                    gates(l * 64 + b, b, 0)
                with pe.Fori(1, 16) as i:
                    for b in range(4):
                        pe.wait_ge(w_ev, i * 4 + (l * 64 + b - 3))
                        gates(i * 4 + (l * 64 + b), b, i)

                def scores(e, b, first):
                    pe.wait_ge(u_split, e + 1)
                    if not first:
                        pe.wait_ge(gelu_done, e - 1)
                    for k in range(KT):
                        mm(PS[:, 4 + b, 0:T], UH[:, b, k, :], HH[:, k, :], start=(k == 0), stop=False)
                        mm(PS[:, 4 + b, 0:T], UH[:, b, k, :], HL[:, k, :], start=False, stop=False)
                        last = mm(PS[:, 4 + b, 0:T], UL[:, b, k, :], HH[:, k, :], start=False, stop=(k == KT - 1))
                    last.then_inc(s_mm, 1)

                def add_experts(e, b, start=False, stop=False):
                    pe.wait_ge(v_split, e + 1)
                    pe.wait_ge(g_ready, e + 1)
                    for t in range(TT):
                        for n, (g, v) in enumerate(((GH, VH), (GH, VL), (GL, VH))):
                            for d in range(2):
                                last = mm(PS[:, 2 * t + d, :], g[:, t * P:(t + 1) * P], v[:, b, d * 512:(d + 1) * 512],
                                          start=start and n == 0, stop=stop and n == 2)
                    last.then_inc(v_used, 1)

                E0 = l * NE
                pe.wait_ge(w_ev, (l + 1) * 64)
                scores(E0, 0, True)
                scores(E0 + 1, 1, l == 0)
                add_experts(E0, 0, start=True)
                scores(E0 + 2, 0, False)
                add_experts(E0 + 1, 1)
                with pe.Fori(1, NE // 2 - 1) as i:
                    for b in (0, 1):
                        scores(i * 2 + (E0 + b + 1), 1 - b, False)
                        add_experts(i * 2 + (E0 + b), b)
                scores(E0 + NE - 1, 1, False)
                add_experts(E0 + NE - 2, 0)
                add_experts(E0 + NE - 1, 1, stop=True)
                pe.wait_ge(acc_ev, l + 1)
                pe.wait_ge(in_const, 32 * (l + 2))
                for k in range(KT):
                    for t in range(TT):
                        o = 2048 + k * T + t * P
                        last = nc.tensor.transpose(ps[:, o:o + P], ACC[:, t, k * P:(k + 1) * P], IDENT[:, :])
                last.then_inc(acc_mm, 1)
            sum_squares(2 * L)

        @block.gpsimd
        def _(pool):
            nc.gpsimd.memset(ZERO4[:, :], 0.0).then_inc(zeros_ready, 1)
            pool.wait_ge(zeros_ready, 1)
            gp = nc.gpsimd
            steps = [0]

            def step(ins):
                steps[0] += 1
                ins.then_inc(pool_step, 1)
                pool.wait_ge(pool_step, steps[0])

            for l in range(L):
                pool.wait_ge(in_ssm, 80 * (l + 1))
                for n, bt in enumerate((BTRE, BTIM)):
                    for half in range(2):
                        last = gp.tensor_scalar(bt[:, :, half * STATES:(half + 1) * STATES], BRAW[:, n, :, :],
                                               MASK[:, half:half + 1], None, ALU.mult)
                last.then_inc(bt_done, 1)
                pool.wait_ge(f_done, l + 1)
                bc = lambda n: SV[:, n, :].unsqueeze(2).to_broadcast([P, ST, GCH])
                gp.memset(CFRE[:, :, :], 0.0)
                gp.memset(CFIM[:, :, :], 0.0)
                gp.tensor_tensor(CTMP[:, 0, :, :], CRAW[:, 0, :, :], bc(13), ALU.mult)
                gp.tensor_tensor(CTMP[:, 1, :, :], CRAW[:, 1, :, :], bc(14), ALU.mult)
                gp.tensor_tensor(CTMP[:, 2, :, :], CRAW[:, 0, :, :], bc(14), ALU.mult)
                step(gp.tensor_tensor(CTMP[:, 3, :, :], CRAW[:, 1, :, :], bc(13), ALU.mult))
                gp.tensor_tensor(CTMP[:, 0, :, :], CTMP[:, 0, :, :], CTMP[:, 1, :, :], ALU.subtract)
                step(gp.tensor_tensor(CTMP[:, 2, :, :], CTMP[:, 2, :, :], CTMP[:, 3, :, :], ALU.add))
                for n, (cf, sign) in enumerate(((CFRE, 1.0), (CFIM, -1.0))):
                    for g in range(2):
                        rows = slice(g * STATES, (g + 1) * STATES)
                        out = bass.AP(cf, g * STATES * ST * P + GCH * g, [[ST * P, STATES], [4 * P, 2], [P + 32, 4], [1, GCH]])
                        last = gp.tensor_scalar(out, CTMP[rows, 2 * n, :, :].rearrange("p (u r) c -> p u r c", r=4),
                                               sign, None, ALU.mult)
                last.then_inc(cf_done, 1)


                def copy_keys(b, tok):
                    nc.gpsimd.tensor_tensor(KEY4[:, b, 0:4], SELT[:, 1, bass.ds(tok, 4)], ZERO4[:, :], ALU.add).then_inc(key_copied, 1)

                def key_onehots(b):
                    for q in range(4):
                        last = nc.gpsimd.tensor_scalar(OHB[:, b, q, :], IOTA[:, 0:P], KEY4[:, b, q:q + 1], None, ALU.is_equal)
                    last.then_inc(key_onehot, 1)

                pool.wait_ge(pickt, l + 1)
                copy_keys(0, 0)
                for b in range(KB):
                    pool.wait_ge(key_copied, l * 16 * KB + b + 1)
                    if b == KB - 1:
                        pool.wait_ge(key_onehot, l * 16 * KB + 1)
                        copy_keys(0, 16)
                    else:
                        copy_keys(b + 1, 4 * b + 4)
                    key_onehots(b)
                with pool.Fori(1, 15) as i:
                    for b in range(KB):
                        pool.wait_ge(key_copied, i * KB + (l * 16 * KB + b + 1))
                        pool.wait_ge(w_mm, i * 4 + (l * 64 + b - 3))
                        if b == KB - 1:
                            pool.wait_ge(key_onehot, i * KB + (l * 16 * KB + 1))
                            copy_keys(0, i * 16 + 16)
                        else:
                            pool.wait_ge(key_onehot, i * KB + (l * 16 * KB + b + 2 - KB))
                            copy_keys(b + 1, i * 16 + (4 * b + 4))
                        key_onehots(b)
                for b in range(KB):
                    pool.wait_ge(key_copied, (l + 1) * 16 * KB - KB + b + 1)
                    pool.wait_ge(w_mm, l * 64 + 57 + b)
                    if b < KB - 1:
                        pool.wait_ge(key_onehot, (l + 1) * 16 * KB - KB + b + 2 - KB)
                        copy_keys(b + 1, 240 + 4 * b + 4)
                    key_onehots(b)

        @block.scalar
        def _(act):
            fn = nc.scalar.activation

            def square(n):
                act.wait_ge(in_x, 16) if n == 0 else act.wait_ge(x_ready, n)
                fn(SQ[:, :, :], X[:, :, :], ACT.Square).then_inc(squared, 1)
                act.wait_ge(var_done, n + 1)
                fn(RSTD[:, :], RSTD[:, :], ACT.Sqrt).then_inc(std_done, 1)

            act.wait_ge(in_cols, 48)
            for l in range(L):
                act.wait_ge(in_c, 16 * (l + 1))
                fn(CB[:, :], CB[:, :], ACT.Silu).then_inc(cond_done, 1)
                fn(SV[:, 0, :], COLS[:, l, C_LDT:C_LDT + ST], ACT.Exp).then_inc(ssm_x, 1)
                act.wait_ge(ssm_e, l + 1)
                fn(SV[:, 2, :], SV[:, 1, :], ACT.Exp).then_inc(ssm_x, 1)
                act.wait_ge(ssm_a, 3 * l + 1)
                fn(SV[:, 6, :], SV[:, 5, :], ACT.Sin)
                fn(SV[:, 7, :], SV[:, 5, :], ACT.Sin, scale=0.5).then_inc(ssm_s, 1)
                square(2 * l)
                act.wait_ge(normed, 2 * l + 1)
                for k in range(KT):
                    last = fn(HT[:, k, :], HT[:, k, :], ACT.Identity, scale=AMP[:, k:k + 1], bias=MOD[:, SH1, k:k + 1])
                last.then_inc(h_done, 1)

                place = ([(UT[:, a, :], 1.0) for a in range(2)] + [(QK[:, a, :], 1.0) for a in range(6)]
                         + [(QA[:, :, a, :], None) for a in range(3)] + [(KA[:, a, :], 1.0) for a in range(3)]
                         + [(o[:, t, :], 1.0) for o in (VA, VR, GR) for t in range(TT)])

                def taken(j):
                    o, scale = place[j]
                    act.wait_ge(proj_mm, l * N_PROJ + j + 1)
                    if scale is None:
                        for parity in range(2):
                            last = fn(o[:, parity, :], PS[:, 5 + j % 3, 0:T], ACT.Copy, scale=MASK[:, 6 + parity:7 + parity])
                        last.then_inc(proj_ev, 1)
                    else:
                        fn(o, PS[:, 5 + j % 3, 0:o.shape[-1]], ACT.Copy).then_inc(proj_ev, 1)

                def trig(u):
                    cos, sin = TRIG[u]
                    act.wait_ge(ssm_a, 3 * l + 2 + u)
                    fn(cos[:, :, :], sin[:, :, :], ACT.Sin, scale=0.5).then_inc(act_step, 1)
                    act.wait_ge(act_step, 4 * l + 2 * u + 1)
                    fn(sin[:, :, :], sin[:, :, :], ACT.Sin)
                    fn(cos[:, :, :], cos[:, :, :], ACT.Square).then_inc(act_step, 1)
                    act.wait_ge(act_step, 4 * l + 2 * u + 2)
                    fn(cos[:, :, :], cos[:, :, :], ACT.Copy, scale=-2.0, bias=1.0).then_inc(ssm_s, 1)

                trig(0)
                for j in range(2):
                    taken(j)
                act.wait_ge(proj_ev, l * N_PROJ + 2)
                for u in range(2):
                    for r in range(4):
                        last = fn(UM[:, u, r, :], UT[:, u, :], ACT.Copy, scale=MASK[:, 2 + r:3 + r])
                last.then_inc(um_done, 1)
                trig(1)
                for j in range(2, 11):
                    taken(j)
                act.wait_ge(sy_in, l + 1)
                fn(YG[:, :, :], YG[:, :, :], ACT.Gelu_apprx_tanh).then_inc(sy_gelu, 1)
                taken(11)
                act.wait_ge(glu_mm, l + 1)
                fn(ZG[:, :, :], PS[:, 0:2, SW:2 * SW], ACT.Sigmoid).then_inc(glu_gate, 1)
                for j in range(12, 17):
                    taken(j)
                act.wait_ge(att_sub, l + 1)
                fn(SAB[:, :], SAB[:, :], ACT.Exp).then_inc(att_exp, 1)
                for j in range(17, N_PROJ):
                    taken(j)
                act.wait_ge(proj_ev, (l + 1) * N_PROJ)
                fn(GR[:, :, :], GR[:, :, :], ACT.Silu).then_inc(gate_silu, 1)

                act.wait_ge(pt_mm, l + 1)
                fn(PT[:, :, :], ps[:, 0:18 * P].rearrange("p (n k) -> p n k", k=P), ACT.Copy).then_inc(pt_ev, 1)
                act.wait_ge(rvar, l + 1)
                fn(SM[:, 3, :], SM[:, 3, :], ACT.Sqrt).then_inc(rstd_done, 1)
                act.wait_ge(mvar, l + 1)
                fn(RMS[:, :], RMS[:, :], ACT.Sqrt).then_inc(mstd, 1)
                act.wait_ge(mt_mm, l + 1)
                for k in range(KT):
                    last = fn(MT[:, k, :], ps[:, 2048 + k * T:2048 + (k + 1) * T], ACT.Copy,
                              scale=COLS[:, l, C_GAIN + k:C_GAIN + k + 1])
                last.then_inc(mt_ev, 1)

                square(2 * l + 1)
                act.wait_ge(normed, 2 * l + 2)
                for k in range(KT):
                    last = fn(HT[:, k, :], HT[:, k, :], ACT.Identity, scale=AMP[:, k:k + 1], bias=MOD[:, SH2, k:k + 1])
                last.then_inc(h_done, 1)
                act.wait_ge(h_done, 2 * l + 2)
                fn(HH[:, :, :], HT[:, :, :], ACT.Copy).then_inc(h_hi, 1)
                for n in range(16):
                    act.wait_ge(q_mm, l * 16 + n + 1)
                    if n >= 2:
                        act.wait_ge(ks_mm, l * 16 + n - 1)
                    fn(QT[:, n % 2, :], PS[:, 4 + n % 2, 0:T], ACT.Copy).then_inc(q_ev, 1)
                act.wait_ge(gate_in, l + 1)
                fn(SEL[:, 2, :, :], SEL[:, 2, :, :], ACT.Exp).then_inc(gate_exp, 1)
                act.wait_ge(pickt_mm, l + 1)
                fn(SELT[:, :, :], ps[:, 0:3 * T].rearrange("p (a t) -> p a t", a=3), ACT.Copy).then_inc(pickt, 1)

                def gates(g, b, tok):
                    act.wait_ge(w_mm, g + 1)
                    fn(WT[:, :, bass.ds(tok, 4)], PS[:, 4 + b, :].rearrange("p (t i) -> p i t", t=4),
                       ACT.Copy).then_inc(w_ev, 1)
                for b in range(4):
                    gates(l * 64 + b, b, b * 4)
                with act.Fori(1, 16) as i:
                    for b in range(4):
                        gates(i * 4 + (l * 64 + b), b, i * 16 + b * 4)

                E0 = l * NE

                def u_high(e, b, i):
                    slot, n = expert_pos(l, 0, b)
                    act.wait_ge(in_ring[slot], i * 16 + n * 16)
                    return fn(UH[:, b, :, :], RING[:, slot, :].rearrange("p (k n) -> p k n", n=P), ACT.Copy).then_inc(u_hi, 1)

                def v_high(e, b, i):
                    slot, n = expert_pos(l, 1, b)
                    act.wait_ge(in_ring[slot], i * 16 + n * 16)
                    return fn(VH[:, b, :], RING[:, slot, :], ACT.Copy).then_inc(v_hi, 1)

                def gelu(e, b):
                    act.wait_ge(s_mm, e + 1)
                    return fn(GE[:, b, :], PS[:, 4 + b, 0:T], ACT.Gelu_apprx_tanh).then_inc(gelu_done, 1)

                u_high(E0, 0, 0)
                for e in (0, 1):
                    if e == 1:
                        act.wait_ge(s_mm, E0 + 1)
                    u_high(E0 + e + 1, (e + 1) % 2, (e + 1) // 2)
                    v_high(E0 + e, e, 0)
                    gelu(E0 + e, e)
                with act.Fori(1, NE // 2 - 1) as i:
                    for b in (0, 1):
                        act.wait_ge(s_mm, i * 2 + (E0 + b))
                        u_high(i * 2 + (E0 + b + 1), 1 - b, i + b)
                        act.wait_ge(v_used, i * 2 + (E0 + b - 1))
                        v_high(i * 2 + (E0 + b), b, i)
                        act.wait_ge(g_ready, i * 2 + (E0 + b - 1))
                        gelu(i * 2 + (E0 + b), b)
                for e in (NE - 2, NE - 1):
                    if e < NE - 1:
                        act.wait_ge(s_mm, E0 + e)
                        u_high(E0 + e + 1, 1, NE // 2 - 1)
                    act.wait_ge(v_used, E0 + e - 1)
                    v_high(E0 + e, e % 2, NE // 2 - 1)
                    act.wait_ge(g_ready, E0 + e - 1)
                    gelu(E0 + e, e % 2)
                act.wait_ge(v_used, E0 + NE)
                fn(ACC[:, :, :], PS[:, 0:4, :], ACT.Copy).then_inc(acc_ev, 1)
            square(2 * L)
            act.wait_ge(normed, 2 * L + 1)
            for k in range(KT):
                last = fn(HT[:, k, :], HT[:, k, :], ACT.Copy, scale=FCOL[:, k:k + 1])
            last.then_inc(fin, 1)

        @block.vector
        def _(dve):
            v = nc.vector
            steps = [0]

            def link(ins):
                steps[0] += 1
                ins.then_inc(dve_step, 1)
                dve.wait_ge(dve_step, steps[0])

            def norm(n):
                dve.wait_ge(sumsq, n + 1)
                v.tensor_scalar(RSTD[:, :], ps[:, 0:T], 1.0 / D, EPS, ALU.mult, ALU.add).then_inc(var_done, 1)
                dve.wait_ge(std_done, n + 1)
                link(v.reciprocal(RSTD[:, :], RSTD[:, :]))
                v.tensor_tensor(HT[:, :, :], X[:, :, :], RSTD[:, :].unsqueeze(1).to_broadcast([P, KT, T]),
                                ALU.mult).then_inc(normed, 1)

            def modulate(which, gain):
                v.scalar_tensor_tensor(AMP[:, :], MOD[:, which, :], 1.0, COLS[:, l, gain:gain + KT], ALU.add, ALU.mult)

            def wrap(out, x, k):
                link(v.tensor_scalar(k, x, 1.0 / (2 * math.pi), ROUND, ALU.mult, ALU.add))
                link(v.tensor_scalar(k, k, ROUND, None, ALU.subtract))
                link(v.scalar_tensor_tensor(out, k, -TWO_PI_HI, x, ALU.mult, ALU.add))
                link(v.scalar_tensor_tensor(out, k, -TWO_PI_LO, out, ALU.mult, ALU.add))
                return v.tensor_scalar(out, out, PI, -PI, ALU.min, ALU.max)

            def top16(rows, vals, idx):
                for half in range(2):
                    o = slice(8 * half, 8 * half + 8)
                    for r, a in zip(rows, vals):
                        last = v.max(a[:, o], r)
                    link(last)
                    for r, a, n in zip(rows, vals, idx):
                        last = v.max_index(n[:, o], a[:, o], r)
                    if half == 0:
                        link(last)
                        for r, a in zip(rows, vals):
                            last = v.match_replace(r, a[:, o], r, -3.0e38)
                    link(last)

            dve.wait_ge(in_cols, 48)
            for l in range(L):
                v.memset(ONES[:, :], 1.0).then_inc(ones_ready, 1)
                dve.wait_ge(cond_done, l + 1)

                def ada(i):
                    for j in range(8):
                        dve.wait_ge(in_ada[j], i * 16 + (l * 6 + 1) * 16)
                        v.tensor_tensor_reduce(out=ADA[:, j, :], in0=ADA[:, j, :], in1=CB[:, :], scale=1.0, scalar=0.0,
                                               op0=ALU.mult, op1=ALU.add, accum_out=ADA8[:, j:j + 1]).then_inc(ada_used, 1)
                    dve.wait_ge(ada_used, i * 8 + (l * 48 + 8))
                    v.tensor_tensor(MOD[:, i, :], ADA8[:, :], COLS[:, l, bass.ds(i * 8, 8)], ALU.add).then_inc(mod_done, 1)
                    dve.wait_ge(mod_done, i + (l * 6 + 1))
                lre, lim = (COLS[:, l, o:o + ST] for o in (C_LRE, C_LIM))
                sv = lambda n: SV[:, n, :]
                dve.wait_ge(ssm_x, 2 * l + 1)
                v.tensor_tensor(sv(1), lre, sv(0), ALU.mult).then_inc(ssm_e, 1)
                link(v.tensor_tensor(sv(3), lim, sv(0), ALU.mult))
                wrap(sv(5), sv(3), sv(4)).then_inc(ssm_a, 1)

                dve.wait_ge(ssm_x, 2 * l + 2)
                dve.wait_ge(ssm_s, 3 * l + 1)
                link(v.tensor_tensor(sv(8), sv(7), sv(7), ALU.mult))
                link(v.tensor_scalar(sv(8), sv(8), -2.0, 1.0, ALU.mult, ALU.add))
                link(v.tensor_tensor(sv(8), sv(8), sv(2), ALU.mult))
                link(v.tensor_scalar(sv(8), sv(8), 1.0, None, ALU.subtract))
                link(v.tensor_tensor(sv(9), sv(6), sv(2), ALU.mult))
                link(v.tensor_tensor(sv(10), lre, lre, ALU.mult))
                link(v.tensor_tensor(sv(11), lim, lim, ALU.mult))
                link(v.tensor_tensor(sv(10), sv(10), sv(11), ALU.add))
                link(v.reciprocal(sv(10), sv(10)))
                link(v.tensor_tensor(sv(11), sv(8), lre, ALU.mult))
                link(v.tensor_tensor(sv(12), sv(9), lim, ALU.mult))
                link(v.tensor_tensor(sv(11), sv(11), sv(12), ALU.add))
                link(v.tensor_tensor(sv(13), sv(11), sv(10), ALU.mult))
                link(v.tensor_tensor(sv(11), sv(9), lre, ALU.mult))
                link(v.tensor_tensor(sv(12), sv(8), lim, ALU.mult))
                link(v.tensor_tensor(sv(11), sv(11), sv(12), ALU.subtract))
                v.tensor_tensor(sv(14), sv(11), sv(10), ALU.mult).then_inc(f_done, 1)
                with dve.Fori(0, 2) as i:
                    ada(i)
                link(v.scalar_tensor_tensor(AMP[:, :], MOD[:, SC1, :], 1.0, COLS[:, l, C_NMIX:C_NMIX + KT],
                                            ALU.add, ALU.mult))
                norm(2 * l)
                for u in range(2):
                    link(v.tensor_tensor(TB[:, :, :], IOTA[:, :].unsqueeze(1).to_broadcast([P, 4, T]),
                                         SV[:, 5, 4 * u:4 * u + 4].unsqueeze(2).to_broadcast([P, 4, T]), ALU.mult))
                    wrap(TRIG[u][1][:, :, :], TB[:, :, :], TURNS[:, :, :]).then_inc(ssm_a, 1)
                    dve.wait_ge(ssm_a, 3 * l + 2 + u)
                for u in range(2):
                    COS, SIN = TRIG[u]
                    dve.wait_ge(ssm_s, 3 * l + 2 + u)
                    dve.wait_ge(bu_mm, 2 * l + u + 1)
                    bre = ps[:, 0:1024].rearrange("p (r t) -> p r t", t=T)
                    bim = ps[:, 1024:2048].rearrange("p (r t) -> p r t", t=T)
                    if u:
                        dve.wait_ge(sy_mm, 2 * l + 1)
                    v.tensor_tensor(TA[:, :, :], COS[:, :, :], bre, ALU.mult)
                    link(v.tensor_tensor(TB[:, :, :], SIN[:, :, :], bim, ALU.mult))
                    link(v.tensor_tensor(ZRE[:, :, :], TA[:, :, :], TB[:, :, :], ALU.add))
                    v.tensor_tensor(TA[:, :, :], COS[:, :, :], bim, ALU.mult)
                    link(v.tensor_tensor(TB[:, :, :], SIN[:, :, :], bre, ALU.mult))
                    v.tensor_tensor(ZIM[:, :, :], TA[:, :, :], TB[:, :, :], ALU.subtract).then_inc(bu_ev, 1)
                    dve.wait_ge(bu_ev, 2 * l + u + 1)
                    for r in range(4):
                        mag = SV[:, 2, 4 * u + r:4 * u + r + 1].to_broadcast([P, T])
                        v.tensor_tensor_scan(ZRE[:, r, :], mag, ZRE[:, r, :], 0.0, ALU.mult, ALU.add)
                        last = v.tensor_tensor_scan(ZIM[:, r, :], mag, ZIM[:, r, :], 0.0, ALU.mult, ALU.add)
                    link(last)
                    v.tensor_tensor(TA[:, :, :], COS[:, :, :], ZRE[:, :, :], ALU.mult)
                    v.tensor_tensor(TB[:, :, :], SIN[:, :, :], ZIM[:, :, :], ALU.mult)
                    v.tensor_tensor(COS[:, :, :], COS[:, :, :], ZIM[:, :, :], ALU.mult)
                    link(v.tensor_tensor(SIN[:, :, :], SIN[:, :, :], ZRE[:, :, :], ALU.mult))
                    v.tensor_tensor(ZRE[:, :, :], TA[:, :, :], TB[:, :, :], ALU.subtract)
                    v.tensor_tensor(ZIM[:, :, :], COS[:, :, :], SIN[:, :, :], ALU.add).then_inc(xs_done, 1)
                    dve.wait_ge(xs_done, 2 * l + u + 1)
                dve.wait_ge(sy_mm, 2 * l + 2)
                for u in range(2):
                    last = v.scalar_tensor_tensor(YG[:, u, :], UT[:, u, :], COLS[:, l, C_D + u:C_D + u + 1],
                                                  PS[:, 4, u * T:(u + 1) * T], ALU.mult, ALU.add)
                last.then_inc(sy_in, 1)
                ada(2)
                dve.wait_ge(glu_gate, l + 1)
                v.tensor_tensor(ZG[:, :, :], PS[:, 0:2, 0:SW], ZG[:, :, :], ALU.mult).then_inc(glu_read, 1)
                dve.wait_ge(glu_read, l + 1)
                for t in range(TT):
                    link(v.tensor_tensor_reduce(out=SCR[:, 0:SW], in0=ZG[:, t, :], in1=ZG[:, t, :],
                                                scale=1.0, scalar=0.0, op0=ALU.mult, op1=ALU.add,
                                                accum_out=RMS[:, 2 + t:3 + t]))

                dve.wait_ge(in_mix, 64 * (l + 1))
                dve.wait_ge(rot_mm, l + 1)
                v.tensor_tensor(ROT[:, :, :], ps[:, 0:1536].rearrange("p (a t) -> p a t", t=T),
                                ROPE[:, 1, :].unsqueeze(1).to_broadcast([P, 6, T]), ALU.mult).then_inc(rot_read, 1)
                link(v.tensor_tensor(QK[:, :, :], QK[:, :, :], ROPE[:, 0, :].unsqueeze(1).to_broadcast([P, 6, T]), ALU.mult))
                link(v.tensor_tensor(QK[:, :, :], QK[:, :, :], ROT[:, :, :], ALU.add))
                for parity in range(2):
                    last = v.tensor_scalar(QM[:, parity, :, :], QK[:, 0:3, :], MASK[:, 8 + parity:9 + parity], None, ALU.mult)
                last.then_inc(rot_done, 1)

                dve.wait_ge(att_mm, l + 1)
                v.tensor_tensor(SA[:, :, :], ps[:, 0:768].rearrange("p (h t) -> p h t", h=NH),
                                bass.AP(BIAS, P - 1, [[NH * T, P], [T, NH], [-1, P]]), ALU.add)
                link(v.tensor_tensor(SB[:, :, :], ps[:, 768:2304].rearrange("p (h t) -> p h t", h=NH),
                                     bass.AP(BIAS, T - 1, [[NH * T, P], [T, NH], [-1, T]]), ALU.add))
                v.memset(SA[0:CHUNK, :, CHUNK:P], NEG)
                link(v.memset(SB[0:CHUNK, :, T - CHUNK:T], NEG))
                v.reduce_max(SM[:, 0, 0:NH], SA[:, :, :], AX.X).then_inc(att_in, 1)
                link(v.reduce_max(SM[:, 0, NH:12], SB[:, :, :], AX.X))
                v.tensor_tensor(SA[:, :, :], SA[:, :, :], SM[:, 0, 0:NH].unsqueeze(2).to_broadcast([P, NH, P]), ALU.subtract)
                v.tensor_tensor(SB[:, :, :], SB[:, :, :], SM[:, 0, NH:12].unsqueeze(2).to_broadcast([P, NH, T]),
                                ALU.subtract).then_inc(att_sub, 1)
                ada(3)

                dve.wait_ge(ret_mm, l + 1)
                v.tensor_tensor(SR0[:, :, :], ps[:, 0:1536].rearrange("p (h t) -> p h t", h=NH), DEC0[:, :, :], ALU.mult)
                v.tensor_tensor(SR1[:, :, :], ps[:, 1536:2304].rearrange("p (h t) -> p h t", h=NH), DEC1[:, :, :],
                                ALU.mult).then_inc(ret_in, 1)
                dve.wait_ge(att_exp, l + 1)
                v.reduce_sum(SM[:, 1, 0:NH], SA[:, :, :], AX.X)
                link(v.reduce_sum(SM[:, 1, NH:12], SB[:, :, :], AX.X))
                link(v.reciprocal(SM[:, 1, :], SM[:, 1, :]))

                yr = YR[:, :, :].rearrange("p t (h e) -> p (t h) e", e=HD)
                dve.wait_ge(ry_mm, l + 1)
                v.tensor_copy(YR[:, :, :], PS[:, 6:8, 0:AW]).then_inc(ry_ev, 1)
                dve.wait_ge(ry_ev, l + 1)
                link(v.reduce_sum(SM[:, 2, :], yr, AX.X))
                link(v.tensor_scalar(SM[:, 2, :], SM[:, 2, :], -1.0 / HD, None, ALU.mult))
                link(v.tensor_tensor(yr, yr, SM[:, 2, :].unsqueeze(2).to_broadcast([P, 12, HD]), ALU.add))
                link(v.tensor_tensor(YSQ, yr, yr, ALU.mult))
                link(v.reduce_sum(SM[:, 3, :], YSQ, AX.X))
                v.tensor_scalar(SM[:, 3, :], SM[:, 3, :], 1.0 / HD, EPS, ALU.mult, ALU.add).then_inc(rvar, 1)
                dve.wait_ge(gate_silu, l + 1)
                dve.wait_ge(rstd_done, l + 1)
                link(v.reciprocal(SM[:, 3, :], SM[:, 3, :]))
                link(v.tensor_tensor(yr, yr, SM[:, 3, :].unsqueeze(2).to_broadcast([P, 12, HD]), ALU.mult))
                link(v.tensor_tensor(MERGED[:, :, AW:2 * AW], YR[:, :, :], GR[:, :, :], ALU.mult))

                dve.wait_ge(ao_mm, l + 1)
                for t in range(TT):
                    link(v.tensor_tensor(MERGED[:, t, 0:AW].rearrange("p (h e) -> p h e", e=HD),
                                         PS[:, 5 + t, 0:AW].rearrange("p (h e) -> p h e", e=HD),
                                         SM[:, 1, t * NH:(t + 1) * NH].unsqueeze(2).to_broadcast([P, NH, HD]), ALU.mult))
                for t in range(TT):
                    link(v.tensor_tensor_reduce(out=SCR[:, 0:AW], in0=MERGED[:, t, 0:AW], in1=MERGED[:, t, 0:AW],
                                                scale=1.0, scalar=0.0, op0=ALU.mult, op1=ALU.add,
                                                accum_out=RMS[:, t:t + 1]))

                v.tensor_scalar(RMS[:, 0:2], RMS[:, 0:2], 1.0 / AW, EPS, ALU.mult, ALU.add)
                v.tensor_scalar(RMS[:, 2:4], RMS[:, 2:4], 1.0 / SW, EPS, ALU.mult, ALU.add).then_inc(mvar, 1)
                dve.wait_ge(mstd, l + 1)
                link(v.reciprocal(RMS[:, :], RMS[:, :]))
                for t in range(TT):
                    v.tensor_scalar(MERGED[:, t, 0:AW], MERGED[:, t, 0:AW], RMS[:, t:t + 1], None, ALU.mult)
                    last = v.tensor_scalar(MERGED[:, t, 2 * AW:D], ZG[:, t, :], RMS[:, 2 + t:3 + t], None, ALU.mult)
                last.then_inc(merged, 1)

                with dve.Fori(4, 6) as i:
                    ada(i)
                for d in range(KT):
                    dve.wait_ge(wo_mm, l * KT + d // 2 * 2 + 2)
                    last = v.scalar_tensor_tensor(X[:, d, :], ps[:, d * T:(d + 1) * T], MOD[:, G1, d:d + 1], X[:, d, :],
                                                  ALU.mult, ALU.add)
                last.then_inc(x_ready, 1)
                dve.wait_ge(x_ready, 2 * l + 1)
                link(v.scalar_tensor_tensor(AMP[:, :], MOD[:, SC2, :], 1.0, COLS[:, l, C_NFFN:C_NFFN + KT],
                                            ALU.add, ALU.mult))
                norm(2 * l + 1)
                dve.wait_ge(h_hi, l + 1)
                v.tensor_tensor(HL[:, :, :], HT[:, :, :], HH[:, :, :].bitcast(F32), ALU.subtract).then_inc(h_split, 1)

                for n in range(16):
                    dve.wait_ge(ks_mm, l * 16 + n + 1)
                    v.tensor_copy(KS[:, :, n, :], PS[:, 6 + n % 2, 0:T].rearrange("p (t k) -> p t k", t=TT)).then_inc(ks_ev, 1)
                    dve.wait_ge(ks_ev, l * 16 + n + 1)
                    top16([KS[:, t, n, :] for t in range(TT)], [V16[:, t, n, :] for t in range(TT)],
                          [I16[:, t, n, :] for t in range(TT)])
                link(v.tensor_copy(I16F[:, :, :, :], I16[:, :, :, :]))
                for t in range(TT):
                    side = V16[:, t, :, :].rearrange("p (h s) a -> p h s a", s=2)
                    link(v.tensor_tensor(CAND[:, :, :, :], side[:, :, 0, :].unsqueeze(3).to_broadcast([P, PH, TOPK, TOPK]),
                                         side[:, :, 1, :].unsqueeze(2).to_broadcast([P, PH, TOPK, TOPK]), ALU.add))
                    for h in range(0, PH, 4):
                        top16([CAND[:, g, :, :].rearrange("p a b -> p (a b)") for g in range(h, h + 4)],
                              [BEST[:, t, g, :] for g in range(h, h + 4)], [POS[:, t, g, :] for g in range(h, h + 4)])
                gate = SEL[:, 2, :, :].rearrange("p t (h k) -> p t h k", h=PH)
                for t in range(TT):
                    last = v.tensor_tensor(gate[:, t], BEST[:, t, :, :], BEST[:, t, :, 0:1].to_broadcast([P, PH, TOPK]), ALU.subtract)
                last.then_inc(gate_in, 1)
                v.tensor_scalar(POSA[:, :, :, :], POS[:, :, :, :], 4, None, ALU.logical_shift_right)
                link(v.tensor_scalar(POSB[:, :, :, :], POS[:, :, :, :], 15, None, ALU.bitwise_and))
                v.tensor_copy(AF[:, :, :, :], POSA[:, :, :, :])
                link(v.tensor_copy(BF[:, :, :, :], POSB[:, :, :, :]))
                for s, pos in enumerate((AF, BF)):
                    for t in range(TT):
                        keys = I16F[:, t, :, :].rearrange("p (h s) a -> p h s a", s=2)[:, :, s, :]
                        link(v.tensor_tensor(EQ[:, :, :, :], pos[:, t, :, :].unsqueeze(3).to_broadcast([P, PH, TOPK, TOPK]),
                                             IOTA[:, 0:TOPK].unsqueeze(1).unsqueeze(1).to_broadcast([P, PH, TOPK, TOPK]),
                                             ALU.is_equal))
                        link(v.tensor_tensor(EQ[:, :, :, :], EQ[:, :, :, :],
                                             keys.unsqueeze(2).to_broadcast([P, PH, TOPK, TOPK]), ALU.mult))
                        link(v.reduce_sum(SEL[:, s, t, :].rearrange("p (h k) -> p h k", h=PH), EQ[:, :, :, :], AX.X))
                dve.wait_ge(gate_exp, l + 1)
                link(v.reduce_sum(GSUM[:, :, :], gate, AX.X))
                link(v.reciprocal(GSUM[:, :, :], GSUM[:, :, :]))
                for t in range(TT):
                    last = v.tensor_tensor(gate[:, t], gate[:, t], GSUM[:, t, :].unsqueeze(2).to_broadcast([P, PH, TOPK]), ALU.mult)
                last.then_inc(picks, 1)

                dve.wait_ge(pickt, l + 1)

                def onehots(b, tok):
                    if b >= KB:
                        v.tensor_tensor(OHB[:, b, :, :], IOTA[:, 0:P].unsqueeze(1).to_broadcast([P, 4, P]),
                                        SELT[:, 1, bass.ds(tok, 4)].unsqueeze(2).to_broadcast([P, 4, P]), ALU.is_equal)
                    for q in range(4):
                        one = lambda a: SELT[:, a, bass.ds(tok + q, 1)]
                        last = v.tensor_scalar(OHA[:, b, q, :], IOTA[:, 0:P], one(0), one(2), ALU.is_equal, ALU.mult)
                    last.then_inc(onehot, 1)
                for b in range(4):
                    onehots(b, 4 * b)
                with dve.Fori(1, 16) as i:
                    for b in range(4):
                        dve.wait_ge(w_mm, i * 4 + (l * 64 + b - 3))
                        onehots(b, i * 16 + 4 * b)

                E0 = l * NE

                def u_low(e, b):
                    dve.wait_ge(u_hi, e + 1)
                    v.tensor_tensor(UL[:, b, :, :], RING[:, b, :].rearrange("p (k n) -> p k n", n=P),
                                    UH[:, b, :, :].bitcast(F32), ALU.subtract).then_inc(u_split, 1)

                def v_low(e, b):
                    dve.wait_ge(v_hi, e + 1)
                    v.tensor_tensor(VL[:, b, :], RING[:, 2 + b, :], VH[:, b, :].bitcast(F32), ALU.subtract).then_inc(v_split, 1)

                def gated(e, b, i, first=False):
                    dve.wait_ge(gelu_done, e + 1)
                    if not first:
                        dve.wait_ge(g_ready, e)
                    v.tensor_tensor(G32[:, :], GE[:, b, :], WT[:, i, :], ALU.mult).then_inc(g_prod, 1)
                    dve.wait_ge(g_prod, e + 1)
                    if not first:
                        dve.wait_ge(v_used, e)
                    v.tensor_copy(GH[:, :], G32[:, :]).then_inc(g_hi, 1)
                    dve.wait_ge(g_hi, e + 1)
                    v.tensor_tensor(GL[:, :], G32[:, :], GH[:, :].bitcast(F32), ALU.subtract).then_inc(g_ready, 1)

                dve.wait_ge(w_ev, (l + 1) * 64)
                u_low(E0, 0)
                for e in (0, 1):
                    u_low(E0 + e + 1, (e + 1) % 2)
                    v_low(E0 + e, e)
                    gated(E0 + e, e, e, first=(e == 0))
                with dve.Fori(1, NE // 2 - 1) as i:
                    for b in (0, 1):
                        u_low(i * 2 + (E0 + b + 1), 1 - b)
                        v_low(i * 2 + (E0 + b), b)
                        gated(i * 2 + (E0 + b), b, i * 2 + b)
                u_low(E0 + NE - 1, 1)
                for e in (NE - 2, NE - 1):
                    v_low(E0 + e, e % 2)
                    gated(E0 + e, e % 2, e)
                dve.wait_ge(acc_mm, l + 1)
                for k in range(KT):
                    last = v.scalar_tensor_tensor(X[:, k, :], ps[:, 2048 + k * T:2048 + (k + 1) * T], MOD[:, G2, k:k + 1],
                                                  X[:, k, :], ALU.mult, ALU.add)
                last.then_inc(x_ready, 1)
                dve.wait_ge(x_ready, 2 * l + 2)
            v.memset(ONES[:, :], 1.0).then_inc(ones_ready, 1)
            norm(2 * L)


def _tables():
    inv = np.float32(10000.0) ** (-np.arange(32, dtype=np.float32) / np.float32(32))
    ang = inv[:, None] * np.arange(T, dtype=np.float32)[None, :]
    cos, sin = np.cos(ang), np.sin(ang)
    rope = np.stack([np.concatenate([cos] * 4), np.concatenate([-sin, sin] * 2)], axis=1)
    perm = np.zeros((P, P), np.float32)
    for p in range(P):
        perm[p ^ 32, p] = 1.0
    log_g = np.log1p(-np.power(2.0, -5.0 - np.arange(NH)))
    tk, tq = np.arange(T)[:, None], np.arange(T)[None, :]
    dec = np.exp(log_g[:, None, None] * np.abs(tq - tk)) * (tk // CHUNK <= tq // CHUNK) * HD ** -0.5
    dec0 = dec[:, :P, :].transpose(1, 0, 2).reshape(P, -1)
    dec1 = dec[:, P:, P:].transpose(1, 0, 2).reshape(P, -1)
    p = np.arange(P)[:, None]
    mask = np.concatenate([p // GCH % 2 == np.arange(2), p // 32 == np.arange(4), (p // HD == np.arange(2)) * HD ** -0.5,
                           p // HD == np.arange(2)], axis=1)
    f = lambda a: np.ascontiguousarray(a, dtype=np.float32)
    return dict(ident_c=np.eye(P, dtype=np.float32), iota_c=f(np.broadcast_to(np.arange(T), (P, T))),
                decay_c=f(np.concatenate([dec0, dec1], axis=1)), rope_c=f(rope), perm_c=perm, mask_c=f(mask))


def _layout(i):
    col = lambda a: a.reshape(L, -1, P).transpose(0, 2, 1)
    wtile = lambda w: w.reshape(L, KT, P, -1, P).transpose(0, 3, 2, 1, 4).reshape(L, -1, P, D)
    ldt = np.repeat(i["ssm_log_dt"], STATES, axis=1)
    cols = np.concatenate([col(i[n]) for n in ("b_ada", "norm_mix", "norm_ffn", "merge_gain", "ssm_d",
                                               "ssm_lambda_re", "ssm_lambda_im")] + [col(ldt)], axis=2)
    bt = lambda b: b.transpose(0, 1, 3, 2).reshape(L, 2, P, STATES).transpose(0, 2, 1, 3)
    ct = lambda c: c.reshape(L, ST, 2, GCH, STATES).transpose(0, 2, 4, 1, 3).reshape(L, P, ST, GCH)
    return dict(
        xT=i["x"][0].T, c=i["c"][0], cols=cols.transpose(1, 0, 2), fcol=i["final_norm"].reshape(KT, P).T,
        w_ada=i["w_ada"].transpose(0, 2, 1), w_in=wtile(i["w_in"]), w_out=wtile(i["w_out"]), w_q=wtile(i["peer_w_q"]),
        w_glu=i["w_glu"], rel_bias=i["rel_bias"], b_re=bt(i["ssm_b_re"]), b_im=bt(i["ssm_b_im"]),
        c_re=ct(i["ssm_c_re"]), c_im=ct(i["ssm_c_im"]),
        subkeys=i["peer_subkeys"].reshape(L, 16 * NK, P).transpose(0, 2, 1),
        u_tab=i["peer_u"].reshape(L, NE, P, KT, P).transpose(0, 1, 4, 3, 2).reshape(L, NE, P, D),
        v_tab=i["peer_v"].reshape(L, NE, P, D))


_ORDER = ["xT", "c", "cols", "fcol", "w_ada", "w_in", "w_out", "w_q", "w_glu", "rel_bias", "b_re", "b_im", "c_re",
          "c_im", "subkeys", "u_tab", "v_tab", "ident_c", "iota_c", "decay_c", "rope_c", "perm_c", "mask_c"]


def kernel(**inputs):
    import concourse.bacc as _bacc
    from concourse.bass_utils import run_bass_kernel_spmd as _run

    data = _layout({k: np.asarray(a) for k, a in inputs.items()})
    data.update(_tables())
    nc = _bacc.Bacc("TRN2", target_bir_lowering=False, num_devices=1)
    arrays, args = {}, []
    for name in _ORDER:
        a = np.ascontiguousarray(data[name])
        arrays[f"in_{name}_dram"] = a
        args.append(nc.dram_tensor(f"in_{name}_dram", a.shape, mybir.dt.from_np(a.dtype), kind="ExternalInput").ap())
    out = nc.dram_tensor("out_T_dram", (D, T), F32, kind="ExternalOutput")
    trunk(nc, *args, out.ap())
    r = _run(nc, [arrays], core_ids=[0])
    return np.ascontiguousarray(r.results[0]["out_T_dram"].T)[None]
```

```python
import math
from contextlib import ExitStack

import numpy as np

import concourse.bass as bass
from concourse import mybir

F32 = mybir.dt.float32
F32R = mybir.dt.float32r
U32 = mybir.dt.uint32
BF16 = mybir.dt.bfloat16
ALU = mybir.AluOpType
ACT = mybir.ActivationFunctionType
AX = mybir.AxisListType

P = 128
L = 2
D = 1024
T = 256
KT = D // P
TT = T // P
CHUNK = 64
HD = 64
NH = 6
AW = NH * HD
SW = 256
STATES = 64
GCH = 16
ST = 16 * STATES // P
IN_COLS = 3 * AW + 4 * AW + SW
IN_TILES = IN_COLS // P
PH = 8
NK = 128
TOPK = 16
NE = NK
EPS = 1e-6
NEG = -1e30
MT_FIRST, MT_LAST = (0, 1, 2, 6, 7), (3, 4, 5)
MT_AT = dict(zip(MT_FIRST + MT_LAST, (0, 256, 512, 768, 1024, 1536, 1792, 2048)))
LAG = 2
PAIRS = [(0, 2, 16, 0), (2, 4, 8, 32), (4, 8, 4, 48), (8, 16, 1, 64)]
NCAND = 72
TWO_PI_HI = 6.28125
TWO_PI_LO = 2.0 * math.pi - 6.28125
ROUND = 1.5 * 2.0 ** 23
PI = 3.1415925

COND_TILE = 100
ADA_TILE = 110
C_BADA, C_NMIX, C_NFFN, C_GAIN, C_D, C_LRE, C_LIM, C_LDT = 0, 48, 56, 64, 72, 74, 82, 90
C_ALL = 98
SH1, SC1, G1, SH2, SC2, G2 = range(6)


def trunk(nc, xT, c, cols, fcol, w_ada, w_in, w_out, w_q, w_glu, rel_bias, b_re, b_im, c_re, c_im,
          subkeys, u_tab, v_tab, ident_c, iota_c, decay_c, rope_c, perm_c, mask_c, outT):
    ctx = ExitStack()
    with ctx:
        base = 16512

        def at(name, floats, shape, dt=F32):
            return nc.alloc_sbuf_tensor_at(name, shape, dt, offset=base + 4 * floats)

        def sem(name):
            return ctx.enter_context(nc.semaphore(name))

        WT = at("gates_T", 0, [P, NE, T])
        HT = at("h_T", 0, [P, KT, T])
        MERGED = at("merged", 16384, [P, TT, D])
        QA = at("q_att_T", 10240, [P, 2, 3, T])
        KA = at("k_att_T", 2816, [P, 3, T])
        VA = at("v_att", 3584, [P, TT, AW])
        QK = at("qk_ret_T", 4352, [P, 6, T])
        VR = at("v_ret", 5888, [P, TT, AW])
        GR = at("g_ret", 6656, [P, TT, AW])
        UT = at("u_ssm_T", 7424, [P, 2, T])
        SQ = at("squares", 7936, [P, KT, T])
        SAB = at("scores_ab", 7936, [P, NH * (P + T)])
        SA = SAB[:, 0:NH * P].rearrange("p (h t) -> p h t", h=NH)
        SB = SAB[:, NH * P:].rearrange("p (h t) -> p h t", h=NH)
        PT = at("probs_T", 10240, [P, 18, P])
        SR0 = at("ret_scores_0", 12544, [P, NH, T])
        SR1 = at("ret_scores_1", 14080, [P, NH, P])
        UM = at("u_masked", 12544, [P, 2, 4, T])
        DEC0 = at("decay_0", 14848, [P, NH, T])
        DEC1 = at("decay_1", 16384, [P, NH, P])
        BIAS = at("rel_bias_rows", 17152, [P, NH, T])
        ROPE = at("rope", 18688, [P, 2, T])
        YSQ = at("y_squares", 19968, [P, 2 * NH, HD])[:, :, :]
        YR = at("y_ret", 19200, [P, TT, AW])
        ROT = at("rotated", 19968, [P, 6, T])
        QM = at("q_ret_masked", 21760, [P, 2, 3, T])
        MT = at("merged_T", 21504, [P, KT, T])
        RSTD = at("rstd", 50688, [P, T])
        ADAN = at("next_w_ada_ring", 2048, [P, 4, D])
        ADA = at("w_ada_ring", 24576, [P, 8, D])
        QT = at("query_T", 2048, [P, 2, T])
        SUBT = at("subkeys_T", 4096, [P, 16, NK])
        KS = at("key_scores", 6144, [P, TT, 16, NK])
        CAND = at("candidates", 10240, [P, 2, 2, NCAND])
        PICKW = at("picked_keys", 10752, [P, 2, TOPK, TT, P], BF16)
        COUNT = at("rows_passed", 18944, [P, TT * P])
        V16 = at("top_scores", 18432, [P, TT, 16, TOPK])
        I16 = at("top_keys", 14848, [P, TT, 16, TOPK], U32)
        I16F = at("top_keys_f", 15360, [P, TT, 16, TOPK])
        BEST = at("best", 15872, [P, TT, PH, TOPK])
        POS = at("best_pos", 16128, [P, TT, PH, TOPK], U32)
        PF = at("best_pos_f", 16384, [P, TT, PH, TOPK])
        PM = at("past_64", 16640, [P, TT, PH, TOPK])
        AF = at("pos_a_f", 16896, [P, TT, PH, TOPK])
        BF = at("pos_b_f", 17152, [P, TT, PH, TOPK])
        GATE = at("gates", 17408, [P, TT, P])
        GSUM = at("gate_sum", 18176, [P, TT, PH])
        ACC = at("mixed", 2048, [P, TT, D])
        X = at("x_T", 32768, [P, KT, T])
        RING = at("weight_ring", 34816, [P, 4, D])
        UH = at("u_hi", 38912, [P, 2, KT, P], F32R)
        UL = at("u_lo", 40960, [P, 2, KT, P], F32R)
        VH = at("v_hi", 43008, [P, 2, D], F32R)
        VL = at("v_lo", 45056, [P, 2, D], F32R)
        HH = at("h_hi", 47104, [P, KT, T], F32R)
        HL = at("h_lo", 49152, [P, KT, T], F32R)
        TRIG = [(at("cos_0", 38912, [P, 4, T]), at("sin_0", 39936, [P, 4, T])),
                (at("cos_1", 19200, [P, 4, T]), at("sin_1", 20224, [P, 4, T]))]
        ZRE = at("z_re", 40960, [P, 4, T])
        ZIM = at("z_im", 41984, [P, 4, T])
        TA = at("tmp_a", 43008, [P, 4, T])
        TB = at("tmp_b", 44032, [P, 4, T])
        CFRE = at("cf_re", 45056, [P, ST, P])
        CFIM = at("cf_im", 46080, [P, ST, P])
        BTRE = at("b_re_T", 47104, [P, 2, P])
        BTIM = at("b_im_T", 47360, [P, 2, P])
        WGLU = at("w_glu_sb", 47616, [P, 2, 2 * SW])
        YG = at("y_gelu_T", 48640, [P, 2, T])
        BRAW = at("b_raw", 49152, [P, 2, 2, STATES])
        CRAW = at("c_raw", 49408, [P, 2, ST, GCH])
        CTMP = at("c_tmp", 49664, [P, 4, ST, GCH])
        ZG = at("z_gate", 50176, [P, TT, SW])
        CB = at("cond", 23552, [P, D])
        SCR = at("scratch_row", 43008, [P, D])
        TURNS = at("turns", 7936, [P, 4, T])
        WQH = at("w_q_hi", 38912, [P, 2, KT, P], F32R)
        WQL = at("w_q_lo", 40960, [P, 2, KT, P], F32R)
        OHA = at("onehot_gate", 38912, [P, 8, 4, P])
        OHB = at("onehot_key", 43008, [P, 8, 4, P])
        GE = at("gelu", 51200, [P, 2, T])
        G32 = at("gated", 51712, [P, T])
        GH = at("gated_hi", 51968, [P, T], F32R)
        GL = at("gated_lo", 52224, [P, T], F32R)
        ONES = at("ones", 51200, [P, P])
        IOTA = at("iota", 51328, [P, T])
        IDENT = at("ident", 51584, [P, P])
        SELT = at("picks_T", 51712, [P, 3, T])
        COLS = at("cols", 52480, [P, L, C_ALL])
        FCOL = at("final_gain", 52680, [P, KT])
        MOD = at("mod", 52688, [P, 6, KT])
        AMP = at("amp", 52736, [P, KT])
        MASK = at("masks", 52944, [P, 10])
        SM = at("softmax_stat", 52752, [P, 4, 12])
        SV = at("ssm_vec", 52800, [P, 15, ST])
        ADA8 = at("ada_dots", 52928, [P, KT])
        POOL_GROUPS = (0, 3, 6)
        ACT_GROUPS = (1, 3, 5, 7)
        KB = len(POOL_GROUPS)
        KEY4 = at("key_columns", 52960, [P, 4, 8])
        ZERO4 = at("zeros", 52992, [P, 4])
        IDENTB = at("ident_bf16", 53000, [P, P], BF16)
        RMS = at("rms_stat", 52936, [P, 4])

        PS = ctx.enter_context(nc.psum_tensor("ps", [P, 8, 512], F32))
        ps = PS[:, :, :].rearrange("p b n -> p (b n)")

        in_x = sem("x_loaded")
        in_cols = sem("cols_loaded")
        in_c = sem("c_loaded")
        in_const = sem("const_loaded")
        in_mix = sem("mix_tables_loaded")
        in_sub = sem("subkeys_loaded")
        in_perm = sem("perm_loaded")
        in_ada = [sem(f"ada_loaded_{i}") for i in range(8)]
        in_ring = [sem(f"ring_loaded_{i}") for i in range(4)]
        out_done = sem("out_done")
        dve_step = sem("dve_step")
        act_step = sem("act_step")
        ada_used = sem("ada_used")
        cond_done = sem("cond_done")
        mod_done = sem("mod_done")
        x_ready = sem("x_ready")
        squared = sem("squared")
        ones_ready = sem("ones_ready")
        sumsq = sem("sumsq_done")
        var_done = sem("var_done")
        std_done = sem("std_done")
        normed = sem("normed")
        h_done = sem("h_done")
        h_hi = sem("h_hi_done")
        rvar = sem("ret_var_done")
        rstd_done = sem("ret_std_done")
        mvar = sem("merge_var_done")
        mstd = sem("merge_std_done")
        h_split = sem("h_split_done")
        proj_mm = sem("proj_product")
        proj_ev = sem("proj_evacuated")
        rot_mm = sem("rot_product")
        rot_done = sem("rotated_done")
        att_mm = sem("att_scores")
        att_in = sem("att_scores_taken")
        att_sub = sem("att_shifted")
        att_exp = sem("att_exp_done")
        ret_mm = sem("ret_scores")
        ret_in = sem("ret_scores_decayed")
        pt_mm = sem("probs_transposed")
        pt_ev = sem("probs_T_taken")
        ry_mm = sem("ret_product")
        ao_mm = sem("att_product")
        wide_mm = sem("wide_product_tile_used")
        ssm_e = sem("ssm_exp_in")
        ssm_x = sem("ssm_exp_out")
        ssm_a = sem("ssm_angle_in")
        ssm_s = sem("ssm_sine_out")
        bt_done = sem("b_masked")
        bu_mm = sem("bu_product")
        bu_ev = sem("bu_taken")
        xs_done = sem("states_done")
        cf_done = sem("cf_done")
        sy_mm = sem("ssm_y_product")
        sy_in = sem("ssm_y_sum")
        sy_gelu = sem("ssm_gelu_done")
        glu_mm = sem("glu_product")
        glu_gate = sem("glu_gate_done")
        merged = sem("merged_done")
        mt_mm = sem("merged_transposed")
        mt_ev = sem("merged_T_taken")
        wo_mm = sem("w_out_product")
        q_mm = sem("query_product")
        q_ev = sem("query_taken")
        ks_mm = sem("key_scores_product")
        ks_ev = sem("key_scores_taken")
        gate_in = sem("gate_shifted")
        gate_exp = sem("gate_exp")
        gates_ready = sem("gates_ready")
        pickt_mm = sem("picks_transposed")
        pickt = sem("picks_T_taken")
        onehot = sem("gate_onehots_done")
        in_ssm = sem("in_ssm_tables")
        um_done = sem("u_masked")
        ident_ready = sem("ident_bf16_ready")
        wq_hi = sem("w_q_hi_done")
        wq_split = sem("w_q_split")
        f_done = sem("ssm_factors_done")
        act_step = sem("scalar_step")
        pool_step = sem("gpsimd_step")
        glu_read = sem("glu_taken")
        rot_read = sem("rotation_product_taken")
        pick_terms = sem("four_terms_of_picked_keys")
        onehot_gated = sem("onehots_gated")
        key_copied = sem("key_columns_copied")
        zeros_ready = sem("zeros_ready")
        key_onehot = sem("key_onehots_done")
        w_mm = sem("gates_product")
        w_ev = sem("gates_taken")
        u_hi = sem("u_hi_done")
        u_split = sem("u_split_done")
        v_hi = sem("v_hi_done")
        v_split = sem("v_split_done")
        s_mm = sem("expert_scores")
        gelu_done = sem("expert_gelu")
        g_prod = sem("gated_product")
        g_hi = sem("gated_hi_done")
        g_ready = sem("gated_split")
        v_used = sem("experts_summed")
        acc_ev = sem("mixed_taken")
        acc_mm = sem("mixed_transposed")

        NSTREAM = IN_TILES + KT + 16
        assert NSTREAM % 4 == 3

        def ring_pos(l, n):
            full, slot = (NSTREAM + 1) // 4 + NE // 2, n % 4
            return slot, 16 * (l * full - (l if slot == 3 else 0) + n // 4 + 1)

        def expert_pos(l, v, b):
            full, slot = (NSTREAM + 1) // 4 + NE // 2, 2 * v + b
            n = (NSTREAM + 1) // 4 - (1 if slot == 3 else 0)
            return slot, l * full - (l if slot == 3 else 0) + n + 1

        TILE_IN, TILE_OUT, TILE_Q = 0, IN_TILES, IN_TILES + KT
        IN_ORDER = [21, 22, 9, 10, 11, 12, 13, 14, 0, 1, 2, 3, 4, 5, 6, 7, 8, 15, 16, 17, 18, 19, 20]

        ADA_BEHIND = [16 + min(8, 2 * max(0, n - 3)) for n in range(15)] + [26, 28, 30, 32, 32, 32, 32, 32, 32, 40, 40, 48]

        N_PROJ = 20

        block = ctx.enter_context(nc.Block())

        @block.sync
        def _(sp):
            for l in range(L):

                def ada(m):
                    n = l * 48 + m
                    if m >= 8:
                        sp.wait_ge(ada_used, n - 7)
                    sp.dma_start(ADA[:, m % 8, :], w_ada[l, m * P:(m + 1) * P, :]).then_inc(in_ada[m % 8], 16)

                def stream(n):
                    slot, value = ring_pos(l, n)
                    if n >= 4:
                        m = n - 4
                        if m < TILE_OUT:
                            g, a = divmod(m - 14, 3)
                            if m < 14:
                                sp.wait_ge(proj_mm, l * N_PROJ + m + 1)
                            elif a < 2:
                                sp.wait_ge(wide_mm, l * 6 + 2 * g + a + 1)
                            else:
                                sp.wait_ge(proj_mm, l * N_PROJ + 16 + 2 * g)
                        elif m < TILE_Q:
                            sp.wait_ge(wo_mm, l * KT + m - TILE_OUT + 1)
                        else:
                            sp.wait_ge(wq_split, l * 16 + m - TILE_Q + 1)
                    if n < TILE_OUT:
                        src = w_in[l, IN_ORDER[n]]
                    elif n < TILE_Q:
                        src = w_out[l, n - TILE_OUT]
                    else:
                        src = w_q[l, n - TILE_Q]
                    sp.dma_start(RING[:, slot, :], src).then_inc(in_ring[slot], 16)

                if l == 0:
                    sp.dma_start(CB[:, :], bass.AP(c.tensor, 0, [[0, P], [1, D]])).then_inc(in_c, 16)
                    for m in range(4):
                        ada(m)
                    sp.dma_start(COLS[:, :, :], cols).then_inc(in_cols, 16)
                    sp.dma_start(FCOL[:, :], fcol).then_inc(in_cols, 16)
                    sp.dma_start(MASK[:, :], mask_c).then_inc(in_cols, 16)
                    sp.dma_start(X[:, :, :], xT.rearrange("(k p) t -> p k t", p=P)).then_inc(in_x, 16)
                    sp.dma_start(IDENT[:, :], ident_c).then_inc(in_const, 16)
                    sp.dma_start(IOTA[:, :], iota_c).then_inc(in_const, 16)
                    for m in range(4, 16):
                        ada(m)
                for n in range(4):
                    stream(n)
                sp.dma_start(BRAW[:, 0, :, :], b_re[l]).then_inc(in_ssm, 16)
                sp.dma_start(BRAW[:, 1, :, :], b_im[l]).then_inc(in_ssm, 16)
                sp.dma_start(CRAW[:, 0, :, :], c_re[l]).then_inc(in_ssm, 16)
                sp.dma_start(CRAW[:, 1, :, :], c_im[l]).then_inc(in_ssm, 16)
                sp.dma_start(WGLU[:, :, :], w_glu[l].rearrange("(k p) n -> p k n", p=P)).then_inc(in_ssm, 16)
                sp.dma_start(ROPE[:, :, :], rope_c).then_inc(in_mix, 16)
                sp.dma_start(DEC0[:, :, :], decay_c[:, 0:NH * T].rearrange("p (h t) -> p h t", h=NH)).then_inc(in_mix, 16)
                sp.dma_start(DEC1[:, :, :], decay_c[:, NH * T:].rearrange("p (h t) -> p h t", h=NH)).then_inc(in_mix, 16)
                sp.dma_start(BIAS[:, :, :], bass.AP(rel_bias.tensor, l * NH * 513 + 129,
                                                    [[1, P], [513, NH], [1, T]])).then_inc(in_mix, 16)
                sp.dma_start(MT[:, 0, 0:P], perm_c).then_inc(in_perm, 16)
                m = 16
                for n in range(4, NSTREAM):
                    if n == TILE_Q:
                        sp.wait_ge(merged, 2 * l + 2)
                        sp.dma_start(SUBT[:, :, :], subkeys[l].rearrange("p (n k) -> p n k", k=NK)).then_inc(in_sub, 16)
                    stream(n)
                    while m < ADA_BEHIND[min(n, len(ADA_BEHIND) - 1)]:
                        ada(m)
                        m += 1
                for v in (0, 1):
                    for e in (0, 1):
                        slot, _ = expert_pos(l, v, e)
                        last = NSTREAM - 1 - (NSTREAM - 1 - slot) % 4
                        sp.wait_ge(wq_split, l * 16 + last - TILE_Q + 1)
                        sp.dma_start(RING[:, slot, :], (v_tab if v else u_tab)[l, e]).then_inc(in_ring[slot], 16)

                def expert_tile(e, b):
                    sp.wait_ge(u_split, e + (l * NE + 1))
                    sp.dma_start(RING[:, b, :], u_tab[l, e + 2]).then_inc(in_ring[b], 16)
                    sp.wait_ge(v_split, e + (l * NE + 1))
                    sp.dma_start(RING[:, 2 + b, :], v_tab[l, e + 2]).then_inc(in_ring[2 + b], 16)

                def expert_tiles(start, stop):
                    with sp.Fori(start // 2, stop // 2) as i:
                        for b in (0, 1):
                            expert_tile(i * 2 + b, b)
                if l == L - 1:
                    expert_tiles(0, NE - 2)
                else:
                    expert_tiles(0, COND_TILE - 2)
                    sp.wait_ge(g_prod, l * NE + COND_TILE - 4)
                    sp.dma_start(CB[:, :], bass.AP(c.tensor, 0, [[0, P], [1, D]])).then_inc(in_c, 16)
                    expert_tiles(COND_TILE - 2, ADA_TILE - 2)
                    with sp.Fori(0, 2) as i:
                        for j in range(8):
                            expert_tile(i * 8 + (ADA_TILE - 2 + j), j % 2)
                            sp.wait_ge(ada_used, i * 8 + ((l + 1) * 48 + j - 3))
                            sp.dma_start(ADAN[:, j % 4, :], w_ada[l + 1, bass.ds(i * (8 * P) + j * P, P), :]).then_inc(in_ada[j], 16)
                    expert_tiles(ADA_TILE + 14, NE - 2)
                sp.wait_ge(v_used, (l + 1) * NE)
                sp.dma_start(IDENT[:, :], ident_c).then_inc(in_const, 16)
                sp.dma_start(IOTA[:, :], iota_c).then_inc(in_const, 16)
            for half in range(2):
                k = half * KT // 2
                sp.wait_ge(normed, 2 * L * KT + k + KT // 2)
                sp.dma_start(outT.rearrange("(k p) t -> p k t", p=P)[:, k:k + KT // 2, :],
                             HT[:, k:k + KT // 2, :]).then_inc(out_done, 16)
            sp.wait_ge(out_done, 32)

        @block.tensor
        def _(pe):
            mm = nc.tensor.matmul

            def sum_squares(n, ks=range(KT)):
                pe.wait_ge(ones_ready, n // 2 + 1)
                bank = 4 * (n % 2)
                for k in ks:
                    pe.wait_ge(squared, n * KT + k + 1)
                    last = mm(PS[:, bank, 0:T], ONES[:, :], SQ[:, k, :], start=(k == 0), stop=(k == KT - 1))
                if k == KT - 1:
                    last.then_inc(sumsq, 1)

            for l in range(L):
                pe.wait_ge(in_const, 32 * (l + 1))
                sum_squares(2 * l)

                loaded = set()

                def tile(n):
                    slot, value = ring_pos(l, n)
                    if n not in loaded:
                        pe.wait_ge(in_ring[slot], value)
                        loaded.add(n)
                    return RING[:, slot, :].rearrange("p (k n) -> p k n", n=P)

                def project(j):
                    bank = 5 + j % 3
                    if j >= 3:
                        pe.wait_ge(proj_ev, l * N_PROJ + j - 2)
                    w = tile(j)
                    for k in range(KT):
                        if j == 0:
                            pe.wait_ge(h_done, l * KT + k + 1)
                        last = mm(PS[:, bank, 0:T], w[:, k, :], HT[:, k, :], start=(k == 0), stop=(k == KT - 1))
                    last.then_inc(proj_mm, 1)

                def project_wide(tiles):
                    for n in tiles:
                        g, a = divmod(n - 14, 3)
                        w = tile(n)
                        if a == 0:
                            pe.wait_ge(proj_ev, l * N_PROJ + 13 + 2 * g)
                        for t in range(TT):
                            for k in range(KT):
                                last = mm(PS[:, 5 + (14 + 2 * g + t) % 3, a * P:(a + 1) * P], HT[:, k, t * P:(t + 1) * P],
                                          w[:, k, :], start=(k == 0), stop=(k == KT - 1))
                            if a == 2:
                                last.then_inc(proj_mm, 1)
                        if a < 2:
                            last.then_inc(wide_mm, 1)

                def ssm_input(u):
                    if u:
                        pe.wait_ge(bu_ev, 2 * l + 1)
                    else:
                        pe.wait_ge(bt_done, l + 1)
                        pe.wait_ge(um_done, l + 1)
                    for im, bt in enumerate((BTRE, BTIM)):
                        for r in range(4):
                            o = im * 1024 + r * T
                            last = mm(ps[:, o:o + T], bt[:, u, :], UM[:, u, r, :], start=True, stop=True)
                    last.then_inc(bu_mm, 1)

                def ssm_output(u):
                    if u == 0:
                        pe.wait_ge(cf_done, l + 1)
                    pe.wait_ge(xs_done, 2 * l + u + 1)
                    for r in range(4):
                        mm(PS[:, 4, u * T:(u + 1) * T], CFRE[:, 4 * u + r, :], ZRE[:, r, :], start=(r == 0), stop=False)
                        last = mm(PS[:, 4, u * T:(u + 1) * T], CFIM[:, 4 * u + r, :], ZIM[:, r, :],
                                  start=False, stop=(r == 3))
                    last.then_inc(sy_mm, 1)

                for j in range(0, 3):
                    project(j)
                ssm_input(0)
                for j in range(3, 6):
                    project(j)
                ssm_input(1)
                project(6)
                ssm_output(0)
                for j in range(7, 12):
                    project(j)
                ssm_output(1)
                project(12)
                pe.wait_ge(sy_gelu, l + 1)
                for t in range(TT):
                    for k in range(2):
                        last = mm(PS[:, t, :], YG[:, k, t * P:(t + 1) * P], WGLU[:, k, :], start=(k == 0), stop=(k == 1))
                last.then_inc(glu_mm, 1)
                project(13)
                pe.wait_ge(in_perm, 16 * (l + 1))
                pe.wait_ge(proj_ev, l * N_PROJ + 8)
                pe.wait_ge(glu_read, l + 1)
                for a in range(6):
                    last = mm(ps[:, a * T:(a + 1) * T], MT[:, 0, 0:P], QK[:, a, :], start=True, stop=True)
                last.then_inc(rot_mm, 1)
                project_wide([14])
                pe.wait_ge(proj_ev, l * N_PROJ + 14)
                pe.wait_ge(rot_read, l + 1)
                for h in range(NH):
                    mm(ps[:, h * P:(h + 1) * P], QA[:, h % 2, h // 2, 0:P], KA[:, h // 2, 0:P], start=True, stop=True)
                for h in range(NH):
                    last = mm(ps[:, 768 + h * T:768 + (h + 1) * T], QA[:, h % 2, h // 2, P:T], KA[:, h // 2, :],
                              start=True, stop=True)
                last.then_inc(att_mm, 1)
                project_wide([15, 16, 17])
                pe.wait_ge(rot_done, l + 1)
                pe.wait_ge(att_in, l + 1)
                for h in range(NH):
                    mm(ps[:, h * T:(h + 1) * T], QK[:, 3 + h // 2, 0:P], QM[:, h % 2, h // 2, :], start=True, stop=True)
                for h in range(NH):
                    o = 1536 + h * P
                    last = mm(ps[:, o:o + P], QK[:, 3 + h // 2, P:T], QM[:, h % 2, h // 2, P:T], start=True, stop=True)
                last.then_inc(ret_mm, 1)

                project_wide([18, 19])
                pe.wait_ge(att_exp, l + 1)
                pe.wait_ge(ret_in, l + 1)
                for h in range(NH):
                    nc.tensor.transpose(ps[:, h * P:(h + 1) * P], SA[:, h, :], IDENT[:, :])
                for h in range(NH):
                    for b in range(2):
                        o = (6 + 2 * h + b) * P
                        last = nc.tensor.transpose(ps[:, o:o + P], SB[:, h, b * P:(b + 1) * P], IDENT[:, :])
                last.then_inc(pt_mm, 1)
                project_wide([20])
                pe.wait_ge(pt_ev, l + 1)
                pe.wait_ge(proj_ev, l * N_PROJ + 18)
                for h in range(NH):
                    mm(PS[:, 0, h * HD:(h + 1) * HD], SR0[:, h, 0:P], VR[:, 0, h * HD:(h + 1) * HD], start=True, stop=True)
                for h in range(NH):
                    o = PS[:, 1, h * HD:(h + 1) * HD]
                    mm(o, SR0[:, h, P:T], VR[:, 0, h * HD:(h + 1) * HD], start=True, stop=False)
                    last = mm(o, SR1[:, h, :], VR[:, 1, h * HD:(h + 1) * HD], start=False, stop=True)
                last.then_inc(ry_mm, 1)

                for h in range(NH):
                    mm(PS[:, 2, h * HD:(h + 1) * HD], PT[:, h, :], VA[:, 0, h * HD:(h + 1) * HD], start=True, stop=True)
                for h in range(NH):
                    o = PS[:, 3, h * HD:(h + 1) * HD]
                    mm(o, PT[:, 6 + 2 * h, :], VA[:, 0, h * HD:(h + 1) * HD], start=True, stop=False)
                    last = mm(o, PT[:, 7 + 2 * h, :], VA[:, 1, h * HD:(h + 1) * HD], start=False, stop=True)
                last.then_inc(ao_mm, 1)
                project_wide([21, 22])

                for part, ks in enumerate((MT_FIRST, MT_LAST)):
                    pe.wait_ge(merged, 2 * l + part + 1)
                    for k in ks:
                        for t in range(TT):
                            o = MT_AT[k] + t * P
                            last = nc.tensor.transpose(ps[:, o:o + P], MERGED[:, t, k * P:(k + 1) * P], IDENT[:, :])
                    last.then_inc(mt_mm, 1)
                pe.wait_ge(mt_ev, 2 * l + 2)
                for d in range(KT):
                    w = tile(TILE_OUT + d)
                    for k in range(KT):
                        last = mm(ps[:, d * T:(d + 1) * T], w[:, k, :], MT[:, k, :], start=(k == 0), stop=(k == KT - 1))
                    last.then_inc(wo_mm, 1)
                    if d == KT - 2:
                        sum_squares(2 * l + 1, range(4))
                sum_squares(2 * l + 1, range(4, KT))
                pe.wait_ge(in_sub, 16 * (l + 1))
                def key_scores(n):
                    g = l * 16 + n
                    pe.wait_ge(q_ev, g + 1)
                    if n >= 2:
                        pe.wait_ge(ks_ev, g - 1)
                    for t in range(TT):
                        last = mm(PS[:, 6 + n % 2, t * P:(t + 1) * P], QT[:, n % 2, t * P:(t + 1) * P],
                                  SUBT[:, n, :], start=True, stop=True)
                    last.then_inc(ks_mm, 1)
                for n in range(16):
                    pe.wait_ge(wq_split, l * 16 + n + 1)
                    if n >= 2:
                        pe.wait_ge(q_ev, l * 16 + n - 1)
                    for k in range(KT):
                        if n == 0:
                            pe.wait_ge(h_split, l * KT + k + 1)
                        b, out = n % 2, PS[:, 4 + n % 2, 0:T]
                        mm(out, WQH[:, b, k, :], HH[:, k, :], start=(k == 0), stop=False)
                        mm(out, WQH[:, b, k, :], HL[:, k, :], start=False, stop=False)
                        last = mm(out, WQL[:, b, k, :], HH[:, k, :], start=False, stop=(k == KT - 1))
                    last.then_inc(q_mm, 1)
                    if n:
                        key_scores(n - 1)
                key_scores(15)

                pe.wait_ge(ident_ready, 1)
                for side in range(2):
                    for j in range(TOPK):
                        if j % 4 == 0:
                            pe.wait_ge(pick_terms, l * 8 + side * 4 + j // 4 + 1)
                        for t in range(TT):
                            last = mm(PS[:, t, side * P:(side + 1) * P], PICKW[:, side, j, t, :], IDENTB[:, :], start=(j == 0),
                               stop=(j == TOPK - 1))
                    if side == 0:
                        pe.wait_ge(gates_ready, l + 1)
                        for t in range(TT):
                            nc.tensor.transpose(PS[:, t, 2 * P:3 * P], GATE[:, t, :], IDENT[:, :])
                last.then_inc(pickt_mm, 1)
                def gates(c, i):
                    if c in ACT_GROUPS:
                        pe.wait_ge(onehot_gated, i * 4 + (l * 32 + ACT_GROUPS.index(c) + 1))
                    else:
                        pe.wait_ge(onehot, i * 8 + (l * 64 + c + 1))
                    if c in POOL_GROUPS:
                        pe.wait_ge(key_onehot, i * KB + (l * 8 * KB + POOL_GROUPS.index(c) + 1))
                    for q in range(4):
                        last = mm(PS[:, c, q * P:(q + 1) * P], OHB[:, c, q, :], OHA[:, c, q, :], start=True, stop=True)
                    last.then_inc(w_mm, 1)
                pe.wait_ge(pickt, l + 1)
                for c in range(8):
                    gates(c, 0)
                with pe.Fori(1, 8) as i:
                    for c in range(8):
                        pe.wait_ge(w_ev, i * 8 + (l * 64 + c - 7))
                        gates(c, i)

                def scores(e, b, first):
                    pe.wait_ge(u_split, e + 1)
                    if not first:
                        pe.wait_ge(gelu_done, e - 1)
                    for k in range(KT):
                        mm(PS[:, 4 + b, 0:T], UH[:, b, k, :], HH[:, k, :], start=(k == 0), stop=False)
                        mm(PS[:, 4 + b, 0:T], UH[:, b, k, :], HL[:, k, :], start=False, stop=False)
                        last = mm(PS[:, 4 + b, 0:T], UL[:, b, k, :], HH[:, k, :], start=False, stop=(k == KT - 1))
                    last.then_inc(s_mm, 1)

                def add_experts(e, b, start=False, stop=False):
                    pe.wait_ge(v_split, e + 1)
                    pe.wait_ge(g_ready, e + 1)
                    for t in range(TT):
                        for n, (g, v) in enumerate(((GH, VH), (GH, VL), (GL, VH))):
                            for d in range(2):
                                last = mm(PS[:, 2 * t + d, :], g[:, t * P:(t + 1) * P], v[:, b, d * 512:(d + 1) * 512],
                                          start=start and n == 0, stop=stop and n == 2)
                    last.then_inc(v_used, 1)

                E0 = l * NE
                pe.wait_ge(w_ev, (l + 1) * 64)
                scores(E0, 0, True)
                scores(E0 + 1, 1, l == 0)
                add_experts(E0, 0, start=True)
                scores(E0 + 2, 0, False)
                add_experts(E0 + 1, 1)
                with pe.Fori(1, NE // 2 - 1) as i:
                    for b in (0, 1):
                        scores(i * 2 + (E0 + b + 1), 1 - b, False)
                        add_experts(i * 2 + (E0 + b), b)
                scores(E0 + NE - 1, 1, False)
                add_experts(E0 + NE - 2, 0)
                add_experts(E0 + NE - 1, 1, stop=True)
                pe.wait_ge(acc_ev, 2 * (l + 1))
                pe.wait_ge(in_const, 32 * (l + 2))
                for k in range(KT):
                    for t in range(TT):
                        o = 2048 + k * T + t * P
                        last = nc.tensor.transpose(ps[:, o:o + P], ACC[:, t, k * P:(k + 1) * P], IDENT[:, :])
                last.then_inc(acc_mm, 1)
            sum_squares(2 * L)

        @block.gpsimd
        def _(pool):
            nc.gpsimd.memset(ZERO4[:, :], 0.0).then_inc(zeros_ready, 1)
            pool.wait_ge(zeros_ready, 1)
            gp = nc.gpsimd
            steps = [0]

            def step(ins):
                steps[0] += 1
                ins.then_inc(pool_step, 1)
                pool.wait_ge(pool_step, steps[0])

            for l in range(L):
                pool.wait_ge(in_ssm, 80 * (l + 1))
                for n, bt in enumerate((BTRE, BTIM)):
                    for half in range(2):
                        last = gp.tensor_scalar(bt[:, :, half * STATES:(half + 1) * STATES], BRAW[:, n, :, :],
                                               MASK[:, half:half + 1], None, ALU.mult)
                last.then_inc(bt_done, 1)
                pool.wait_ge(f_done, l + 1)
                bc = lambda n: SV[:, n, :].unsqueeze(2).to_broadcast([P, ST, GCH])
                gp.memset(CFRE[:, :, :], 0.0)
                gp.memset(CFIM[:, :, :], 0.0)
                gp.tensor_tensor(CTMP[:, 0, :, :], CRAW[:, 0, :, :], bc(13), ALU.mult)
                gp.tensor_tensor(CTMP[:, 1, :, :], CRAW[:, 1, :, :], bc(14), ALU.mult)
                gp.tensor_tensor(CTMP[:, 2, :, :], CRAW[:, 0, :, :], bc(14), ALU.mult)
                step(gp.tensor_tensor(CTMP[:, 3, :, :], CRAW[:, 1, :, :], bc(13), ALU.mult))
                gp.tensor_tensor(CTMP[:, 0, :, :], CTMP[:, 0, :, :], CTMP[:, 1, :, :], ALU.subtract)
                step(gp.tensor_tensor(CTMP[:, 2, :, :], CTMP[:, 2, :, :], CTMP[:, 3, :, :], ALU.add))
                for n, (cf, sign) in enumerate(((CFRE, 1.0), (CFIM, -1.0))):
                    for g in range(2):
                        rows = slice(g * STATES, (g + 1) * STATES)
                        out = bass.AP(cf, g * STATES * ST * P + GCH * g, [[ST * P, STATES], [4 * P, 2], [P + 32, 4], [1, GCH]])
                        last = gp.tensor_scalar(out, CTMP[rows, 2 * n, :, :].rearrange("p (u r) c -> p u r c", r=4),
                                               sign, None, ALU.mult)
                last.then_inc(cf_done, 1)


                for n in range(16):
                    slot, _ = ring_pos(l, TILE_Q + n)
                    pool.wait_ge(wq_hi, l * 16 + n + 1)
                    gp.tensor_tensor(WQL[:, n % 2, :, :], RING[:, slot, :].rearrange("p (k n) -> p k n", n=P),
                                     WQH[:, n % 2, :, :].bitcast(F32), ALU.subtract).then_inc(wq_split, 1)

                def copy_keys(b, tok):
                    nc.gpsimd.tensor_tensor(KEY4[:, b, 0:4], SELT[:, 1, bass.ds(tok, 4)], ZERO4[:, :], ALU.add).then_inc(key_copied, 1)

                def key_onehots(b):
                    for q in range(4):
                        last = nc.gpsimd.tensor_scalar(OHB[:, POOL_GROUPS[b], q, :], IOTA[:, 0:P], KEY4[:, b, q:q + 1], None,
                                                       ALU.is_equal)
                    last.then_inc(key_onehot, 1)

                done = l * 8 * KB
                pool.wait_ge(pickt, l + 1)
                copy_keys(0, 0)
                for b in range(KB):
                    pool.wait_ge(key_copied, done + b + 1)
                    if b == KB - 1:
                        pool.wait_ge(key_onehot, done + 1)
                        copy_keys(0, 32)
                    else:
                        copy_keys(b + 1, 4 * POOL_GROUPS[b + 1])
                    key_onehots(b)
                with pool.Fori(1, 7) as i:
                    for b in range(KB):
                        pool.wait_ge(key_copied, i * KB + (done + b + 1))
                        pool.wait_ge(w_mm, i * 8 + (l * 64 + POOL_GROUPS[b] - 7))
                        if b == KB - 1:
                            pool.wait_ge(key_onehot, i * KB + (done + 1))
                            copy_keys(0, i * 32 + 32)
                        else:
                            pool.wait_ge(key_onehot, i * KB + (done + b + 2 - KB))
                            copy_keys(b + 1, i * 32 + 4 * POOL_GROUPS[b + 1])
                        key_onehots(b)
                for b in range(KB):
                    pool.wait_ge(key_copied, done + 7 * KB + b + 1)
                    pool.wait_ge(w_mm, l * 64 + 49 + POOL_GROUPS[b])
                    if b < KB - 1:
                        pool.wait_ge(key_onehot, done + 7 * KB + b + 2 - KB)
                        copy_keys(b + 1, 7 * 32 + 4 * POOL_GROUPS[b + 1])
                    key_onehots(b)

        @block.scalar
        def _(act):
            fn = nc.scalar.activation

            def w_q_high(l, n):
                slot, value = ring_pos(l, TILE_Q + n)
                act.wait_ge(in_ring[slot], value)
                fn(WQH[:, n % 2, :, :], RING[:, slot, :].rearrange("p (k n) -> p k n", n=P), ACT.Copy).then_inc(wq_hi, 1)

            def norm(n):
                for k in range(KT):
                    if n == 0:
                        act.wait_ge(in_x, 16)
                    else:
                        act.wait_ge(x_ready, (n - 1) * KT + k + 1)
                    fn(SQ[:, k, :], X[:, k, :], ACT.Square).then_inc(squared, 1)
                if n % 2:
                    w_q_high(n // 2, 1)
                act.wait_ge(var_done, n + 1)
                fn(RSTD[:, :], RSTD[:, :], ACT.Sqrt).then_inc(std_done, 1)

            def shift(n, which):
                for k in range(KT):
                    act.wait_ge(normed, n * KT + k + 1)
                    fn(HT[:, k, :], HT[:, k, :], ACT.Identity, bias=MOD[:, which, k:k + 1]).then_inc(h_done, 1)

            for l in range(L):
                if l == 0:
                    act.wait_ge(in_c, 16)
                    fn(CB[:, :], CB[:, :], ACT.Silu).then_inc(cond_done, 1)
                    act.wait_ge(in_cols, 48)
                norm(2 * l)
                shift(2 * l, SH1)
                fn(SV[:, 0, :], COLS[:, l, C_LDT:C_LDT + ST], ACT.Exp).then_inc(ssm_x, 1)
                act.wait_ge(ssm_e, l + 1)
                fn(SV[:, 2, :], SV[:, 1, :], ACT.Exp).then_inc(ssm_x, 1)
                act.wait_ge(ssm_a, 3 * l + 1)
                fn(SV[:, 6, :], SV[:, 5, :], ACT.Sin)
                fn(SV[:, 7, :], SV[:, 5, :], ACT.Sin, scale=0.5).then_inc(ssm_s, 1)

                place = ([(UT[:, a, :], 1.0) for a in range(2)] + [(QK[:, a, :], 1.0) for a in range(6)]
                         + [(QA[:, :, a, :], None) for a in range(3)] + [(KA[:, a, :], 1.0) for a in range(3)]
                         + [(o[:, t, :], 1.0) for o in (VA, VR, GR) for t in range(TT)])

                def taken(j):
                    o, scale = place[j]
                    act.wait_ge(proj_mm, l * N_PROJ + j + 1)
                    if scale is None:
                        for parity in range(2):
                            last = fn(o[:, parity, :], PS[:, 5 + j % 3, 0:T], ACT.Copy, scale=MASK[:, 6 + parity:7 + parity])
                        last.then_inc(proj_ev, 1)
                    else:
                        fn(o, PS[:, 5 + j % 3, 0:o.shape[-1]], ACT.Copy).then_inc(proj_ev, 1)

                def trig(u):
                    cos, sin = TRIG[u]
                    act.wait_ge(ssm_a, 3 * l + 2 + u)
                    fn(cos[:, :, :], sin[:, :, :], ACT.Sin, scale=0.5).then_inc(act_step, 1)
                    act.wait_ge(act_step, 4 * l + 2 * u + 1)
                    fn(sin[:, :, :], sin[:, :, :], ACT.Sin)
                    fn(cos[:, :, :], cos[:, :, :], ACT.Square).then_inc(act_step, 1)
                    act.wait_ge(act_step, 4 * l + 2 * u + 2)
                    fn(cos[:, :, :], cos[:, :, :], ACT.Copy, scale=-2.0, bias=1.0).then_inc(ssm_s, 1)

                for j in range(2):
                    taken(j)
                act.wait_ge(proj_ev, l * N_PROJ + 2)
                for u in range(2):
                    for r in range(4):
                        last = fn(UM[:, u, r, :], UT[:, u, :], ACT.Copy, scale=MASK[:, 2 + r:3 + r])
                last.then_inc(um_done, 1)
                trig(0)
                taken(2)
                taken(3)
                trig(1)
                for j in range(4, 12):
                    taken(j)
                act.wait_ge(sy_in, l + 1)
                fn(YG[:, :, :], YG[:, :, :], ACT.Gelu_apprx_tanh).then_inc(sy_gelu, 1)
                taken(12)
                act.wait_ge(glu_mm, l + 1)
                fn(ZG[:, :, :], PS[:, 0:2, SW:2 * SW], ACT.Sigmoid).then_inc(glu_gate, 1)
                for j in range(13, 16):
                    taken(j)
                act.wait_ge(att_sub, l + 1)
                fn(SAB[:, :], SAB[:, :], ACT.Exp).then_inc(att_exp, 1)
                taken(16)
                taken(17)
                act.wait_ge(pt_mm, l + 1)
                fn(PT[:, :, :], ps[:, 0:18 * P].rearrange("p (n k) -> p n k", k=P), ACT.Copy).then_inc(pt_ev, 1)
                act.wait_ge(rvar, l + 1)
                fn(SM[:, 3, :], SM[:, 3, :], ACT.Sqrt).then_inc(rstd_done, 1)
                act.wait_ge(mvar, l + 1)
                fn(RMS[:, :], RMS[:, :], ACT.Sqrt).then_inc(mstd, 1)
                for j in range(18, N_PROJ):
                    act.wait_ge(proj_mm, l * N_PROJ + j + 1)
                    fn(GR[:, j - 18, :], PS[:, 5 + j % 3, 0:AW], ACT.Silu).then_inc(proj_ev, 1)
                for part, ks in enumerate((MT_FIRST, MT_LAST)):
                    act.wait_ge(mt_mm, 2 * l + part + 1)
                    for k in ks:
                        last = fn(MT[:, k, :], ps[:, MT_AT[k]:MT_AT[k] + T], ACT.Copy,
                                  scale=COLS[:, l, C_GAIN + k:C_GAIN + k + 1])
                    last.then_inc(mt_ev, 1)

                w_q_high(l, 0)
                norm(2 * l + 1)
                for k in range(KT):
                    act.wait_ge(normed, (2 * l + 1) * KT + k + 1)
                    fn(HH[:, k, :], HT[:, k, :], ACT.Identity, bias=MOD[:, SH2, k:k + 1]).then_inc(h_hi, 1)
                for n in range(16):
                    act.wait_ge(q_mm, l * 16 + n + 1)
                    if n >= 2:
                        act.wait_ge(ks_mm, l * 16 + n - 1)
                    fn(QT[:, n % 2, :], PS[:, 4 + n % 2, 0:T], ACT.Copy).then_inc(q_ev, 1)
                    if n + 2 < 16:
                        w_q_high(l, n + 2)
                act.wait_ge(gate_in, l + 1)
                fn(GATE[:, :, :], GATE[:, :, :], ACT.Exp).then_inc(gate_exp, 1)
                act.wait_ge(pickt_mm, l + 1)
                fn(SELT[:, :, :].rearrange("p a (t k) -> p a t k", t=TT), PS[:, 0:TT, 0:3 * P].rearrange("p t (a k) -> p a t k", a=3),
                   ACT.Copy).then_inc(pickt, 1)

                def apply_gates(c, i, tok):
                    act.wait_ge(onehot, i * 8 + (l * 64 + c + 1))
                    for q in range(4):
                        last = fn(OHA[:, c, q, :], OHA[:, c, q, :], ACT.Copy, scale=SELT[:, 2, bass.ds(tok + q, 1)])
                    last.then_inc(onehot_gated, 1)

                def gates(c, i, tok):
                    act.wait_ge(w_mm, i * 8 + (l * 64 + c + 1))
                    fn(WT[:, :, bass.ds(tok, 4)], PS[:, c, :].rearrange("p (t i) -> p i t", t=4),
                       ACT.Copy).then_inc(w_ev, 1)

                act.wait_ge(pickt, l + 1)
                for c in range(8 + LAG):
                    if c in ACT_GROUPS:
                        apply_gates(c, 0, 4 * c)
                    if c >= LAG:
                        gates(c - LAG, 0, 4 * (c - LAG))
                with act.Fori(1, 8) as i:
                    for c in range(8 + LAG):
                        if c in ACT_GROUPS:
                            apply_gates(c, i, i * 32 + 4 * c)
                        if c >= LAG:
                            gates(c - LAG, i, i * 32 + 4 * (c - LAG))

                E0 = l * NE

                def u_high(e, b, i):
                    slot, n = expert_pos(l, 0, b)
                    act.wait_ge(in_ring[slot], i * 16 + n * 16)
                    return fn(UH[:, b, :, :], RING[:, slot, :].rearrange("p (k n) -> p k n", n=P), ACT.Copy).then_inc(u_hi, 1)

                def v_high(e, b, i):
                    slot, n = expert_pos(l, 1, b)
                    act.wait_ge(in_ring[slot], i * 16 + n * 16)
                    return fn(VH[:, b, :], RING[:, slot, :], ACT.Copy).then_inc(v_hi, 1)

                def gelu(e, b):
                    act.wait_ge(s_mm, e + 1)
                    return fn(GE[:, b, :], PS[:, 4 + b, 0:T], ACT.Gelu_apprx_tanh).then_inc(gelu_done, 1)

                u_high(E0, 0, 0)
                for e in (0, 1):
                    if e == 1:
                        act.wait_ge(s_mm, E0 + 1)
                    u_high(E0 + e + 1, (e + 1) % 2, (e + 1) // 2)
                    v_high(E0 + e, e, 0)
                    gelu(E0 + e, e)
                def expert_tiles(start, stop):
                    with act.Fori(start // 2, stop // 2) as i:
                        for b in (0, 1):
                            act.wait_ge(s_mm, i * 2 + (E0 + b))
                            u_high(i * 2 + (E0 + b + 1), 1 - b, i + b)
                            act.wait_ge(v_used, i * 2 + (E0 + b - 1))
                            v_high(i * 2 + (E0 + b), b, i)
                            act.wait_ge(g_ready, i * 2 + (E0 + b - 1))
                            gelu(i * 2 + (E0 + b), b)
                if l < L - 1:
                    expert_tiles(2, COND_TILE)
                    act.wait_ge(in_c, 16 * (l + 2))
                    fn(CB[:, :], CB[:, :], ACT.Silu).then_inc(cond_done, 1)
                    expert_tiles(COND_TILE, NE - 2)
                else:
                    expert_tiles(2, NE - 2)
                for e in (NE - 2, NE - 1):
                    if e < NE - 1:
                        act.wait_ge(s_mm, E0 + e)
                        u_high(E0 + e + 1, 1, NE // 2 - 1)
                    act.wait_ge(v_used, E0 + e - 1)
                    v_high(E0 + e, e % 2, NE // 2 - 1)
                    act.wait_ge(g_ready, E0 + e - 1)
                    gelu(E0 + e, e % 2)
                act.wait_ge(v_used, E0 + NE)
                fn(ACC[:, 0, :], ps[:, 0:D], ACT.Copy).then_inc(acc_ev, 1)
            norm(2 * L)

        @block.vector
        def _(dve):
            v = nc.vector
            steps = [0]

            def link(ins):
                steps[0] += 1
                ins.then_inc(dve_step, 1)
                dve.wait_ge(dve_step, steps[0])

            def rms(n):
                dve.wait_ge(sumsq, n + 1)
                v.tensor_scalar(RSTD[:, :], PS[:, 4 * (n % 2), 0:T], 1.0 / D, EPS, ALU.mult, ALU.add).then_inc(var_done, 1)
                dve.wait_ge(std_done, n + 1)
                link(v.reciprocal(RSTD[:, :], RSTD[:, :]))

            def norm(gain, behind=None):
                for k in range(KT):
                    v.scalar_tensor_tensor(HT[:, k, :], X[:, k, :], gain[:, k:k + 1], RSTD[:, :], ALU.mult,
                                           ALU.mult).then_inc(normed, 1)
                    if behind and k >= 2:
                        behind(k - 2)
                if behind:
                    dve.wait_ge(normed, (2 * l + 2) * KT)
                    behind(KT - 2)
                    behind(KT - 1)

            def wrap(out, x, k):
                link(v.tensor_scalar(k, x, 1.0 / (2 * math.pi), ROUND, ALU.mult, ALU.add))
                link(v.tensor_scalar(k, k, ROUND, None, ALU.subtract))
                link(v.scalar_tensor_tensor(out, k, -TWO_PI_HI, x, ALU.mult, ALU.add))
                link(v.scalar_tensor_tensor(out, k, -TWO_PI_LO, out, ALU.mult, ALU.add))
                return v.tensor_scalar(out, out, PI, -PI, ALU.min, ALU.max)

            def top16(rows, taken=None):
                wrote = {}

                def stage(r, ins):
                    steps[0] += 1
                    wrote[r] = (dve_step, steps[0])
                    ins.then_inc(dve_step, 1)

                for half in range(2):
                    o = slice(8 * half, 8 * half + 8)
                    for r, row in enumerate(rows):
                        if half:
                            dve.wait_ge(*wrote[r])
                        stage(r, v.max(row[2][:, o], row[half]))
                    for r, row in enumerate(rows):
                        dve.wait_ge(*wrote[r])
                        stage(r, v.max_index(row[3][:, o], row[2][:, o], row[half]))
                    if half == 0:
                        for r, (src, rest, vals, _) in enumerate(rows):
                            dve.wait_ge(*wrote[r])
                            ins = v.match_replace(rest, vals[:, o], src, -3.0e38)
                            if taken and r == len(rows) - 1:
                                ins.then_inc(taken[0], 1)
                                wrote[r] = taken
                            else:
                                stage(r, ins)
                dve.wait_ge(dve_step, steps[0])

            v.memset(ONES[:, :], 1.0).then_inc(ones_ready, 1)
            for l in range(L):
                dve.wait_ge(cond_done, l + 1)

                def ada(i):
                    for j in range(8):
                        dve.wait_ge(in_ada[j], i * 16 + (l * 6 + 1) * 16)
                        v.tensor_tensor_reduce(out=ADA[:, j, :], in0=ADA[:, j, :], in1=CB[:, :], scale=1.0, scalar=0.0,
                                               op0=ALU.mult, op1=ALU.add, accum_out=ADA8[:, j:j + 1]).then_inc(ada_used, 1)
                    dve.wait_ge(ada_used, i * 8 + (l * 48 + 8))
                    v.tensor_tensor(MOD[:, i, :], ADA8[:, :], COLS[:, l, bass.ds(i * 8, 8)], ALU.add).then_inc(mod_done, 1)
                    dve.wait_ge(mod_done, i + (l * 6 + 1))
                if l == 0:
                    dve.wait_ge(in_cols, 48)
                    ada(0)
                    rms(0)
                    ada(1)
                else:
                    rms(2 * l)
                link(v.scalar_tensor_tensor(AMP[:, :], MOD[:, SC1, :], 1.0, COLS[:, l, C_NMIX:C_NMIX + KT],
                                            ALU.add, ALU.mult))
                norm(AMP)
                lre, lim = (COLS[:, l, o:o + ST] for o in (C_LRE, C_LIM))
                sv = lambda n: SV[:, n, :]
                dve.wait_ge(ssm_x, 2 * l + 1)
                v.tensor_tensor(sv(1), lre, sv(0), ALU.mult).then_inc(ssm_e, 1)
                link(v.tensor_tensor(sv(3), lim, sv(0), ALU.mult))
                wrap(sv(5), sv(3), sv(4)).then_inc(ssm_a, 1)

                if l == 0:
                    dve.wait_ge(in_const, 32)
                    v.tensor_copy(IDENTB[:, :], IDENT[:, :]).then_inc(ident_ready, 1)
                dve.wait_ge(ssm_a, 3 * l + 1)
                for u in range(2):
                    link(v.tensor_tensor(TB[:, :, :], IOTA[:, :].unsqueeze(1).to_broadcast([P, 4, T]),
                                         SV[:, 5, 4 * u:4 * u + 4].unsqueeze(2).to_broadcast([P, 4, T]), ALU.mult))
                    wrap(TRIG[u][1][:, :, :], TB[:, :, :], TURNS[:, :, :]).then_inc(ssm_a, 1)
                    dve.wait_ge(ssm_a, 3 * l + 2 + u)
                    if u == 0:
                        dve.wait_ge(ssm_x, 2 * l + 2)
                        dve.wait_ge(ssm_s, 3 * l + 1)
                        link(v.tensor_tensor(sv(8), sv(7), sv(7), ALU.mult))
                        link(v.tensor_scalar(sv(8), sv(8), -2.0, 1.0, ALU.mult, ALU.add))
                        link(v.tensor_tensor(sv(8), sv(8), sv(2), ALU.mult))
                        link(v.tensor_scalar(sv(8), sv(8), 1.0, None, ALU.subtract))
                        link(v.tensor_tensor(sv(9), sv(6), sv(2), ALU.mult))
                        link(v.tensor_tensor(sv(10), lre, lre, ALU.mult))
                        link(v.tensor_tensor(sv(11), lim, lim, ALU.mult))
                        link(v.tensor_tensor(sv(10), sv(10), sv(11), ALU.add))
                        link(v.reciprocal(sv(10), sv(10)))
                        link(v.tensor_tensor(sv(11), sv(8), lre, ALU.mult))
                        link(v.tensor_tensor(sv(12), sv(9), lim, ALU.mult))
                        link(v.tensor_tensor(sv(11), sv(11), sv(12), ALU.add))
                        link(v.tensor_tensor(sv(13), sv(11), sv(10), ALU.mult))
                        link(v.tensor_tensor(sv(11), sv(9), lre, ALU.mult))
                        link(v.tensor_tensor(sv(12), sv(8), lim, ALU.mult))
                        link(v.tensor_tensor(sv(11), sv(11), sv(12), ALU.subtract))
                        v.tensor_tensor(sv(14), sv(11), sv(10), ALU.mult).then_inc(f_done, 1)
                for u in range(2):
                    COS, SIN = TRIG[u]
                    dve.wait_ge(ssm_s, 3 * l + 2 + u)
                    dve.wait_ge(bu_mm, 2 * l + u + 1)
                    bre = ps[:, 0:1024].rearrange("p (r t) -> p r t", t=T)
                    bim = ps[:, 1024:2048].rearrange("p (r t) -> p r t", t=T)
                    if u:
                        dve.wait_ge(sy_mm, 2 * l + 1)
                    v.tensor_tensor(TA[:, :, :], COS[:, :, :], bre, ALU.mult)
                    link(v.tensor_tensor(TB[:, :, :], SIN[:, :, :], bim, ALU.mult))
                    link(v.tensor_tensor(ZRE[:, :, :], TA[:, :, :], TB[:, :, :], ALU.add))
                    v.tensor_tensor(TA[:, :, :], COS[:, :, :], bim, ALU.mult)
                    link(v.tensor_tensor(TB[:, :, :], SIN[:, :, :], bre, ALU.mult))
                    v.tensor_tensor(ZIM[:, :, :], TA[:, :, :], TB[:, :, :], ALU.subtract).then_inc(bu_ev, 1)
                    dve.wait_ge(bu_ev, 2 * l + u + 1)
                    for r in range(4):
                        mag = SV[:, 2, 4 * u + r:4 * u + r + 1].to_broadcast([P, T])
                        v.tensor_tensor_scan(ZRE[:, r, :], mag, ZRE[:, r, :], 0.0, ALU.mult, ALU.add)
                        last = v.tensor_tensor_scan(ZIM[:, r, :], mag, ZIM[:, r, :], 0.0, ALU.mult, ALU.add)
                    link(last)
                    v.tensor_tensor(TA[:, :, :], COS[:, :, :], ZRE[:, :, :], ALU.mult)
                    v.tensor_tensor(TB[:, :, :], SIN[:, :, :], ZIM[:, :, :], ALU.mult)
                    v.tensor_tensor(COS[:, :, :], COS[:, :, :], ZIM[:, :, :], ALU.mult)
                    link(v.tensor_tensor(SIN[:, :, :], SIN[:, :, :], ZRE[:, :, :], ALU.mult))
                    v.tensor_tensor(ZRE[:, :, :], TA[:, :, :], TB[:, :, :], ALU.subtract)
                    v.tensor_tensor(ZIM[:, :, :], COS[:, :, :], SIN[:, :, :], ALU.add).then_inc(xs_done, 1)
                    dve.wait_ge(xs_done, 2 * l + u + 1)
                dve.wait_ge(sy_mm, 2 * l + 2)
                for u in range(2):
                    last = v.scalar_tensor_tensor(YG[:, u, :], UT[:, u, :], COLS[:, l, C_D + u:C_D + u + 1],
                                                  PS[:, 4, u * T:(u + 1) * T], ALU.mult, ALU.add)
                last.then_inc(sy_in, 1)
                ada(2)
                dve.wait_ge(glu_gate, l + 1)
                v.tensor_tensor(ZG[:, :, :], PS[:, 0:2, 0:SW], ZG[:, :, :], ALU.mult).then_inc(glu_read, 1)
                dve.wait_ge(glu_read, l + 1)
                for t in range(TT):
                    link(v.tensor_tensor_reduce(out=SCR[:, 0:SW], in0=ZG[:, t, :], in1=ZG[:, t, :],
                                                scale=1.0, scalar=0.0, op0=ALU.mult, op1=ALU.add,
                                                accum_out=RMS[:, 2 + t:3 + t]))

                dve.wait_ge(in_mix, 64 * (l + 1))
                dve.wait_ge(rot_mm, l + 1)
                v.tensor_tensor(ROT[:, :, :], ps[:, 0:1536].rearrange("p (a t) -> p a t", t=T),
                                ROPE[:, 1, :].unsqueeze(1).to_broadcast([P, 6, T]), ALU.mult).then_inc(rot_read, 1)
                link(v.tensor_tensor(QK[:, :, :], QK[:, :, :], ROPE[:, 0, :].unsqueeze(1).to_broadcast([P, 6, T]), ALU.mult))
                link(v.tensor_tensor(QK[:, :, :], QK[:, :, :], ROT[:, :, :], ALU.add))
                for parity in range(2):
                    last = v.tensor_scalar(QM[:, parity, :, :], QK[:, 0:3, :], MASK[:, 8 + parity:9 + parity], None, ALU.mult)
                last.then_inc(rot_done, 1)

                dve.wait_ge(att_mm, l + 1)
                v.tensor_tensor(SA[:, :, :], ps[:, 0:768].rearrange("p (h t) -> p h t", h=NH),
                                bass.AP(BIAS, P - 1, [[NH * T, P], [T, NH], [-1, P]]), ALU.add)
                link(v.tensor_tensor(SB[:, :, :], ps[:, 768:2304].rearrange("p (h t) -> p h t", h=NH),
                                     bass.AP(BIAS, T - 1, [[NH * T, P], [T, NH], [-1, T]]), ALU.add))
                v.memset(SA[0:CHUNK, :, CHUNK:P], NEG)
                link(v.memset(SB[0:CHUNK, :, T - CHUNK:T], NEG))
                v.reduce_max(SM[:, 0, 0:NH], SA[:, :, :], AX.X).then_inc(att_in, 1)
                link(v.reduce_max(SM[:, 0, NH:12], SB[:, :, :], AX.X))
                v.tensor_tensor(SA[:, :, :], SA[:, :, :], SM[:, 0, 0:NH].unsqueeze(2).to_broadcast([P, NH, P]), ALU.subtract)
                v.tensor_tensor(SB[:, :, :], SB[:, :, :], SM[:, 0, NH:12].unsqueeze(2).to_broadcast([P, NH, T]),
                                ALU.subtract).then_inc(att_sub, 1)

                dve.wait_ge(ret_mm, l + 1)
                v.tensor_tensor(SR0[:, :, :], ps[:, 0:1536].rearrange("p (h t) -> p h t", h=NH), DEC0[:, :, :], ALU.mult)
                v.tensor_tensor(SR1[:, :, :], ps[:, 1536:2304].rearrange("p (h t) -> p h t", h=NH), DEC1[:, :, :],
                                ALU.mult).then_inc(ret_in, 1)
                dve.wait_ge(att_exp, l + 1)
                v.reduce_sum(SM[:, 1, 0:NH], SA[:, :, :], AX.X)
                link(v.reduce_sum(SM[:, 1, NH:12], SB[:, :, :], AX.X))
                link(v.reciprocal(SM[:, 1, :], SM[:, 1, :]))

                ada(3)

                yr = YR[:, :, :].rearrange("p t (h e) -> p (t h) e", e=HD)
                dve.wait_ge(ry_mm, l + 1)
                link(v.tensor_copy(YR[:, :, :], PS[:, 0:2, 0:AW]))
                link(v.reduce_sum(SM[:, 2, :], yr, AX.X))
                link(v.tensor_scalar(SM[:, 2, :], SM[:, 2, :], -1.0 / HD, None, ALU.mult))
                link(v.tensor_tensor(yr, yr, SM[:, 2, :].unsqueeze(2).to_broadcast([P, 12, HD]), ALU.add))
                link(v.tensor_tensor(YSQ, yr, yr, ALU.mult))
                link(v.reduce_sum(SM[:, 3, :], YSQ, AX.X))
                v.tensor_scalar(SM[:, 3, :], SM[:, 3, :], 1.0 / HD, EPS, ALU.mult, ALU.add).then_inc(rvar, 1)

                dve.wait_ge(ao_mm, l + 1)
                for t in range(TT):
                    last = v.tensor_tensor(MERGED[:, t, 0:AW].rearrange("p (h e) -> p h e", e=HD),
                                           PS[:, 2 + t, 0:AW].rearrange("p (h e) -> p h e", e=HD),
                                           SM[:, 1, t * NH:(t + 1) * NH].unsqueeze(2).to_broadcast([P, NH, HD]), ALU.mult)
                link(last)
                for t in range(TT):
                    link(v.tensor_tensor_reduce(out=SCR[:, 0:AW], in0=MERGED[:, t, 0:AW], in1=MERGED[:, t, 0:AW],
                                                scale=1.0, scalar=0.0, op0=ALU.mult, op1=ALU.add,
                                                accum_out=RMS[:, t:t + 1]))
                v.tensor_scalar(RMS[:, 2:4], RMS[:, 2:4], 1.0 / SW, EPS, ALU.mult, ALU.add)
                v.tensor_scalar(RMS[:, 0:2], RMS[:, 0:2], 1.0 / AW, EPS, ALU.mult, ALU.add).then_inc(mvar, 1)
                dve.wait_ge(rstd_done, l + 1)
                link(v.reciprocal(SM[:, 3, :], SM[:, 3, :]))
                dve.wait_ge(mstd, l + 1)
                link(v.reciprocal(RMS[:, :], RMS[:, :]))
                for t in range(TT):
                    v.tensor_scalar(MERGED[:, t, 2 * AW:D], ZG[:, t, :], RMS[:, 2 + t:3 + t], None, ALU.mult)
                    last = v.tensor_scalar(MERGED[:, t, 0:AW], MERGED[:, t, 0:AW], RMS[:, t:t + 1], None, ALU.mult)
                last.then_inc(merged, 1)
                link(v.tensor_tensor(yr, yr, SM[:, 3, :].unsqueeze(2).to_broadcast([P, 12, HD]), ALU.mult))
                dve.wait_ge(proj_ev, (l + 1) * N_PROJ)
                v.tensor_tensor(MERGED[:, :, AW:2 * AW], YR[:, :, :], GR[:, :, :], ALU.mult).then_inc(merged, 1)

                with dve.Fori(4, 6) as i:
                    ada(i)
                link(v.scalar_tensor_tensor(AMP[:, :], MOD[:, SC2, :], 1.0, COLS[:, l, C_NFFN:C_NFFN + KT],
                                            ALU.add, ALU.mult))
                for d in range(KT):
                    dve.wait_ge(wo_mm, l * KT + d // 2 * 2 + 2)
                    v.scalar_tensor_tensor(X[:, d, :], ps[:, d * T:(d + 1) * T], MOD[:, G1, d:d + 1], X[:, d, :],
                                           ALU.mult, ALU.add).then_inc(x_ready, 1)
                dve.wait_ge(x_ready, (2 * l + 1) * KT)
                rms(2 * l + 1)

                def h_low(k):
                    dve.wait_ge(h_hi, l * KT + k + 1)
                    v.scalar_tensor_tensor(HL[:, k, :], HT[:, k, :], MOD[:, SH2, k:k + 1], HH[:, k, :].bitcast(F32), ALU.add,
                                           ALU.subtract).then_inc(h_split, 1)
                norm(AMP, h_low)

                def pairs(m):
                    h, t = m // 2, m % 2
                    cand = CAND[:, t, :, :]
                    for i0, i1, w, o in PAIRS:
                        shape = [P, i1 - i0, w]
                        last = v.tensor_tensor(cand[:, 0, o:o + (i1 - i0) * w].rearrange("p (i j) -> p i j", j=w),
                                               V16[:, t, 2 * h, i0:i1].unsqueeze(2).to_broadcast(shape),
                                               V16[:, t, 2 * h + 1, 0:w].unsqueeze(1).to_broadcast(shape), ALU.add)
                    return last, (cand[:, 0, :], cand[:, 1, :], BEST[:, t, h, :], POS[:, t, h, :])

                for n in range(16):
                    rows = []
                    if n >= 2:
                        last, row = pairs(n - 2)
                        link(last)
                        rows.append(row)
                    dve.wait_ge(ks_mm, l * 16 + n + 1)
                    for t in range(TT):
                        rows.append((PS[:, 6 + n % 2, t * P:(t + 1) * P], KS[:, t, n, :], V16[:, t, n, :], I16[:, t, n, :]))
                    top16(rows, (ks_ev, l * 16 + n + 1))
                rows = []
                for m in (14, 15):
                    last, row = pairs(m)
                    rows.append(row)
                link(last)
                top16(rows)
                gate = GATE[:, :, :].rearrange("p t (h k) -> p t h k", h=PH)
                for t in range(TT):
                    last = v.tensor_tensor(gate[:, t], BEST[:, t, :, :], BEST[:, t, :, 0:1].to_broadcast([P, PH, TOPK]), ALU.subtract)
                last.then_inc(gate_in, 1)
                flat = lambda a: a[:, :, :, :].rearrange("p t h k -> p (t h k)")
                pos, past, row, col, count = flat(PF), flat(PM), flat(AF), flat(BF), COUNT[:, :]
                v.tensor_copy(I16F[:, :, :, :], I16[:, :, :, :])
                link(v.tensor_copy(PF[:, :, :, :], POS[:, :, :, :]))
                link(v.tensor_scalar(past, pos, 64.0, 0.0, ALU.subtract, ALU.max))
                v.tensor_copy(row, past)
                link(v.tensor_tensor(col, pos, past, ALU.subtract))
                for width, starts in ((16, (16, 32)), (8, (40, 48)), (4, (52, 56, 60, 64))):
                    link(v.tensor_scalar(count, pos, float(starts[0]), None, ALU.is_ge))
                    for start in starts[1:]:
                        link(v.scalar_tensor_tensor(count, pos, float(start), count, ALU.is_ge, ALU.add))
                    v.tensor_tensor(row, row, count, ALU.add)
                    link(v.scalar_tensor_tensor(col, count, -float(width), col, ALU.mult, ALU.add))
                keys = I16F[:, :, :, :].rearrange("p t (h s) a -> p t h s a", s=2)
                for side, rank in enumerate((AF, BF)):
                    if side == 1:
                        dve.wait_ge(gate_exp, l + 1)
                        link(v.reduce_sum(GSUM[:, :, :], gate, AX.X))
                        link(v.reciprocal(GSUM[:, :, :], GSUM[:, :, :]))
                        for t in range(TT):
                            last = v.tensor_tensor(gate[:, t], gate[:, t], GSUM[:, t, :].unsqueeze(2).to_broadcast([P, PH, TOPK]), ALU.mult)
                        last.then_inc(gates_ready, 1)
                    for j in range(TOPK):
                        last = v.scalar_tensor_tensor(PICKW[:, side, j, :, :].rearrange("p t (h k) -> p t h k", h=PH),
                                                      rank[:, :, :, :], float(j),
                                                      keys[:, :, :, side, j].unsqueeze(3).to_broadcast([P, TT, PH, TOPK]),
                                                      ALU.is_equal, ALU.mult)
                        if j % 4 == 3:
                            last.then_inc(pick_terms, 1)
                dve.wait_ge(pickt, l + 1)

                def onehots(c, tok):
                    wide = lambda a: (IOTA[:, 0:P].unsqueeze(1).to_broadcast([P, 4, P]),
                                      SELT[:, a, bass.ds(tok, 4)].unsqueeze(2).to_broadcast([P, 4, P]), ALU.is_equal)
                    if c not in POOL_GROUPS:
                        v.tensor_tensor(OHB[:, c, :, :], *wide(1))
                    if c in ACT_GROUPS:
                        v.tensor_tensor(OHA[:, c, :, :], *wide(0)).then_inc(onehot, 1)
                    else:
                        for q in range(4):
                            one = lambda a: SELT[:, a, bass.ds(tok + q, 1)]
                            last = v.tensor_scalar(OHA[:, c, q, :], IOTA[:, 0:P], one(0), one(2), ALU.is_equal, ALU.mult)
                        last.then_inc(onehot, 1)
                for c in range(8):
                    onehots(c, 4 * c)
                with dve.Fori(1, 8) as i:
                    for c in range(8):
                        dve.wait_ge(w_mm, i * 8 + (l * 64 + c - 7))
                        onehots(c, i * 32 + 4 * c)

                E0 = l * NE

                def u_low(e, b):
                    dve.wait_ge(u_hi, e + 1)
                    v.tensor_tensor(UL[:, b, :, :], RING[:, b, :].rearrange("p (k n) -> p k n", n=P),
                                    UH[:, b, :, :].bitcast(F32), ALU.subtract).then_inc(u_split, 1)

                def v_low(e, b):
                    dve.wait_ge(v_hi, e + 1)
                    v.tensor_tensor(VL[:, b, :], RING[:, 2 + b, :], VH[:, b, :].bitcast(F32), ALU.subtract).then_inc(v_split, 1)

                def gated(e, b, i, first=False):
                    dve.wait_ge(gelu_done, e + 1)
                    if not first:
                        dve.wait_ge(g_ready, e)
                    v.tensor_tensor(G32[:, :], GE[:, b, :], WT[:, i, :], ALU.mult).then_inc(g_prod, 1)
                    dve.wait_ge(g_prod, e + 1)
                    if not first:
                        dve.wait_ge(v_used, e)
                    v.tensor_copy(GH[:, :], G32[:, :]).then_inc(g_hi, 1)
                    dve.wait_ge(g_hi, e + 1)
                    v.tensor_tensor(GL[:, :], G32[:, :], GH[:, :].bitcast(F32), ALU.subtract).then_inc(g_ready, 1)

                dve.wait_ge(w_ev, (l + 1) * 64)
                u_low(E0, 0)
                for e in (0, 1):
                    u_low(E0 + e + 1, (e + 1) % 2)
                    v_low(E0 + e, e)
                    gated(E0 + e, e, e, first=(e == 0))
                def expert_tiles(start, stop):
                    with dve.Fori(start // 2, stop // 2) as i:
                        for b in (0, 1):
                            u_low(i * 2 + (E0 + b + 1), 1 - b)
                            v_low(i * 2 + (E0 + b), b)
                            gated(i * 2 + (E0 + b), b, i * 2 + b)
                if l == L - 1:
                    expert_tiles(2, NE - 2)
                else:
                    expert_tiles(2, ADA_TILE)
                    dve.wait_ge(cond_done, l + 2)
                    with dve.Fori(0, 2) as i:
                        for j in range(8):
                            e = i * 8 + (E0 + ADA_TILE + j)
                            u_low(e + 1, (j + 1) % 2)
                            v_low(e, j % 2)
                            gated(e, j % 2, i * 8 + (ADA_TILE + j))
                            dve.wait_ge(in_ada[j], i * 16 + ((l + 1) * 6 + 1) * 16)
                            v.tensor_tensor_reduce(out=ADAN[:, j % 4, :], in0=ADAN[:, j % 4, :], in1=CB[:, :], scale=1.0,
                                                   scalar=0.0, op0=ALU.mult, op1=ALU.add,
                                                   accum_out=ADA8[:, j:j + 1]).then_inc(ada_used, 1)
                        dve.wait_ge(ada_used, i * 8 + ((l + 1) * 48 + 8))
                        v.tensor_tensor(MOD[:, i, :], ADA8[:, :], COLS[:, l + 1, bass.ds(i * 8, 8)], ALU.add).then_inc(mod_done, 1)
                        dve.wait_ge(mod_done, i + ((l + 1) * 6 + 1))
                    assert ADA_TILE + 16 == NE - 2
                u_low(E0 + NE - 1, 1)
                for e in (NE - 2, NE - 1):
                    v_low(E0 + e, e % 2)
                    gated(E0 + e, e % 2, e)
                dve.wait_ge(v_used, E0 + NE)
                v.tensor_copy(ACC[:, 1, :], ps[:, D:2 * D]).then_inc(acc_ev, 1)
                v.memset(ONES[:, :], 1.0).then_inc(ones_ready, 1)
                dve.wait_ge(acc_mm, l + 1)
                for k in range(KT):
                    v.scalar_tensor_tensor(X[:, k, :], ps[:, 2048 + k * T:2048 + (k + 1) * T], MOD[:, G2, k:k + 1],
                                           X[:, k, :], ALU.mult, ALU.add).then_inc(x_ready, 1)
                dve.wait_ge(x_ready, (2 * l + 2) * KT)
            rms(2 * L)
            norm(FCOL)


def _tables():
    inv = np.float32(10000.0) ** (-np.arange(32, dtype=np.float32) / np.float32(32))
    ang = inv[:, None] * np.arange(T, dtype=np.float32)[None, :]
    cos, sin = np.cos(ang), np.sin(ang)
    rope = np.stack([np.concatenate([cos] * 4), np.concatenate([-sin, sin] * 2)], axis=1)
    perm = np.zeros((P, P), np.float32)
    for p in range(P):
        perm[p ^ 32, p] = 1.0
    log_g = np.log1p(-np.power(2.0, -5.0 - np.arange(NH)))
    tk, tq = np.arange(T)[:, None], np.arange(T)[None, :]
    dec = np.exp(log_g[:, None, None] * np.abs(tq - tk)) * (tk // CHUNK <= tq // CHUNK) * HD ** -0.5
    dec0 = dec[:, :P, :].transpose(1, 0, 2).reshape(P, -1)
    dec1 = dec[:, P:, P:].transpose(1, 0, 2).reshape(P, -1)
    p = np.arange(P)[:, None]
    mask = np.concatenate([p // GCH % 2 == np.arange(2), p // 32 == np.arange(4), (p // HD == np.arange(2)) * HD ** -0.5,
                           p // HD == np.arange(2)], axis=1)
    f = lambda a: np.ascontiguousarray(a, dtype=np.float32)
    return dict(ident_c=np.eye(P, dtype=np.float32), iota_c=f(np.broadcast_to(np.arange(T), (P, T))),
                decay_c=f(np.concatenate([dec0, dec1], axis=1)), rope_c=f(rope), perm_c=perm, mask_c=f(mask))


def _layout(i):
    col = lambda a: a.reshape(L, -1, P).transpose(0, 2, 1)
    wtile = lambda w: w.reshape(L, KT, P, -1, P).transpose(0, 3, 2, 1, 4).reshape(L, -1, P, D)
    ldt = np.repeat(i["ssm_log_dt"], STATES, axis=1)
    cols = np.concatenate([col(i[n]) for n in ("b_ada", "norm_mix", "norm_ffn", "merge_gain", "ssm_d",
                                               "ssm_lambda_re", "ssm_lambda_im")] + [col(ldt)], axis=2)
    bt = lambda b: b.transpose(0, 1, 3, 2).reshape(L, 2, P, STATES).transpose(0, 2, 1, 3)
    ct = lambda c: c.reshape(L, ST, 2, GCH, STATES).transpose(0, 2, 4, 1, 3).reshape(L, P, ST, GCH)
    return dict(
        xT=i["x"][0].T, c=i["c"][0], cols=cols.transpose(1, 0, 2), fcol=i["final_norm"].reshape(KT, P).T,
        w_ada=i["w_ada"].transpose(0, 2, 1), w_in=wtile(i["w_in"]), w_out=wtile(i["w_out"]), w_q=wtile(i["peer_w_q"]),
        w_glu=i["w_glu"], rel_bias=i["rel_bias"], b_re=bt(i["ssm_b_re"]), b_im=bt(i["ssm_b_im"]),
        c_re=ct(i["ssm_c_re"]), c_im=ct(i["ssm_c_im"]),
        subkeys=i["peer_subkeys"].reshape(L, 16 * NK, P).transpose(0, 2, 1),
        u_tab=i["peer_u"].reshape(L, NE, P, KT, P).transpose(0, 1, 4, 3, 2).reshape(L, NE, P, D),
        v_tab=i["peer_v"].reshape(L, NE, P, D))


_ORDER = ["xT", "c", "cols", "fcol", "w_ada", "w_in", "w_out", "w_q", "w_glu", "rel_bias", "b_re", "b_im", "c_re",
          "c_im", "subkeys", "u_tab", "v_tab", "ident_c", "iota_c", "decay_c", "rope_c", "perm_c", "mask_c"]


def kernel(**inputs):
    import concourse.bacc as _bacc
    from concourse.bass_utils import run_bass_kernel_spmd as _run

    data = _layout({k: np.asarray(a) for k, a in inputs.items()})
    data.update(_tables())
    nc = _bacc.Bacc("TRN2", target_bir_lowering=False, num_devices=1)
    arrays, args = {}, []
    for name in _ORDER:
        a = np.ascontiguousarray(data[name])
        arrays[f"in_{name}_dram"] = a
        args.append(nc.dram_tensor(f"in_{name}_dram", a.shape, mybir.dt.from_np(a.dtype), kind="ExternalInput").ap())
    out = nc.dram_tensor("out_T_dram", (D, T), F32, kind="ExternalOutput")
    trunk(nc, *args, out.ap())
    r = _run(nc, [arrays], core_ids=[0])
    return np.ascontiguousarray(r.results[0]["out_T_dram"].T)[None]
```
